# Optimizing a Trainium2 kernel written in Bass

```python
import math
import jax, jax.numpy as jnp
from jax import lax
import numpy as np

D_MODEL = 2048
BATCH = 1
SEQ = 256
DEPTH = 1

MEM_LEN = 256
EPS = 1e-6
NSA_HEADS = 8
NSA_KV_GROUPS = 2
NSA_HPG = NSA_HEADS // NSA_KV_GROUPS
HEAD_DIM = 128
CMP_BLOCK = 32
CMP_STRIDE = 16
CMP_HIDDEN = 256
SEL_BLOCK = 64
SEL_TOPK = 16
SEL_LOCAL = 2
FORCE_SCORE = 1e4
WINDOW = 512
WIN_QBLOCK = 128
SEL_QCHUNK = 32
RET_HEADS = 4
RET_QK_DIM = 128
RET_V_DIM = 256
RET_CHUNK = 128
MEM_HEADS = 4
MEM_HEAD_DIM = 256
REL_BUCKETS = 32
REL_MAX_DIST = 128
D_FF = 5632
CONV_WIDTH = 3
NSA_Q = NSA_HEADS * HEAD_DIM
NSA_KV = 3 * 2 * NSA_KV_GROUPS * HEAD_DIM
NSA_GATES = 3 * NSA_HEADS
RET_QK = RET_HEADS * RET_QK_DIM
RET_V = RET_HEADS * RET_V_DIM
MEM_Q = MEM_HEADS * MEM_HEAD_DIM
N_BRANCH = 3
BRANCH_GATES = N_BRANCH * D_MODEL
SPLITS = (NSA_Q, NSA_KV, NSA_GATES, RET_QK, RET_QK, RET_V, RET_V, MEM_Q, BRANCH_GATES)
IN_COLS = NSA_Q + NSA_KV + NSA_GATES + 2 * RET_QK + 2 * RET_V + MEM_Q + BRANCH_GATES

kernel_name = 'hybrid_nsa_retention_memory_block'

def rmsnorm(x, g):
    xf = x.astype(jnp.float32)
    y = xf * lax.rsqrt(jnp.mean(xf * xf, axis=-1, keepdims=True) + EPS)
    return (y * g.astype(jnp.float32)).astype(x.dtype)

def t5_bucket(rel):
    n = jnp.maximum(rel, 0)
    max_exact = REL_BUCKETS // 2
    nf = jnp.maximum(n, 1).astype(jnp.float32)
    large = max_exact + (jnp.log(nf / max_exact) / math.log(REL_MAX_DIST / max_exact)
                         * (REL_BUCKETS - max_exact)).astype(jnp.int32)
    large = jnp.minimum(large, REL_BUCKETS - 1)
    return jnp.where(n < max_exact, n, large)

def masked_softmax(s, mask):
    s = jnp.where(mask, s.astype(jnp.float32), -1e30)
    m = jnp.max(s, axis=-1, keepdims=True)
    p = jnp.where(mask, jnp.exp(s - m), 0.0)
    return p / jnp.maximum(jnp.sum(p, axis=-1, keepdims=True), 1e-30)

def nsa_attention(q, kv, gates, tbl, pe_k, w1_k, w2_k, pe_v, w1_v, w2_v):
    B, G, Hg, S, dh = q.shape
    scale = dh ** -0.5
    t_pos = jnp.arange(S)
    k_c, v_c = kv[0, 0], kv[0, 1]
    k_s, v_s = kv[1, 0], kv[1, 1]
    k_w, v_w = kv[2, 0], kv[2, 1]

    n_cmp = (S - CMP_BLOCK) // CMP_STRIDE + 1
    starts = jnp.arange(n_cmp) * CMP_STRIDE
    tok = starts[:, None] + jnp.arange(CMP_BLOCK)[None, :]

    def compress(t, pe, w1, w2):
        blocks = t[:, :, tok] + pe
        flat = blocks.reshape(B, G, n_cmp, CMP_BLOCK * dh)
        return jax.nn.silu(flat @ w1) @ w2

    kc = compress(k_c, pe_k, w1_k, w2_k)
    vc = compress(v_c, pe_v, w1_v, w2_v)
    rel_c = t_pos[:, None] - (starts + CMP_BLOCK - 1)[None, :]
    s_cmp = jnp.einsum('bghsd,bgnd->bghsn', q, kc) * scale + tbl[:, :, t5_bucket(rel_c)]
    p_cmp = masked_softmax(s_cmp, rel_c >= 0)
    o_cmp = jnp.einsum('bghsn,bgnd->bghsd', p_cmp.astype(vc.dtype), vc)

    n_sel = S // SEL_BLOCK
    top_k = min(SEL_TOPK, n_sel)
    blk_start = jnp.arange(n_sel) * SEL_BLOCK
    overlap = ((starts[:, None] < blk_start[None, :] + SEL_BLOCK)
               & (starts[:, None] + CMP_BLOCK > blk_start[None, :])).astype(jnp.float32)
    imp = jnp.einsum('bghsn,nj->bgsj', p_cmp, overlap)
    cur = (t_pos // SEL_BLOCK)[:, None]
    jb = jnp.arange(n_sel)[None, :]
    forced = (jb == 0) | ((cur - jb >= 0) & (cur - jb < SEL_LOCAL))
    imp = jnp.where(forced, FORCE_SCORE, imp)
    imp = jnp.where(jb <= cur, imp, -1.0)
    _, sel_idx = lax.top_k(imp, top_k)

    n_ch = S // SEL_QCHUNK
    L = top_k * SEL_BLOCK
    q_ch = jnp.moveaxis(q.reshape(B, G, Hg, n_ch, SEL_QCHUNK, dh), 3, 0)
    idx_ch = jnp.moveaxis(sel_idx.reshape(B, G, n_ch, SEL_QCHUNK, top_k), 2, 0)
    offs = jnp.arange(SEL_BLOCK)
    g_i = jnp.arange(G)[None, :, None, None, None]
    h_i = jnp.arange(Hg)[None, None, :, None, None]
    gather = jax.vmap(jax.vmap(lambda src, ix: src[ix]))

    def sel_chunk(args):
        qc, ic, c0 = args
        t = c0 * SEL_QCHUNK + jnp.arange(SEL_QCHUNK)
        pos = (ic[..., None] * SEL_BLOCK + offs).reshape(B, G, SEL_QCHUNK, L)
        ks = gather(k_s, pos)
        vs = gather(v_s, pos)
        rel = t[None, None, :, None] - pos
        bias = tbl[g_i, h_i, t5_bucket(rel)[:, :, None]]
        s = jnp.einsum('bghcd,bgcld->bghcl', qc, ks) * scale + bias
        p = masked_softmax(s, (rel >= 0)[:, :, None])
        return jnp.einsum('bghcl,bgcld->bghcd', p.astype(vs.dtype), vs)

    o_sel = lax.map(sel_chunk, (q_ch, idx_ch, jnp.arange(n_ch)))
    o_sel = jnp.moveaxis(o_sel, 0, 3).reshape(B, G, Hg, S, dh)

    nqb = S // WIN_QBLOCK
    span = WINDOW + WIN_QBLOCK
    kpad = jnp.pad(k_w, ((0, 0), (0, 0), (WINDOW, 0), (0, 0)))
    vpad = jnp.pad(v_w, ((0, 0), (0, 0), (WINDOW, 0), (0, 0)))
    q_wb = jnp.moveaxis(q.reshape(B, G, Hg, nqb, WIN_QBLOCK, dh), 3, 0)
    a = jnp.arange(WIN_QBLOCK)[:, None]
    c = jnp.arange(span)[None, :]
    rel_w = WINDOW + a - c
    bias_w = tbl[:, :, t5_bucket(rel_w)]
    band = (rel_w >= 0) & (rel_w < WINDOW)

    def win_block(args):
        qb, i = args
        kb = lax.dynamic_slice_in_dim(kpad, i * WIN_QBLOCK, span, axis=2)
        vb = lax.dynamic_slice_in_dim(vpad, i * WIN_QBLOCK, span, axis=2)
        valid = band & (i * WIN_QBLOCK - WINDOW + c >= 0)
        s = jnp.einsum('bghqd,bgkd->bghqk', qb, kb) * scale + bias_w
        p = masked_softmax(s, valid)
        return jnp.einsum('bghqk,bgkd->bghqd', p.astype(vb.dtype), vb)

    o_win = lax.map(win_block, (q_wb, jnp.arange(nqb)))
    o_win = jnp.moveaxis(o_win, 0, 3).reshape(B, G, Hg, S, dh)

    o = gates[0] * o_cmp + gates[1] * o_sel + gates[2] * o_win
    return o.transpose(0, 3, 1, 2, 4).reshape(B, S, G * Hg * dh)

def rotate_half(x, cos, sin):
    x1, x2 = jnp.split(x, 2, axis=-1)
    return jnp.concatenate([x1 * cos - x2 * sin, x2 * cos + x1 * sin], axis=-1)

def retention(q, k, v):
    B, H, S, dk = q.shape
    dv = v.shape[-1]
    q = q.astype(jnp.float32)
    k = k.astype(jnp.float32)
    v = v.astype(jnp.float32)
    theta = 1.0 / (10000.0 ** jnp.linspace(0.0, 1.0, dk // 2, dtype=jnp.float32))
    ang = jnp.arange(S, dtype=jnp.float32)[:, None] * theta[None, :]
    cos, sin = jnp.cos(ang), jnp.sin(ang)
    q = rotate_half(q, cos, sin)
    k = rotate_half(k, cos, sin) * (dk ** -0.5)
    gamma = 1.0 - jnp.exp2(-5.0 - jnp.arange(H, dtype=jnp.float32))
    log_g = jnp.log(gamma)
    C = RET_CHUNK
    n = S // C
    j = jnp.arange(C, dtype=jnp.float32)
    diff = j[:, None] - j[None, :]
    dmat = jnp.where(diff >= 0, jnp.exp(jnp.maximum(diff, 0.0)[None] * log_g[:, None, None]), 0.0)
    xi = jnp.exp((j + 1.0)[None, :] * log_g[:, None])
    zeta = jnp.exp((C - 1.0 - j)[None, :] * log_g[:, None])
    g_chunk = jnp.exp(C * log_g)

    def to_chunks(t):
        return jnp.moveaxis(t.reshape(B, H, n, C, t.shape[-1]), 2, 0)

    def step(R, inp):
        qi, ki, vi = inp
        inner = jnp.einsum('bhid,bhmd->bhim', qi, ki) * dmat
        o = (jnp.einsum('bhim,bhme->bhie', inner, vi)
             + jnp.einsum('bhid,bhde->bhie', qi, R) * xi[:, :, None])
        R = R * g_chunk[:, None, None] + jnp.einsum('bhmd,bhme->bhde', ki * zeta[:, :, None], vi)
        return R, o

    R0 = jnp.zeros((B, H, dk, dv), jnp.float32)
    _, o = lax.scan(step, R0, (to_chunks(q), to_chunks(k), to_chunks(v)))
    o = jnp.moveaxis(o, 0, 2).reshape(B, H, S, dv)
    mu = jnp.mean(o, axis=-1, keepdims=True)
    var = jnp.mean(jnp.square(o - mu), axis=-1, keepdims=True)
    o = (o - mu) * lax.rsqrt(var + EPS)
    return o.transpose(0, 2, 1, 3).reshape(B, S, H * dv)

def memory_attention(mq, mk, mv):
    scale = mq.shape[-1] ** -0.5
    s = jnp.einsum('bshd,bmhd->bhsm', mq, mk).astype(jnp.float32) * scale
    p = jax.nn.softmax(s, axis=-1)
    o = jnp.einsum('bhsm,bmhd->bshd', p.astype(mv.dtype), mv)
    return o.reshape(mq.shape[0], mq.shape[1], -1)

def causal_dwconv(u, w, b):
    S = u.shape[1]
    up = jnp.pad(u, ((0, 0), (CONV_WIDTH - 1, 0), (0, 0)))
    y = b
    for kk in range(CONV_WIDTH):
        y = y + w[kk] * up[:, kk:kk + S]
    return y

def setup_inputs(seed: int = 0) -> dict:
    key = jax.random.key(seed)
    ks = jax.random.split(key, 26)
    f32 = jnp.float32

    def nrm(k, shape, scale):
        return jax.random.normal(k, shape, f32) * scale

    def gain(k):
        return 1.0 + 0.05 * jax.random.normal(k, (DEPTH, D_MODEL), f32)

    flat_cmp = CMP_BLOCK * HEAD_DIM
    return {
        'x': nrm(ks[0], (BATCH, SEQ, D_MODEL), 1.0),
        'mem': nrm(ks[1], (BATCH, MEM_LEN, D_MODEL), 1.0),
        'w_in': nrm(ks[2], (DEPTH, D_MODEL, IN_COLS), D_MODEL ** -0.5),
        'cmp_pe_k': nrm(ks[3], (DEPTH, CMP_BLOCK, HEAD_DIM), 0.5),
        'cmp_w1_k': nrm(ks[4], (DEPTH, flat_cmp, CMP_HIDDEN), flat_cmp ** -0.5),
        'cmp_w2_k': nrm(ks[5], (DEPTH, CMP_HIDDEN, HEAD_DIM), CMP_HIDDEN ** -0.5),
        'cmp_pe_v': nrm(ks[6], (DEPTH, CMP_BLOCK, HEAD_DIM), 0.5),
        'cmp_w1_v': nrm(ks[7], (DEPTH, flat_cmp, CMP_HIDDEN), flat_cmp ** -0.5),
        'cmp_w2_v': nrm(ks[8], (DEPTH, CMP_HIDDEN, HEAD_DIM), CMP_HIDDEN ** -0.5),
        'rel_bias': nrm(ks[9], (REL_BUCKETS, NSA_HEADS), 0.5),
        'w_mem_kv': nrm(ks[10], (DEPTH, D_MODEL, 2 * MEM_Q), D_MODEL ** -0.5),
        'w_br_nsa': nrm(ks[11], (DEPTH, NSA_Q, D_MODEL), NSA_Q ** -0.5),
        'w_br_ret': nrm(ks[12], (DEPTH, RET_V, D_MODEL), RET_V ** -0.5),
        'w_br_mem': nrm(ks[13], (DEPTH, MEM_Q, D_MODEL), MEM_Q ** -0.5),
        'w_o': nrm(ks[14], (DEPTH, D_MODEL, D_MODEL), D_MODEL ** -0.5),
        'w_up': nrm(ks[15], (DEPTH, D_MODEL, 2 * D_FF), D_MODEL ** -0.5),
        'conv_w': nrm(ks[16], (DEPTH, CONV_WIDTH, 2 * D_FF), CONV_WIDTH ** -0.5),
        'conv_b': nrm(ks[17], (DEPTH, 2 * D_FF), 0.01),
        'w_down': nrm(ks[18], (DEPTH, D_FF, D_MODEL), D_FF ** -0.5),
        'g_pre_mix': gain(ks[19]),
        'g_post_mix': gain(ks[20]),
        'g_mem': gain(ks[21]),
        'g_pre_ffn': gain(ks[22]),
        'g_post_ffn': gain(ks[23]),
    }

def reference(x, mem, w_in, cmp_pe_k, cmp_w1_k, cmp_w2_k, cmp_pe_v, cmp_w1_v, cmp_w2_v,
              rel_bias, w_mem_kv, w_br_nsa, w_br_ret, w_br_mem, w_o, w_up, conv_w, conv_b,
              w_down, g_pre_mix, g_post_mix, g_mem, g_pre_ffn, g_post_ffn):
    B, S, D = x.shape
    M = mem.shape[1]
    G, Hg, dh = NSA_KV_GROUPS, NSA_HPG, HEAD_DIM
    pts = np.cumsum(np.array(SPLITS))[:-1].tolist()
    tbl = rel_bias.T.reshape(G, Hg, REL_BUCKETS)
    for l in range(DEPTH):
        h = rmsnorm(x, g_pre_mix[l])
        proj = h @ w_in[l]
        nq, nkv, ngate, rq, rk, rv, rg, mq, bg = jnp.split(proj, pts, axis=-1)

        q_a = nq.reshape(B, S, G, Hg, dh).transpose(0, 2, 3, 1, 4)
        kv_a = nkv.reshape(B, S, 3, 2, G, dh).transpose(2, 3, 0, 4, 1, 5)
        gate_a = jax.nn.sigmoid(ngate.reshape(B, S, 3, G, Hg)).transpose(2, 0, 3, 4, 1)[..., None]
        y_a = nsa_attention(q_a, kv_a, gate_a.astype(x.dtype), tbl,
                            cmp_pe_k[l], cmp_w1_k[l], cmp_w2_k[l],
                            cmp_pe_v[l], cmp_w1_v[l], cmp_w2_v[l])

        q_r = rq.reshape(B, S, RET_HEADS, RET_QK_DIM).transpose(0, 2, 1, 3)
        k_r = rk.reshape(B, S, RET_HEADS, RET_QK_DIM).transpose(0, 2, 1, 3)
        v_r = rv.reshape(B, S, RET_HEADS, RET_V_DIM).transpose(0, 2, 1, 3)
        y_b = (retention(q_r, k_r, v_r).astype(x.dtype) * jax.nn.silu(rg))

        mem_n = rmsnorm(mem, g_mem[l])
        mkv = (mem_n @ w_mem_kv[l]).reshape(B, M, 2, MEM_HEADS, MEM_HEAD_DIM)
        y_c = memory_attention(mq.reshape(B, S, MEM_HEADS, MEM_HEAD_DIM),
                               mkv[:, :, 0], mkv[:, :, 1])

        bgate = jax.nn.sigmoid(bg.reshape(B, S, N_BRANCH, D))
        merged = (bgate[:, :, 0] * (y_a @ w_br_nsa[l])
                  + bgate[:, :, 1] * (y_b @ w_br_ret[l])
                  + bgate[:, :, 2] * (y_c @ w_br_mem[l]))
        x = x + rmsnorm(merged @ w_o[l], g_post_mix[l])

        h2 = rmsnorm(x, g_pre_ffn[l])
        u = causal_dwconv(h2 @ w_up[l], conv_w[l], conv_b[l])
        u_gate, u_val = jnp.split(u, 2, axis=-1)
        f = (jax.nn.gelu(u_gate, approximate=True) * u_val) @ w_down[l]
        x = x + rmsnorm(f, g_post_ffn[l])
    return x


_drawn_inputs = setup_inputs


def setup_inputs(seed=0):
    import zlib

    import numpy as np

    out = dict(_drawn_inputs(seed))
    spreads = {}
    factors = {'conv_b': 7.031,
     'g_mem': 5.878,
     'cmp_pe_k': 8.0,
     'cmp_w1_k': 5.173,
     'cmp_w2_k': 5.051,
     'rel_bias': 3.609}
    for name, (base, spread) in spreads.items():
        noise = np.random.default_rng([zlib.crc32(name.encode()), seed]).standard_normal(out[name].shape)
        drawn = base * np.exp(spread * noise) if base else spread * noise
        out[name] = __import__('jax').numpy.asarray(drawn.astype(out[name].dtype))
    for name, factor in factors.items():
        out[name] = (out[name] * factor).astype(out[name].dtype)
    return out
```

```python
import math
from contextlib import ExitStack

import numpy as np
import concourse.bass as bass
from concourse import mybir

F32 = mybir.dt.float32
F32R = mybir.dt.float32r
ACT = mybir.ActivationFunctionType
ALU = mybir.AluOpType
AX = mybir.AxisListType

P = 128
S = 256
D = 2048
KT = D // P
TT = S // P
GW = 256
CK = 4
EPS = 1e-6
HEADS, GROUPS, DH = 8, 2, 128
HPG = HEADS // GROUPS
CB, CS = 32, 16
NC = (S - CB) // CS + 1
NC0 = (P - CB) // CS + 1
RH, RDK, RDV = 4, 128, 256
MH, MD = 4, 256
FF = 5632
BUCKETS, MAXD = 32, 128
MASKED = -1e30
REL = 384
STEPS = FF // 512

C_NQ = 0
C_KV = 1024
C_NG = C_KV + 1536
C_RQ = C_NG + 24
C_RK = C_RQ + 512
C_RV = C_RK + 512
C_RG = C_RV + 1024
C_MQ = C_RG + 1024
C_BG = C_MQ + 1024

PHASES = [("mq", 4, 4), ("mk", 4, 4), ("mv", 4, 4), ("nq", 4, 4), ("kv0", 3, 3), ("cmp", 4, 2),
          ("kv1", 3, 3), ("rqk", 4, 4), ("rv", 4, 4), ("rg", 4, 4),
          ("bg0", 8, 8), ("br0", 4, 8), ("bg1", 8, 8), ("br1", 4, 8), ("bg2", 8, 8), ("br2", 4, 8),
          ("wo", 8, 8), ("up0", 4, 4), ("ffn", 6 * (STEPS - 1), 12 * (STEPS - 1)), ("dn", 2, 8)]
Q0, G0 = {}, {}
_q = _g = 0
for _n, _a, _b in PHASES:
    Q0[_n], G0[_n] = _q, _g
    _q, _g = _q + _a, _g + _b
QUADS = _q

A_X, A_M = 0, 4096
A_MQ, A_MK, A_MV = 0, 2048, 4096
A_NQ = 6144
A_KC, A_VC, A_KS, A_VS, A_KW, A_VW = (8192 + 512 * n for n in range(6))
A_RQ, A_RK, A_RV, A_RG = 0, 1024, 4096, 6144
A_MERGED, A_GATE, A_GPOST = 0, 8192, 8192
NSA_P = [(768, NC0), (0, P), (P, P), (768 + NC0, NC), (2 * P, S), (2 * P + S, S)]
W_P, W_PT, W_CT, W_QS = 0, 792, 1560, 1816
W_MP, W_MPT, W_MS, W_MVS = 0, 512, 1024, 1536
W_QR, W_RT, W_IN, W_YB = 0, 512, 1024, 1408
W_RGT = 2048
W_RB = 1408
W_Y, W_PROD, W_TMP = 0, 1024, 0


NSA_LINKS, RET_LINKS = 11, 8


class Chain:

    def __init__(self, eng, sem):
        self.eng, self.sem, self.n, self.base = eng, sem, 0, 0

    def add(self, ins):
        ins.then_inc(self.sem, 1)
        self.n += 1

    def wait(self):
        self.eng.wait_ge(self.sem, self.base + self.n)

    def link(self, ins):
        self.add(ins)
        self.wait()

    def enter(self, i, per):
        self.start = self.n
        self.base, self.n = self.start + per * i, 0

    def leave(self, trips, per):
        assert self.n == per, (self.n, per)
        self.base, self.n = 0, self.start + trips * per


def build(nc, x, mem, w_in, cmp_pe_k, cmp_w1_k, cmp_w2_k, cmp_pe_v, cmp_w1_v, cmp_w2_v, rel_bias,
          w_mem_kv, w_br_nsa, w_br_ret, w_br_mem, w_o, w_up, conv_w, conv_b, w_down, g_pre_mix,
          g_post_mix, g_mem, g_pre_ffn, g_post_ffn, c_eye, c_rot, c_onehot, c_ret, scratch, out):
    ctx = ExitStack()
    with ctx:
        def sb(name, shape, dt=F32):
            return ctx.enter_context(nc.sbuf_tensor(name, shape, dt))

        def sem(name):
            return ctx.enter_context(nc.semaphore(name))

        h_hi, h_lo = (sb(n, [P, KT, S], F32R) for n in ("h_hi", "h_lo"))
        m_hi, m_lo = (sb(n, [P, KT, S], F32R) for n in ("m_hi", "m_lo"))
        r_hi, r_lo = (sb(n, [P, 8, S], F32R) for n in ("r_hi", "r_lo"))
        wraw = sb("wraw", [P, 4, CK, GW])
        whi, wlo = (sb(n, [P, 4, CK, GW], F32R) for n in ("whi", "wlo"))
        arena = sb("arena", [P, 12288])
        tables = sb("tables", [P, 2048])
        work = sb("work", [P, 2560])
        eye = sb("eye", [P, P])
        rot = sb("rot", [P, P])
        gain = sb("gain", [P, 3 * KT])
        conv = sb("conv", [P, 4, 88])
        wgr = sb("wgr", [P, KT, 24])
        wgh, wgl = (sb(n, [P, KT, 24], F32R) for n in ("wgh", "wgl"))
        sig = sb("sig", [P, TT, 24])
        kc = sb("kc", [P, GROUPS, NC])
        vc = sb("vc", [NC, GROUPS, DH])
        hid = sb("hid", [P, 2, 2, 2 * NC])
        w2 = sb("w2", [P, 2, 2, DH])
        peT = sb("peT", [P, 2, CB])
        st = sb("st", [P, 64])

        ps = [ctx.enter_context(nc.psum_tensor(f"bank{i}", [P, 512], F32)) for i in range(8)]

        loaded = [sem(f"loaded{c}") for c in range(4)]
        hi_done, lo_done = sem("hi_done"), sem("lo_done")
        pe_done = sem("pe_done")
        evac = [sem(f"evac{b}") for b in range(2)]
        dch, ach, pch = sem("vector_chain"), sem("scalar_chain"), sem("pool_chain")
        s_x = [sem("x_in0"), sem("x_in1")]
        s_m = [sem("mem_in0"), sem("mem_in1")]
        s_eye, s_const, s_rows, s_rows2 = sem("eye_in"), sem("rot_in"), sem("gain_rows_in"), sem("conv_rows_in")
        s_wg, s_pe2, s_oh = sem("wg_in"), sem("pe_w2_in"), sem("onehot_in")
        s_ssq, s_var, s_rstd, s_xn = sem("ssq"), sem("var"), sem("rstd"), sem("xn")
        s_tr, s_trh, s_trl = sem("transposed"), sem("tile_hi"), sem("tile_lo")
        s_half = sem("half_const")
        s_vt, s_ve, s_neg, s_wide = sem("vectors_transposed"), sem("vectors_out"), sem("masked_row"), sem("bias_columns")
        s_rb, s_rbc, s_scr, s_tab, s_tab2 = sem("bias_row"), sem("bias_row_out"), sem("bias_stored"), sem("bias_in"), sem("ret_in")
        s_wgh, s_wgl, s_gp, s_gt, s_sig = sem("wg_hi"), sem("wg_lo"), sem("gate_ps"), sem("gate_tanh"), sem("gate_sig")
        s_bk, s_bkh, s_bkl = sem("blocks"), sem("blocks_hi"), sem("blocks_lo")
        s_ht, s_hid, s_kc, s_kce = sem("hid_tanh"), sem("hid"), sem("kc_ps"), sem("kc_out")
        m_st, m_s, m_nm, m_ex, m_p, m_t, m_te, m_o, m_h, m_l = (sem("mem_" + n) for n in (
            "staged", "scores", "max", "exp", "probs", "transposed", "pt", "out", "hi", "lo"))
        a_st, a_s, a_nm, a_ex, a_p, a_t, a_ta, a_tv, a_o, a_h, a_l = (sem("nsa_" + n) for n in (
            "staged", "scores", "max", "exp", "probs", "transposed", "pt_win", "pt_sel", "out", "hi", "lo"))
        r_r, r_q, r_i, r_d, r_o, r_v, r_rs, r_y, r_t, r_h, r_l = (sem("ret_" + n) for n in (
            "rotated", "qk", "inner", "decayed", "out", "var", "rstd", "y", "transposed", "hi", "lo"))
        s_rgt, s_stats = sem("rg_tanh"), sem("stats_made")
        s_mg, s_mgh, s_mgl = sem("merged"), sem("merged_hi"), sem("merged_lo")
        s_gpost = sem("gpost_in")
        s_mo = sem("mo_done")
        s_x2 = sem("x2")
        s_y, s_gelu, s_prod, s_ah, s_al = sem("conv_tap2"), sem("gelu"), sem("prod"), sem("act_hi"), sem("act_lo")
        s_f0 = sem("f_zero")
        s_fin, s_out = sem("final"), sem("out_stored")

        block = ctx.enter_context(nc.Block())

        X = arena[:, A_X:A_X + 4096].rearrange("p (t n) -> p t n", t=TT)
        M = arena[:, A_M:A_M + 4096].rearrange("p (t n) -> p t n", t=TT)
        gpost = arena[:, A_GPOST:A_GPOST + D]
        merged = arena[:, A_MERGED:A_MERGED + 4096]
        GP = gpost
        half = st[:, 60:61]

        def bank(g, t=None):
            b = ps[g][:, :].rearrange("p (t n) -> p t n", t=TT)
            return b if t is None else b[:, t, :]

        def blocks(src, n):
            return src[:, 4 * n:4 * n + 4, :].rearrange("p k s -> p (k s)")[:, 0:2 * NC * CB]

        def up_group(s):
            if isinstance(s, int):
                assert s == 0
                return G0["up0"] // 2
            return 6 * s + (G0["ffn"] // 2 - 6)

        def rows(w, k0, col, n=GW, kt=CK):
            return w[0, k0 * P:(k0 + kt) * P, :].rearrange("(k p) n -> p k n", p=P)[:, :, bass.ds(col, n)]

        @block.sync
        def _(sp):
            def quad(q, src):
                for c in range(4):
                    if q:
                        sp.wait_ge(lo_done, 4 * (q - 1) + c + 1)
                    sp.dma_start(wraw[:, c], src(c)).then_inc(loaded[c], 16)

            def loop(q0, trips, per, sources):
                with sp.Fori(0, trips) as i:
                    free = [sp.snap(4 * per * i + (4 * (q0 - 1) + k + 1)) for k in range(4 * per)]
                    src = sources(i)
                    for j in range(per):
                        for c in range(4):
                            sp.wait_ge(lo_done, free[4 * j + c])
                            sp.dma_start(wraw[:, c], src[j](c)).then_inc(loaded[c], 16)

            def cols(w, base, count=2):
                def sources(i):
                    at = [sp.snap(count * GW * i + (base + GW * j)) for j in range(count)]
                    return [lambda c, o=o: rows(w, 4 * c, o) for o in at]
                return sources

            for t in range(TT):
                sp.dma_start(X[:, t, :], x[0, t * P:(t + 1) * P, :]).then_inc(s_x[t], 16)
            for n, g in enumerate((g_pre_mix, g_mem, g_pre_ffn)):
                sp.dma_start(work[n * KT:(n + 1) * KT, 0:P], g.rearrange("o (k p) -> (o k) p", p=P)).then_inc(s_rows, 16)
            sp.dma_start(eye[:, :], c_eye[:, :]).then_inc(s_eye, 16)
            quad(0, lambda c: rows(w_in, 4 * c, C_MQ))
            for t in range(TT):
                sp.dma_start(M[:, t, :], mem[0, t * P:(t + 1) * P, :]).then_inc(s_m[t], 16)
            for k in range(3):
                sp.dma_start(work[0:88, P * (1 + k):P * (2 + k)],
                             conv_w[0, k:k + 1, :].rearrange("o (k p) -> (o k) p", p=P)).then_inc(s_rows2, 16)
            sp.dma_start(work[0:88, 4 * P:5 * P], conv_b.rearrange("o (k p) -> (o k) p", p=P)).then_inc(s_rows2, 16)
            sp.dma_start(work[0:CB, 5 * P:6 * P], cmp_pe_k[0]).then_inc(s_rows2, 16)
            sp.dma_start(work[0:CB, 6 * P:7 * P], cmp_pe_v[0]).then_inc(s_rows2, 16)
            sp.dma_start(work[0:BUCKETS, W_RB:W_RB + HEADS], rel_bias[:, :]).then_inc(s_oh, 16)
            sp.dma_start(work[0:BUCKETS + 1, 1024:1024 + REL], c_onehot[:, :]).then_inc(s_oh, 16)
            sp.dma_start(rot[:, :], c_rot[:, :]).then_inc(s_const, 16)
            sp.dma_start(wgr[:, :, :], rows(w_in, 0, C_NG, 24, KT)).then_inc(s_wg, 16)
            sp.dma_start(w2[:, 0], cmp_w2_k[0].rearrange("(k p) n -> p k n", p=P)).then_inc(s_pe2, 16)
            sp.dma_start(w2[:, 1], cmp_w2_v[0].rearrange("(k p) n -> p k n", p=P)).then_inc(s_pe2, 16)
            quad(1, lambda c: rows(w_in, 4 * c, C_MQ + GW))
            sp.wait_ge(s_rbc, HEADS)
            sp.dma_start(scratch.rearrange("h p n -> p h n"),
                         arena[:, A_NQ:A_NQ + HEADS * REL].rearrange("p (h n) -> p h n", h=HEADS)).then_inc(s_scr, 16)
            sp.wait_ge(s_scr, 16)
            sp.dma_start(tables[:, :].rearrange("p (h n) -> p h n", h=HEADS),
                         bass.AP(scratch.tensor, P - 1, [[REL - 1, P], [P * REL, HEADS], [1, S]])).then_inc(s_tab, 16)
            loop(2, 1, 2, cols(w_in, C_MQ + 2 * GW))
            loop(Q0["mk"], 4, 2, cols(w_mem_kv[:, :, :], 0))
            loop(Q0["nq"], 2, 2, cols(w_in, C_NQ))
            for n in range(3):
                quad(Q0["kv0"] + n, lambda c: rows(w_in, 4 * c, C_KV + n * GW))
            for n, w in enumerate((cmp_w1_k, cmp_w1_v)):
                for j in range(2):
                    quad(Q0["cmp"] + 2 * n + j, lambda c: rows(w, 16 * j + 4 * c, 0))
            for n in range(3):
                quad(Q0["kv1"] + n, lambda c: rows(w_in, 4 * c, C_KV + (3 + n) * GW))
            loop(Q0["rqk"], 6, 2, cols(w_in, C_RQ))
            sp.wait_ge(a_nm, HEADS)
            sp.dma_start(tables[:, :], c_ret[:, :]).then_inc(s_tab2, 16)
            for n, (b, w) in enumerate(((2, w_br_mem), (0, w_br_nsa), (1, w_br_ret))):
                loop(Q0[f"bg{n}"], 4, 2, cols(w_in, C_BG + b * D))

                def pairs(i):
                    at = [sp.snap(4 * GW * i + GW * j) for j in range(4)]
                    return [lambda c, j=j: rows(w, 4 * (c % 2), at[2 * j + c // 2]) for j in range(2)]
                loop(Q0[f"br{n}"], 2, 2, pairs)
            loop(Q0["wo"], 4, 2, cols(w_o, 0))
            sp.wait_ge(s_mgl, 1)
            for t in range(TT):
                sp.dma_start(X[:, t, :], x[0, t * P:(t + 1) * P, :]).then_inc(s_x[t], 16)
            sp.dma_start(GP, g_post_mix.to_broadcast([P, D])).then_inc(s_gpost, 16)

            def up_col(n):
                return (n // 2) * GW + (n % 2) * FF

            def down(r0):
                w = w_down[0, bass.ds(r0, 512), :].rearrange("(k p) n -> p k n", p=P)
                return [lambda c, j=j: w[:, :, (4 * j + c) * GW:(4 * j + c + 1) * GW] for j in range(2)]

            for n in range(4):
                quad(Q0["up0"] + n, lambda c: rows(w_up, 4 * c, up_col(n)))
                if n == 1:
                    sp.wait_ge(s_x2, TT)
                    sp.dma_start(GP, g_post_ffn.to_broadcast([P, D])).then_inc(s_gpost, 16)

            def step(i):
                at = [sp.snap(512 * i + (512 + up_col(n))) for n in range(4)]
                return [lambda c, o=o: rows(w_up, 4 * c, o) for o in at] + down(sp.snap(512 * i))
            loop(Q0["ffn"], STEPS - 1, 6, step)
            for j in range(2):
                quad(Q0["dn"] + j, down((STEPS - 1) * 512)[j])
            for t in range(TT):
                sp.wait_ge(s_fin, t + 1)
                sp.dma_start(out[0, t * P:(t + 1) * P, :], M[:, t, :]).then_inc(s_out, 16)
            sp.wait_ge(s_out, 16 * TT)

        @block.gpsimd
        def _(pool):
            nc.gpsimd.memset(half, -0.5).then_inc(s_half, 1)
            pool.wait_ge(s_half, 1)
            nc.gpsimd.memset(work[BUCKETS:BUCKETS + 1, W_RB:W_RB + HEADS], MASKED).then_inc(s_neg, 1)
            pool.wait_ge(s_neg, 1)

            def rstd(n):
                pool.wait_ge(s_var, n + 1)
                nc.gpsimd.tensor_tensor(st[:, 4:6], st[:, 2:4], half.to_broadcast([P, 2]), ALU.pow).then_inc(s_rstd, 1)

            rstd(0)
            rstd(1)
            pool.wait_ge(s_scr, 16)
            for b in range(2):
                pool.wait_ge(evac[b], G0["nq"] // 2)
            with pool.Fori(0, MH) as m:
                pool.wait_ge(m_o, m + 1)
                nc.gpsimd.tensor_copy(work[:, W_MS:W_MS + 512], arena[:, bass.ds(512 * m + A_MQ, 512)]).then_inc(m_st, 1)
                pool.wait_ge(m_st, 2 * m + 1)
                nc.gpsimd.tensor_copy(work[:, W_MVS:W_MVS + 512], arena[:, bass.ds(512 * m + A_MV, 512)]).then_inc(m_st, 1)
            pool.wait_ge(s_bkl, 2)
            with pool.Fori(0, HEADS) as h:
                pool.wait_ge(a_s, h + 1)
                nc.gpsimd.tensor_copy(work[:, W_QS:W_QS + S], arena[:, bass.ds(S * h + A_NQ, S)]).then_inc(a_st, 1)
            with pool.Fori(0, RH) as r:
                pool.wait_ge(r_v, r + 1)
                nc.gpsimd.tensor_tensor(st[:, 44:46], st[:, 42:44], half.to_broadcast([P, 2]), ALU.pow).then_inc(r_rs, 1)
            rstd(2)
            rstd(3)
            pool.wait_ge(s_trl, 3 * KT // 2)
            nc.gpsimd.memset(arena[:, A_M:A_M + 4096], 0.0).then_inc(s_f0, 1)
            rstd(4)

        @block.scalar
        def _(act):
            def hi(q, c):
                act.wait_ge(loaded[c], 16 * q + 16)
                if not (isinstance(q, int) and q == 0):
                    act.wait_ge(pe_done, 4 * q + (c - 3))
                nc.scalar.activation(whi[:, c], wraw[:, c], ACT.Copy).then_inc(hi_done, 1)

            def ahead(q, chunks=range(4)):
                for c in chunks:
                    hi(q + 1, c)

            def plain(q0, trips):
                with act.Fori(0, trips) as i:
                    for j in range(2):
                        ahead(2 * i + (q0 + j))

            def squares(n, src, wait):
                for t in range(TT):
                    if n:
                        act.wait_ge(s_ssq, 2 * n - 1 + t)
                    act.wait_ge(*wait(t))
                    nc.scalar.activation((r_hi, r_lo)[t][:, :, :].rearrange("p k s -> p (k s)"), src[:, t, :], ACT.Square,
                                         accum_out=st[:, t:t + 1]).then_inc(s_ssq, 1)

            def tiles_hi(dst, n):
                for k in range(0, KT, 2):
                    act.wait_ge(s_tr, (KT * n + k) // 2 + 1)
                    for u in range(2):
                        e = nc.scalar.activation(dst[:, k + u, :], bank(2 + (k // 2) % 6, u), ACT.Copy,
                                                 scale=gain[:, n * KT + k + u:n * KT + k + u + 1])
                    e.then_inc(s_trh, 1)

            squares(0, X, lambda t: (s_x[t], 16))
            for c in range(4):
                hi(0, c)
            act.wait_ge(s_ve, 1)
            tiles_hi(h_hi, 0)
            squares(1, M, lambda t: (s_m[t], 16))
            act.wait_ge(s_wg, 16)
            nc.scalar.activation(wgh[:, :, :], wgr[:, :, :], ACT.Copy).then_inc(s_wgh, 1)
            ahead(0)
            tiles_hi(m_hi, 1)
            ahead(1)
            act.wait_ge(s_gp, 1)
            nc.scalar.activation(sig[:, :, :], ps[7][:, 448:496].rearrange("p (t n) -> p t n", t=TT), ACT.Tanh, scale=0.5).then_inc(s_gt, 1)
            plain(2, 1)
            plain(Q0["mk"], 4)

            with act.Fori(0, 2) as i:
                for j in range(2):
                    m, q = 2 * i + j, 2 * i + (Q0["nq"] + j)
                    ahead(q, (0,))
                    act.wait_ge(m_nm, m + 1)
                    for t in range(TT):
                        e = nc.scalar.activation(work[:, W_MP + S * t:W_MP + S * (t + 1)], bank(2, t), ACT.Exp,
                                                 bias=st[:, 32 + t:33 + t], accum_out=st[:, 34 + t:35 + t])
                    e.then_inc(m_ex, 1)
                    ahead(q, (1, 2, 3))
                    act.wait_ge(m_o, m + 2)
                    nc.scalar.activation(m_hi[:, bass.ds(2 * m, 2), :], bank(6), ACT.Copy).then_inc(m_h, 1)
            ahead(Q0["kv0"])
            ahead(Q0["kv0"] + 1)
            for n in range(2):
                act.wait_ge(s_bk, n + 1)
                nc.scalar.activation(blocks(r_hi, n), work[:, 960 * n:960 * (n + 1)], ACT.Copy).then_inc(s_bkh, 1)
            ahead(Q0["kv0"] + 2)
            for n in range(2):
                ahead(Q0["cmp"] + 2 * n)
                ahead(Q0["cmp"] + 2 * n + 1)
                nc.scalar.activation(hid[:, n], bank((G0["cmp"] + n) % 2)[:, :, 0:2 * NC], ACT.Tanh, scale=0.5).then_inc(s_ht, 1)
            for n in range(3):
                ahead(Q0["kv1"] + n)

            for g, ph in enumerate(("rqk", "rv")):
                with act.Fori(0, 2) as i:
                    for j in range(2):
                        h, q = 2 * i + (HPG * g + j), 2 * i + (Q0[ph] + j)
                        ahead(q, (0,))
                        act.wait_ge(a_nm, h + 1)
                        for n, (o, w) in enumerate(NSA_P):
                            e = nc.scalar.activation(work[:, W_P + o:W_P + o + w], work[:, W_P + o:W_P + o + w], ACT.Exp,
                                                     bias=st[:, n:n + 1], accum_out=st[:, 12 + n:13 + n])
                        e.then_inc(a_ex, 1)
                        ahead(q, (1, 2))
                        act.wait_ge(a_t, h + 1)
                        nc.scalar.activation(work[:, W_PT + 384:W_PT + 768], ps[5][:, 0:384], ACT.Copy)
                        nc.scalar.activation(work[0:NC, W_CT + P:W_CT + 2 * P], ps[5][0:NC, 384:512], ACT.Copy).then_inc(a_ta, 1)
                        ahead(q, (3,))
                        act.wait_ge(a_o, h + 1)
                        nc.scalar.activation(m_hi[:, bass.ds(h + 8, 1), :], ps[6][:, 0:S].unsqueeze(1), ACT.Copy).then_inc(a_h, 1)
            with act.Fori(0, 2) as i:
                for j in range(2):
                    ahead(2 * i + (Q0["rg"] + j))
                    act.wait_ge(evac[1 - j], i + (G0["rg"] // 2 + j))
                    nc.scalar.activation(work[:, W_RGT:W_RGT + 512], ps[j][:, :], ACT.Tanh, scale=0.5).then_inc(s_rgt, 1)

            for n in range(3):
                q0 = Q0[f"bg{n}"]
                for b in range(2):
                    act.wait_ge(evac[b], G0[f"bg{n}"] // 2)
                if n == 0:
                    with act.Fori(0, 2) as i:
                        for j in range(2):
                            r, q = 2 * i + j, 2 * i + (q0 + j)
                            ahead(q)
                            nc.scalar.activation(arena[:, bass.ds(1024 * i + (A_GATE + 512 * j), 512)], ps[j][:, :],
                                                 ACT.Tanh, scale=0.5).then_inc(evac[j], 1)
                            act.wait_ge(r_t, r + 1)
                            nc.scalar.activation(r_hi[:, bass.ds(2 * r, 2), :], bank(6), ACT.Copy).then_inc(r_h, 1)
                with act.Fori(0, 2 if n == 0 else 4) as i:
                    for j in range(2):
                        k = 8 - (4 if n == 0 else 8) + j
                        ahead(2 * i + (q0 + k))
                        nc.scalar.activation(arena[:, bass.ds(1024 * i + (A_GATE + 512 * k), 512)], ps[j][:, :],
                                             ACT.Tanh, scale=0.5).then_inc(evac[j], 1)
                plain(Q0[f"br{n}"], 2)
            act.wait_ge(s_mg, 1)
            nc.scalar.activation(m_hi[:, :, :].rearrange("p k s -> p (k s)"), merged, ACT.Copy, scale=0.5).then_inc(s_mgh, 1)
            plain(Q0["wo"], 4)
            squares(2, M, lambda t: (s_mo, 1))
            squares(3, X, lambda t: (s_x2, t + 1))
            tiles_hi(h_hi, 2)

            def up_quads(q, s):
                for n in range(4):
                    a, j = n // 2, n % 2
                    ahead(q + n)
                    if not (isinstance(s, int) and a == 0):
                        act.wait_ge(s_prod, 2 * s + a)
                    for t in range(2):
                        col = 4 * s + (44 * j + 2 * a + t)
                        e = nc.scalar.activation(work[:, W_Y + 512 * j + S * t:W_Y + 512 * j + S * (t + 1)], bank(j, t),
                                                 ACT.Identity, bias=conv[:, 3, bass.ds(col, 1)], scale=conv[:, 2, bass.ds(col, 1)])
                    e.then_inc(s_y, 1)
                    if j:
                        act.wait_ge(evac[0], up_group(s) + a + 1)
                        nc.scalar.activation(work[:, W_Y:W_Y + 512], work[:, W_Y:W_Y + 512], ACT.Gelu_apprx_tanh).then_inc(s_gelu, 1)

            def split_hi(s):
                act.wait_ge(s_prod, 2 * s + 2)
                nc.scalar.activation(r_hi[:, 0:4, :].rearrange("p k s -> p (k s)"), work[:, W_PROD:W_PROD + 1024], ACT.Copy).then_inc(s_ah, 1)

            up_quads(Q0["up0"], 0)
            split_hi(0)
            with act.Fori(0, STEPS - 1) as i:
                q = 6 * i + Q0["ffn"]
                up_quads(q, i + 1)
                ahead(q + 4)
                ahead(q + 5)
                split_hi(i + 1)
            ahead(Q0["dn"])
            for b in range(2):
                act.wait_ge(evac[b], G0["dn"] // 2 + 4)
            for t in range(TT):
                nc.scalar.activation(h_hi[:, 8 * t:8 * t + 8, :].rearrange("p k s -> p (k s)"), M[:, t, :], ACT.Square,
                                     accum_out=st[:, t:t + 1]).then_inc(s_ssq, 1)

        @block.vector
        def _(dve):
            V = nc.vector
            ch = Chain(dve, dch)
            for free in (m_l, a_l, r_l):
                dve.sem_inc(free, 1)

            def lo(q, c):
                dve.wait_ge(hi_done, 4 * q + (c + 1))
                V.tensor_tensor(wlo[:, c], wraw[:, c], whi[:, c].bitcast(F32), ALU.subtract).then_inc(lo_done, 1)

            def ahead(q, chunks=range(4)):
                for c in chunks:
                    lo(q + 1, c)

            def store(q, b, dst, scale=None):
                dve.wait_ge(pe_done, 4 * q + 4)
                if scale is None:
                    return V.tensor_copy(dst, ps[b][:, :]).then_inc(evac[b], 1)
                return V.tensor_scalar(dst, ps[b][:, :], scale, None, ALU.mult).then_inc(evac[b], 1)

            def stores(q0, trips, base, scale=None):
                with dve.Fori(0, trips) as i:
                    for j in range(2):
                        ahead(2 * i + (q0 + j))
                        store(2 * i + (q0 + j), j, arena[:, bass.ds(1024 * i + (base + 512 * j), 512)], scale)

            def mean_square(n):
                dve.wait_ge(s_ssq, 2 * n + 2)
                V.tensor_scalar(st[:, 2:4], st[:, 0:2], 1.0 / D, EPS, ALU.mult, ALU.add).then_inc(s_var, 1)
                dve.wait_ge(s_rstd, n + 1)

            def normed(dst, src):
                for t in range(TT):
                    V.tensor_scalar(dst[:, t, :], src[:, t, :], st[:, 4 + t:5 + t], None, ALU.mult).then_inc(s_xn, 1)

            def tiles_lo(dst_hi, dst, n):
                for k in range(0, KT, 2):
                    dve.wait_ge(s_trh, (KT * n + k) // 2 + 1)
                    for u in range(2):
                        e = V.scalar_tensor_tensor(dst[:, k + u, :], bank(2 + (k // 2) % 6, u), gain[:, n * KT + k + u:n * KT + k + u + 1],
                                                   dst_hi[:, k + u, :].bitcast(F32), ALU.mult, ALU.subtract)
                    e.then_inc(s_trl, 1)

            mean_square(0)
            normed(X, X)
            dve.wait_ge(s_vt, 1)
            V.tensor_copy(gain[:, :], ps[2][:, 0:48]).then_inc(s_ve, 1)
            for c in range(4):
                lo(0, c)
            dve.wait_ge(s_ve, 1)
            tiles_lo(h_hi, h_lo, 0)
            mean_square(1)
            normed(M, M)
            ahead(0)
            store(0, 0, arena[:, A_MQ:A_MQ + 512], 1.0 / math.sqrt(MD))
            tiles_lo(m_hi, m_lo, 1)
            dve.wait_ge(s_wgh, 1)
            V.tensor_tensor(wgl[:, :, :], wgr[:, :, :], wgh[:, :, :].bitcast(F32), ALU.subtract).then_inc(s_wgl, 1)
            dve.wait_ge(s_oh, 32)
            dve.wait_ge(s_neg, 1)
            V.tensor_copy(work[0:BUCKETS + 1, 1536:2560].rearrange("p (h n) -> p h n", h=HEADS),
                          work[0:BUCKETS + 1, W_RB:W_RB + HEADS].unsqueeze(2).to_broadcast([BUCKETS + 1, HEADS, P])).then_inc(s_wide, 1)
            dve.wait_ge(s_vt, 2)
            V.tensor_copy(conv[:, :, :].rearrange("p a n -> p (a n)"), ps[2][:, 0:352])
            V.tensor_copy(peT[:, :, :].rearrange("p a n -> p (a n)"), ps[3][:, 0:64]).then_inc(s_ve, 1)
            for h in range(HEADS):
                dve.wait_ge(s_vt, 3 + h)
                V.tensor_copy(arena[:, A_NQ + REL * h:A_NQ + REL * (h + 1)], ps[4 + h % 3][:, 0:REL]).then_inc(s_rbc, 1)
            ahead(1)
            store(1, 1, arena[:, A_MQ + 512:A_MQ + 1024], 1.0 / math.sqrt(MD))
            dve.wait_ge(s_gt, 1)
            V.tensor_scalar(sig[:, :, :], sig[:, :, :], 0.5, 0.5, ALU.mult, ALU.add).then_inc(s_sig, 1)
            stores(2, 1, A_MQ + 1024, 1.0 / math.sqrt(MD))
            stores(Q0["mk"], 4, A_MK)

            with dve.Fori(0, 2) as i:
                ch.enter(i, 2)
                for j in range(2):
                    m, q = 2 * i + j, 2 * i + (Q0["nq"] + j)
                    ahead(q, (0,))
                    dve.wait_ge(m_s, m + 1)
                    V.tensor_reduce(st[:, 32:34], bank(2), AX.X, ALU.max, negate=True).then_inc(m_nm, 1)
                    dve.wait_ge(m_ex, m + 1)
                    ch.link(V.reciprocal(st[:, 36:38], st[:, 34:36]))
                    for t in range(TT):
                        e = V.tensor_scalar(work[:, W_MP + S * t:W_MP + S * (t + 1)], work[:, W_MP + S * t:W_MP + S * (t + 1)],
                                            st[:, 36 + t:37 + t], None, ALU.mult)
                    e.then_inc(m_p, 1)
                    ahead(q, (1, 2))
                    dve.wait_ge(m_t, m + 1)
                    V.tensor_copy(work[:, W_MPT:W_MPT + 512], ps[4][:, :]).then_inc(m_te, 1)
                    ahead(q, (3,))
                    store(q, j, arena[:, bass.ds(1024 * i + (A_NQ + 512 * j), 512)], DH ** -0.5)
                    dve.wait_ge(m_h, m + 1)
                    V.tensor_tensor(m_lo[:, bass.ds(2 * m, 2), :], bank(6), m_hi[:, bass.ds(2 * m, 2), :].bitcast(F32),
                                    ALU.subtract).then_inc(m_l, 1)
                ch.leave(2, 2)
            for n, dst in enumerate((A_KC, A_VC)):
                ahead(Q0["kv0"] + n)
                store(Q0["kv0"] + n, n, arena[:, dst:dst + 512])
            dve.wait_ge(evac[0], G0["kv0"] // 2 + 1)
            dve.wait_ge(evac[1], G0["kv0"] // 2 + 1)
            dve.wait_ge(s_ve, 2)
            for n, src in enumerate((A_KC, A_VC)):
                base = arena[:, src:src + 512]
                for g in range(GROUPS):
                    e = V.tensor_tensor(work[:, 960 * n:960 * (n + 1)].rearrange("p (j g n) -> p j g n", j=CB, g=GROUPS)[:, :, g, :],
                                        bass.AP(base.tensor, base.offset + S * g, [base.ap[0], [1, CB], [CS, NC]]),
                                        peT[:, n, :].unsqueeze(2).to_broadcast([P, CB, NC]), ALU.add)
                e.then_inc(s_bk, 1)
            for n in range(2):
                dve.wait_ge(s_bkh, n + 1)
                V.tensor_tensor(blocks(r_lo, n), work[:, 960 * n:960 * (n + 1)], blocks(r_hi, n).bitcast(F32), ALU.subtract).then_inc(s_bkl, 1)
            ahead(Q0["kv0"] + 2)
            store(Q0["kv0"] + 2, 0, arena[:, A_KS:A_KS + 512])
            for n in range(2):
                ahead(Q0["cmp"] + 2 * n)
                ahead(Q0["cmp"] + 2 * n + 1)
                b = (G0["cmp"] + n) % 2
                dve.wait_ge(s_ht, n + 1)
                V.scalar_tensor_tensor(hid[:, n], hid[:, n], 1.0, bank(b)[:, :, 0:2 * NC], ALU.add, ALU.mult).then_inc(evac[b], 1)
            for n, dst in enumerate((A_VS, A_KW, A_VW)):
                ahead(Q0["kv1"] + n)
                store(Q0["kv1"] + n, (G0["kv1"] + n) % 2, arena[:, dst:dst + 512])
                if n == 1:
                    dve.wait_ge(s_kc, 1)
                    V.tensor_scalar(kc[:, :, :], ps[7][:, 0:2 * NC].rearrange("p (g n) -> p g n", g=GROUPS), 0.5, None, ALU.mult)
                    V.tensor_scalar(vc[:, :, :], ps[7][0:NC, 256:512].rearrange("p (g n) -> p g n", g=GROUPS), 0.5, None,
                                    ALU.mult).then_inc(s_kce, 1)

            dve.wait_ge(s_tab, 16)
            dve.wait_ge(s_sig, 1)
            for g, (ph, base) in enumerate((("rqk", A_RQ), ("rv", A_RV))):
                with dve.Fori(0, 2) as i:
                    ch.enter(i, NSA_LINKS * 2)
                    for j in range(2):
                        h, q = 2 * i + (HPG * g + j), 2 * i + (Q0[ph] + j)
                        ahead(q, (0,))
                        dve.wait_ge(a_s, h + 2)

                        def bias(lo_, n, step=1):
                            return tables[:, bass.ds(S * h + lo_, n, step)]
                        p0, p1 = work[:, W_P:W_P + 256].rearrange("p (b n) -> p b n", b=2), work[:, W_P + 256:W_P + 768].rearrange("p (b n) -> p b n", b=2)
                        c0, c1 = work[:, W_P + 768:W_P + 768 + NC0], work[:, W_P + 768 + NC0:W_P + 768 + NC0 + NC]
                        ch.add(V.tensor_tensor(p0, bank(2)[:, :, 0:P], bias(P, P).unsqueeze(1).to_broadcast([P, 2, P]), ALU.add))
                        ch.add(V.tensor_tensor(p1, bank(3), bias(0, S).unsqueeze(1).to_broadcast([P, 2, S]), ALU.add))
                        ch.add(V.tensor_tensor(c0, ps[2][:, P:P + NC0], bias(P + CB - 1, NC0, CS), ALU.add))
                        ch.link(V.tensor_tensor(c1, ps[2][:, P + CS:P + CS + NC], bias(CB - 1, NC, CS), ALU.add))
                        ch.add(V.tensor_reduce(st[:, 7:9], p0, AX.X, ALU.max))
                        ch.add(V.tensor_reduce(st[:, 10:12], p1, AX.X, ALU.max))
                        ch.add(V.tensor_reduce(st[:, 6:7], c0, AX.X, ALU.max))
                        ch.link(V.tensor_reduce(st[:, 9:10], c1, AX.X, ALU.max))
                        V.tensor_scalar(st[:, 0:6], st[:, 6:12], MASKED / 10, -1.0, ALU.max, ALU.mult).then_inc(a_nm, 1)
                        dve.wait_ge(a_ex, h + 1)
                        ch.link(V.tensor_scalar(st[:, 12:18], st[:, 12:18], 1e-30, None, ALU.max))
                        ch.link(V.reciprocal(st[:, 18:24], st[:, 12:18]))
                        ch.link(V.tensor_tensor(st[:, 18:24].rearrange("p (t b) -> p t b", t=TT), st[:, 18:24].rearrange("p (t b) -> p t b", t=TT),
                                                sig[:, :, :].rearrange("p t (b h) -> p t b h", b=3)[:, :, :, bass.ds(h, 1)].squeeze(), ALU.mult))
                        for n, (o, w) in enumerate(NSA_P):
                            e = V.tensor_scalar(work[:, W_P + o:W_P + o + w], work[:, W_P + o:W_P + o + w],
                                                st[:, 18 + n:19 + n], None, ALU.mult)
                        e.then_inc(a_p, 1)
                        ahead(q, (1, 2))
                        dve.wait_ge(a_t, h + 1)
                        V.tensor_copy(work[:, W_PT:W_PT + 384], ps[4][:, 0:384])
                        V.tensor_copy(work[0:NC0, W_CT:W_CT + P], ps[4][0:NC0, 384:512]).then_inc(a_tv, 1)
                        ahead(q, (3,))
                        store(q, j, arena[:, bass.ds(1024 * i + (base + 512 * j), 512)])
                        dve.wait_ge(a_h, h + 1)
                        V.tensor_tensor(m_lo[:, bass.ds(h + 8, 1), :], ps[6][:, 0:S].unsqueeze(1), m_hi[:, bass.ds(h + 8, 1), :].bitcast(F32),
                                        ALU.subtract).then_inc(a_l, 1)
                    ch.leave(2, NSA_LINKS * 2)
            with dve.Fori(0, 2) as i:
                for j in range(2):
                    ahead(2 * i + (Q0["rg"] + j))
                    dve.wait_ge(s_rgt, 2 * i + (j + 1))
                    V.scalar_tensor_tensor(arena[:, bass.ds(1024 * i + (A_RG + 512 * j), 512)], work[:, W_RGT:W_RGT + 512], 1.0,
                                           ps[j][:, :], ALU.add, ALU.mult).then_inc(evac[j], 1)

            dve.wait_ge(s_tab2, 16)
            for b in range(2):
                dve.wait_ge(evac[b], G0["bg0"] // 2)
            qk = arena[:, A_RQ:A_RQ + 2048].rearrange("p (a n) -> p a n", a=2)
            with dve.Fori(0, 2) as i:
                ch.enter(i, RET_LINKS * 2)
                for j in range(2):
                    r, q = 2 * i + j, 2 * i + (Q0["bg0"] + j)
                    ahead(q, (0,))
                    qr = work[:, W_QR:W_QR + 512]
                    ch.add(V.tensor_tensor(qr.rearrange("p (a n) -> p a n", a=2), qk[:, :, bass.ds(S * r, S)],
                                           tables[:, 0:512].rearrange("p (a n) -> p a n", a=2), ALU.mult))
                    dve.wait_ge(r_r, r + 1)
                    ch.link(V.tensor_tensor(work[:, W_RT:W_RT + 512], ps[2][:, :], tables[:, 512:1024], ALU.mult))
                    V.tensor_tensor(qr, qr, work[:, W_RT:W_RT + 512], ALU.add).then_inc(r_q, 1)
                    ahead(q, (1,))
                    dve.wait_ge(r_i, r + 1)
                    V.tensor_tensor(work[:, W_IN:W_IN + S], ps[3][:, 0:S], tables[:, bass.ds(S * r + 1024, S)], ALU.mult)
                    V.tensor_tensor(work[:, W_IN + S:W_IN + S + P], ps[3][:, S:S + P], tables[:, bass.ds(S * r + 1024, P)],
                                    ALU.mult).then_inc(r_d, 1)
                    ahead(q, (2,))
                    dve.wait_ge(r_o, r + 1)
                    for t in range(TT):
                        ch.add(V.bn_stats(st[:, 46 + 6 * t:52 + 6 * t], bank(4, t)))
                    ch.wait()
                    dve.sem_inc(s_stats, 1)
                    for t in range(TT):
                        ch.add(V.bn_aggr(st[:, 24 + 2 * t:26 + 2 * t], st[:, 46 + 6 * t:52 + 6 * t]))
                    ch.wait()
                    V.tensor_scalar(st[:, 42:44], st[:, 24:28].rearrange("p (t a) -> p a t", t=TT)[:, 1, :], EPS, None, ALU.add).then_inc(r_v, 1)
                    dve.wait_ge(r_rs, r + 1)
                    for t in range(TT):
                        ch.add(V.tensor_scalar(work[:, W_YB + S * t:W_YB + S * (t + 1)], bank(4, t), st[:, 24 + 2 * t:25 + 2 * t],
                                               st[:, 44 + t:45 + t], ALU.subtract, ALU.mult))
                    ch.wait()
                    V.scalar_tensor_tensor(work[:, W_YB:W_YB + 512], work[:, W_YB:W_YB + 512], 0.5,
                                           arena[:, bass.ds(512 * r + A_RG, 512)], ALU.mult, ALU.mult).then_inc(r_y, 1)
                    ahead(q, (3,))
                    dve.wait_ge(r_h, r + 1)
                    V.tensor_tensor(r_lo[:, bass.ds(2 * r, 2), :], bank(6), r_hi[:, bass.ds(2 * r, 2), :].bitcast(F32),
                                    ALU.subtract).then_inc(r_l, 1)
                ch.leave(2, RET_LINKS * 2)

            for n in range(3):
                q0 = Q0[f"bg{n}"] + (4 if n == 0 else 0)
                with dve.Fori(0, 2 if n == 0 else 4) as i:
                    for j in range(2):
                        ahead(2 * i + (q0 + j))
                for b in range(2):
                    dve.wait_ge(evac[b], G0[f"br{n}"] // 2)
                with dve.Fori(0, 2) as i:
                    ch.enter(i, 4 if n else 0)
                    for j in range(2):
                        for b in range(2):
                            q = 2 * i + (Q0[f"br{n}"] + j)
                            ahead(q, (2 * b, 2 * b + 1))
                            at = 2048 * i + (1024 * j + 512 * b)
                            gate, sum_ = arena[:, bass.ds(at + A_GATE, 512)], arena[:, bass.ds(at + A_MERGED, 512)]
                            dve.wait_ge(pe_done, 4 * q + (2 * b + 2))
                            if n == 0:
                                V.scalar_tensor_tensor(sum_, gate, 1.0, ps[b][:, :], ALU.add, ALU.mult).then_inc(evac[b], 1)
                            else:
                                tmp = work[:, W_TMP + 512 * b:W_TMP + 512 * (b + 1)]
                                ch.link(V.scalar_tensor_tensor(tmp, gate, 1.0, ps[b][:, :], ALU.add, ALU.mult))
                                V.tensor_tensor(sum_, sum_, tmp, ALU.add).then_inc(evac[b], 1)
                    ch.leave(2, 4 if n else 0)
            ch.link(V.memset(st[:, 61:62], 0.0))
            V.tensor_copy(st[:, 62:63], st[:, 61:62]).then_inc(s_mg, 1)
            dve.wait_ge(s_mgh, 1)
            V.scalar_tensor_tensor(m_lo[:, :, :].rearrange("p k s -> p (k s)"), merged, 0.5,
                                   m_hi[:, :, :].rearrange("p k s -> p (k s)").bitcast(F32), ALU.mult, ALU.subtract).then_inc(s_mgl, 1)
            with dve.Fori(0, 4) as i:
                for j in range(2):
                    ahead(2 * i + (Q0["wo"] + j))
                    dve.wait_ge(pe_done, 8 * i + (4 * (Q0["wo"] + j) + 4))
                    V.tensor_copy(M[:, :, bass.ds(512 * i + GW * j, GW)], bank(j)).then_inc(evac[j], 1)
            for b in range(2):
                dve.wait_ge(evac[b], G0["up0"] // 2)
            V.tensor_copy(st[:, 62:63], st[:, 61:62]).then_inc(s_mo, 1)

            def post(dst, n, done):
                for t in range(TT):
                    ch.link(V.scalar_tensor_tensor(M[:, t, :], M[:, t, :], st[:, 4 + t:5 + t], GP, ALU.mult, ALU.mult))
                    V.tensor_tensor(dst[:, t, :], M[:, t, :], X[:, t, :], ALU.add).then_inc(done, 1)

            mean_square(2)
            dve.wait_ge(s_gpost, 16)
            for t in range(TT):
                dve.wait_ge(s_x[t], 32)
            post(X, 2, s_x2)
            mean_square(3)
            normed(M, X)
            tiles_lo(h_hi, h_lo, 2)

            def up_quads(q, s):
                for n in range(4):
                    a, j = n // 2, n % 2
                    ahead(q + n)
                    dve.wait_ge(s_y, 4 * s + (n + 1))
                    for t in range(2):
                        col = 4 * s + (44 * j + 2 * a + t)
                        y = work[:, W_Y + 512 * j + S * t:W_Y + 512 * j + S * (t + 1)]
                        ch.link(V.scalar_tensor_tensor(y[:, 1:S], bank(j, t)[:, 0:S - 1], conv[:, 1, bass.ds(col, 1)], y[:, 1:S],
                                                       ALU.mult, ALU.add))
                        e = V.scalar_tensor_tensor(y[:, 2:S], bank(j, t)[:, 0:S - 2], conv[:, 0, bass.ds(col, 1)], y[:, 2:S],
                                                   ALU.mult, ALU.add)
                    e.then_inc(evac[j], 1)
                    if j:
                        dve.wait_ge(s_gelu, 2 * s + (a + 1))
                        dve.wait_ge(evac[1], up_group(s) + a + 1)
                        if not isinstance(s, int):
                            dve.wait_ge(s_ah, s)
                        V.tensor_tensor(work[:, W_PROD + 512 * a:W_PROD + 512 * (a + 1)], work[:, W_Y:W_Y + 512],
                                        work[:, W_Y + 512:W_Y + 1024], ALU.mult).then_inc(s_prod, 1)

            def split_lo(s):
                dve.wait_ge(s_ah, s + 1)
                V.tensor_tensor(r_lo[:, 0:4, :].rearrange("p k s -> p (k s)"), work[:, W_PROD:W_PROD + 1024],
                                r_hi[:, 0:4, :].rearrange("p k s -> p (k s)").bitcast(F32), ALU.subtract).then_inc(s_al, 1)

            def down(q, j, last=False):
                for c in range(4):
                    if not last:
                        ahead(q, (c,))
                    dve.wait_ge(pe_done, 4 * q + (c + 1))
                    f = M[:, :, (4 * j + c) * GW:(4 * j + c + 1) * GW]
                    V.tensor_tensor(f, bank(c % 2), f, ALU.add).then_inc(evac[c % 2], 1)

            up_quads(Q0["up0"], 0)
            split_lo(0)
            dve.wait_ge(s_f0, 1)
            with dve.Fori(0, STEPS - 1) as i:
                ch.enter(i, 8)
                q = 6 * i + Q0["ffn"]
                up_quads(q, i + 1)
                down(q + 4, 0)
                down(q + 5, 1)
                split_lo(i + 1)
                ch.leave(STEPS - 1, 8)
            down(Q0["dn"], 0)
            down(Q0["dn"] + 1, 1, last=True)
            mean_square(4)
            dve.wait_ge(s_gpost, 32)
            post(M, 4, s_fin)

        @block.tensor
        def _(pe):
            T = nc.tensor

            def chunk_t(q, c, b, hi_, lo_, k0, first, last, n=S):
                pe.wait_ge(lo_done, 4 * q + (c + 1))
                for k in range(CK):
                    for t in range(2):
                        wh, wl = whi[:, c, k, t * P:(t + 1) * P], wlo[:, c, k, t * P:(t + 1) * P]
                        xh, xl = hi_(k0 + k), lo_(k0 + k)
                        o = bank(b, t)[:, 0:n]
                        T.matmul(o, wh, xh, start=first and k == 0 and t == 0, stop=False, skip_group_check=True)
                        T.matmul(o, wh, xl, start=False, stop=False, skip_group_check=True)
                        e = T.matmul(o, wl, xh, start=False, stop=last and k == CK - 1, skip_group_check=True)
                e.then_inc(pe_done, 1)

            def chunk_n(q, c, b, hi_, lo_, k0, first, last):
                pe.wait_ge(lo_done, 4 * q + (c + 1))
                for k in range(CK):
                    for t in range(TT):
                        xh, xl = hi_(k0 + k)[:, t * P:(t + 1) * P], lo_(k0 + k)[:, t * P:(t + 1) * P]
                        wh, wl = whi[:, c, k, :], wlo[:, c, k, :]
                        o = bank(b, t)
                        T.matmul(o, xh, wh, start=first and k == 0 and t == 0, stop=False, skip_group_check=True)
                        T.matmul(o, xh, wl, start=False, stop=False, skip_group_check=True)
                        e = T.matmul(o, xl, wh, start=False, stop=last and k == CK - 1, skip_group_check=True)
                e.then_inc(pe_done, 1)

            def tiles(src, first=0):
                return lambda k: src[:, first + k, :]

            H, MM = (tiles(h_hi), tiles(h_lo)), (tiles(m_hi), tiles(m_lo))
            YM = MM
            YA = (tiles(m_hi, 8), tiles(m_lo, 8))
            YR = (tiles(r_hi), tiles(r_lo))

            def bank_free(b, before):
                if not (isinstance(before, int) and before == 0):
                    pe.wait_ge(evac[b], before)

            def quad(chunk, q, b, before, x_, between=None):
                bank_free(b, before)
                for c in range(4):
                    chunk(q, c, b, *x_, 4 * c, c == 0, c == 3)
                    if between and c in between:
                        between[c]()

            def quads(chunk, ph, trips, x_, k=0):
                with pe.Fori(0, trips) as i:
                    for j in range(2):
                        quad(chunk, 2 * i + (Q0[ph] + k + j), j, i + (G0[ph] + k) // 2, x_)

            def transpose_tiles(src, n):
                for k in range(0, KT, 2):
                    if k >= 12:
                        pe.wait_ge(s_trl, (KT * n + k) // 2 - 5)
                    for u in range(2):
                        for t in range(TT):
                            e = T.transpose(bank(2 + (k // 2) % 6, u)[:, t * P:(t + 1) * P], src[:, t, (k + u) * P:(k + u + 1) * P], eye[:, :])
                    e.then_inc(s_tr, 1)

            for free in (m_o, a_s):
                pe.sem_inc(free, 1)
            pe.wait_ge(s_rows, 48)
            pe.wait_ge(s_eye, 16)
            T.transpose(ps[2][:, 0:48], work[0:48, 0:P], eye[0:48, 0:48]).then_inc(s_vt, 1)
            pe.wait_ge(s_ve, 1)
            pe.wait_ge(s_xn, 2)
            transpose_tiles(X, 0)
            pe.wait_ge(s_trl, KT // 2)
            quad(chunk_t, 0, 0, 0, H)
            pe.wait_ge(s_xn, 4)
            transpose_tiles(M, 1)
            quad(chunk_t, 1, 1, 0, H)
            pe.wait_ge(s_rows2, 96)
            pe.wait_ge(s_trl, KT)
            for k in range(4):
                T.transpose(ps[2][:, 88 * k:88 * (k + 1)], work[0:88, P * (1 + k):P * (2 + k)], eye[0:88, 0:88])
            for k in range(2):
                e = T.transpose(ps[3][:, 32 * k:32 * (k + 1)], work[0:CB, P * (5 + k):P * (6 + k)], eye[0:CB, 0:CB])
            e.then_inc(s_vt, 1)
            pe.wait_ge(s_wide, 1)
            for h in range(HEADS):
                if h >= 3:
                    pe.wait_ge(s_rbc, h - 2)
                T.matmul(ps[4 + h % 3][:, 0:REL], work[0:BUCKETS + 1, 1536 + P * h:1536 + P * (h + 1)],
                         work[0:BUCKETS + 1, 1024:1024 + REL], start=True, stop=True).then_inc(s_vt, 1)
            pe.wait_ge(s_wgl, 1)
            for t in range(TT):
                o = ps[7][:, 448 + 24 * t:448 + 24 * (t + 1)]
                for k in range(KT):
                    xh, xl = h_hi[:, k, t * P:(t + 1) * P], h_lo[:, k, t * P:(t + 1) * P]
                    T.matmul(o, xh, wgh[:, k, :], start=k == 0, stop=False)
                    T.matmul(o, xh, wgl[:, k, :], start=False, stop=False)
                    e = T.matmul(o, xl, wgh[:, k, :], start=False, stop=k == KT - 1)
            e.then_inc(s_gp, 1)
            quads(chunk_t, "mq", 1, H, 2)
            quads(chunk_t, "mk", 2, MM)
            quads(chunk_n, "mv", 2, MM)

            with pe.Fori(0, 2) as i:
                for j in range(2):
                    m, q = 2 * i + j, 2 * i + (Q0["nq"] + j)

                    def scores():
                        pe.wait_ge(m_st, 2 * m + 2)
                        if j == 0:
                            for b in range(2):
                                pe.wait_ge(evac[b], G0["nq"] // 2)
                        for t in range(TT):
                            for d in range(2):
                                e = T.matmul(bank(2, t), work[:, W_MS + S * d + P * t:W_MS + S * d + P * (t + 1)],
                                             arena[:, bass.ds(512 * m + (A_MK + S * d), S)], start=d == 0, stop=d == 1)
                        e.then_inc(m_s, 1)

                    def transposes():
                        pe.wait_ge(m_p, m + 1)
                        for u in range(TT):
                            for t in range(TT):
                                e = T.transpose(bank(4, u)[:, t * P:(t + 1) * P], work[:, W_MP + S * t + P * u:W_MP + S * t + P * (u + 1)], eye[:, :])
                        e.then_inc(m_t, 1)

                    def output():
                        pe.wait_ge(m_te, m + 1)
                        pe.wait_ge(m_l, m + 1)
                        for d in range(2):
                            for u in range(TT):
                                e = T.matmul(bank(6, d), work[:, W_MVS + S * u + P * d:W_MVS + S * u + P * (d + 1)],
                                             work[:, W_MPT + S * u:W_MPT + S * (u + 1)], start=u == 0, stop=u == 1)
                        e.then_inc(m_o, 1)

                    quad(chunk_t, q, j, i + G0["nq"] // 2, H, {0: scores, 2: transposes, 3: output})
            for n in range(3):
                quad(chunk_t, Q0["kv0"] + n, n % 2, (G0["kv0"] + n) // 2, H)
            pe.wait_ge(s_bkl, 2)
            for n in range(2):
                g = G0["cmp"] + n
                bank_free(g % 2, g // 2)
                bh = [(lambda k, src=src: blocks(src, n)[:, 2 * NC * k:2 * NC * (k + 1)]) for src in (r_hi, r_lo)]
                for c in range(8):
                    chunk_t(Q0["cmp"] + 2 * n + c // 4, c % 4, g % 2, *bh, 4 * c, c == 0, c == 7, 2 * NC)
            for n in range(3):
                g = G0["kv1"] + n
                quad(chunk_t if n == 1 else chunk_n, Q0["kv1"] + n, g % 2, g // 2, H)
                if n == 0:
                    for b in range(2):
                        pe.wait_ge(evac[b], G0["kv1"] // 2 + (b == 0))
                    pe.wait_ge(s_pe2, 32)
                    for t in range(2):
                        T.matmul(ps[7][:, 0:2 * NC], w2[:, 0, t, :], hid[:, 0, t, :], start=t == 0, stop=t == 1)
                    for g2 in range(GROUPS):
                        for t in range(2):
                            e = T.matmul(ps[7][0:NC, 256 + DH * g2:256 + DH * (g2 + 1)], hid[:, 1, t, NC * g2:NC * (g2 + 1)],
                                         w2[:, 1, t, :], start=t == 0, stop=t == 1)
                    e.then_inc(s_kc, 1)

            for g, ph in enumerate(("rqk", "rv")):
                with pe.Fori(0, 2) as i:
                    for j in range(2):
                        h, q = 2 * i + (HPG * g + j), 2 * i + (Q0[ph] + j)

                        def scores():
                            pe.wait_ge(a_st, h + 1)
                            if g == 0 and j == 0:
                                pe.wait_ge(s_kce, 1)
                                for b in range(2):
                                    pe.wait_ge(evac[b], G0["rqk"] // 2)
                            q0, q1 = work[:, W_QS:W_QS + P], work[:, W_QS + P:W_QS + S]
                            for n, k in enumerate((A_KS, A_KW)):
                                T.matmul(bank(2, n)[:, 0:P], q0, arena[:, k + S * g:k + S * g + P], start=True, stop=True)
                                T.matmul(bank(3, n), q1, arena[:, k + S * g:k + S * (g + 1)], start=True, stop=True)
                            T.matmul(ps[2][:, P:P + NC0], q0, kc[:, g, 0:NC0], start=True, stop=True)
                            T.matmul(ps[2][:, P + CS:P + CS + NC], q1, kc[:, g, :], start=True, stop=True).then_inc(a_s, 1)

                        def transposes():
                            pe.wait_ge(a_p, h + 1)
                            for n in range(2):
                                b = ps[4 + n]
                                T.transpose(b[:, 0:P], work[:, W_P + P * n:W_P + P * (n + 1)], eye[:, :])
                                for u in range(TT):
                                    o = W_P + S * (1 + n) + P * u
                                    T.transpose(b[:, P * (1 + u):P * (2 + u)], work[:, o:o + P], eye[:, :])
                            T.transpose(ps[4][0:NC0, 384:512], work[:, W_P + 768:W_P + 768 + NC0], eye[:, :])
                            T.transpose(ps[5][0:NC, 384:512], work[:, W_P + 768 + NC0:W_P + 768 + NC0 + NC], eye[:, :]).then_inc(a_t, 1)

                        def output():
                            pe.wait_ge(a_ta, h + 1)
                            pe.wait_ge(a_tv, h + 1)
                            pe.wait_ge(a_l, h + 1)
                            for n, v in enumerate((A_VS, A_VW)):
                                T.matmul(ps[6][:, 0:S], arena[:, v + DH * g:v + DH * (g + 1)], work[:, W_PT + 384 * n:W_PT + 384 * n + S],
                                         start=n == 0, stop=False, skip_group_check=True)
                                T.matmul(ps[6][:, P:S], arena[:, v + S + DH * g:v + S + DH * (g + 1)],
                                         work[:, W_PT + 384 * n + S:W_PT + 384 * (n + 1)], start=False, stop=False, skip_group_check=True)
                            T.matmul(ps[6][:, 0:P], vc[0:NC0, g, :], work[0:NC0, W_CT:W_CT + P], start=False, stop=False, skip_group_check=True)
                            T.matmul(ps[6][:, P:S], vc[:, g, :], work[0:NC, W_CT + P:W_CT + S], start=False, stop=True,
                                     skip_group_check=True).then_inc(a_o, 1)

                        quad((chunk_t, chunk_n)[g], q, j, i + G0[ph] // 2, H, {0: scores, 2: transposes, 3: output})
            quads(chunk_n, "rg", 2, H)

            pe.wait_ge(s_const, 16)
            with pe.Fori(0, 2) as i:
                for j in range(2):
                    r, q = 2 * i + j, 2 * i + (Q0["bg0"] + j)

                    def rotate():
                        for n, a in enumerate((A_RQ, A_RK)):
                            e = T.matmul(bank(2, n), rot[:, :], arena[:, bass.ds(S * r + a, S)], start=True, stop=True)
                        e.then_inc(r_r, 1)

                    def inner():
                        pe.wait_ge(r_q, r + 1)
                        k = W_QR + S
                        T.matmul(ps[3][:, 0:S], work[:, k:k + P], work[:, W_QR:W_QR + S], start=True, stop=True)
                        T.matmul(ps[3][:, S:S + P], work[:, k + P:k + S], work[:, W_QR + P:W_QR + S], start=True, stop=True).then_inc(r_i, 1)

                    def output():
                        pe.wait_ge(r_d, r + 1)
                        v = [arena[:, bass.ds(512 * r + (A_RV + S * u), S)] for u in range(TT)]
                        T.matmul(bank(4, 0), work[:, W_IN:W_IN + P], v[0], start=True, stop=True)
                        T.matmul(bank(4, 1), work[:, W_IN + P:W_IN + 2 * P], v[0], start=True, stop=False)
                        T.matmul(bank(4, 1), work[:, W_IN + 2 * P:W_IN + 3 * P], v[1], start=False, stop=True).then_inc(r_o, 1)

                    def transposes():
                        pe.wait_ge(r_y, r + 1)
                        pe.wait_ge(r_l, r + 1)
                        for u in range(2):
                            for t in range(TT):
                                e = T.transpose(bank(6, u)[:, t * P:(t + 1) * P], work[:, W_YB + S * t + P * u:W_YB + S * t + P * (u + 1)], eye[:, :])
                        e.then_inc(r_t, 1)

                    quad(chunk_t, q, j, i + G0["bg0"] // 2, H, {0: rotate, 1: inner, 2: output, 3: transposes})
            for n, y in enumerate((YM, YA, YR)):
                if n == 0:
                    quads(chunk_t, "bg0", 2, H, 4)
                else:
                    quads(chunk_t, f"bg{n}", 4, H)
                if n == 2:
                    pe.wait_ge(r_l, RH + 1)
                with pe.Fori(0, 2) as i:
                    for j in range(2):
                        for c in range(4):
                            if c % 2 == 0:
                                bank_free(c // 2, 2 * i + (G0[f"br{n}"] // 2 + j))
                            chunk_t(2 * i + (Q0[f"br{n}"] + j), c, c // 2, *y, 4 * (c % 2), c % 2 == 0, c % 2 == 1)
            pe.wait_ge(s_mgl, 1)
            quads(chunk_n, "wo", 4, MM)
            pe.wait_ge(s_xn, 6)
            transpose_tiles(M, 2)
            pe.wait_ge(s_trl, 3 * KT // 2)

            def up_quads(q, s):
                for n in range(4):
                    quad(chunk_t, q + n, n % 2, up_group(s) + n // 2, H)

            def down(q, before):
                for c in range(4):
                    bank_free(c % 2, before + c // 2)
                    chunk_n(q, c, c % 2, *YR, 0, True, True)

            up_quads(Q0["up0"], 0)
            with pe.Fori(0, STEPS - 1) as i:
                q = 6 * i + Q0["ffn"]
                up_quads(q, i + 1)
                pe.wait_ge(s_al, i + 1)
                down(q + 4, 6 * i + (G0["ffn"] // 2 + 2))
                down(q + 5, 6 * i + (G0["ffn"] // 2 + 4))
            pe.wait_ge(s_al, STEPS)
            down(Q0["dn"], G0["dn"] // 2)
            down(Q0["dn"] + 1, G0["dn"] // 2 + 2)


def constants():
    eye = np.eye(P, dtype=np.float32)
    rot = np.zeros((P, P), np.float32)
    for d in range(P // 2):
        rot[d + P // 2, d] = -1.0
        rot[d, d + P // 2] = 1.0
    onehot = np.zeros((BUCKETS + 1, REL), np.float32)
    for c in range(REL):
        rel = S - 1 - c
        if rel < 0:
            onehot[BUCKETS, c] = 1.0
            continue
        b = rel
        if rel >= BUCKETS // 2:
            b = BUCKETS // 2 + int(math.log(rel / (BUCKETS // 2)) / math.log(MAXD / (BUCKETS // 2)) * (BUCKETS - BUCKETS // 2))
        onehot[min(b, BUCKETS - 1), c] = 1.0
    theta = (np.float32(1.0) / np.power(np.float32(10000.0), np.linspace(0.0, 1.0, RDK // 2, dtype=np.float32))).astype(np.float32)
    ang = (theta[:, None] * np.arange(S, dtype=np.float32)[None, :]).astype(np.float32).astype(np.float64)
    cos, sin = np.tile(np.cos(ang), (2, 1)), np.tile(np.sin(ang), (2, 1))
    scale = RDK ** -0.5
    parts = [cos, cos * scale, sin, sin * scale]
    diff = np.arange(S)[None, :] - np.arange(P)[:, None]
    for hh in range(RH):
        parts.append(np.where(diff >= 0, (1.0 - 2.0 ** (-5.0 - hh)) ** np.maximum(diff, 0), 0.0))
    return {"c_eye": eye, "c_rot": rot, "c_onehot": onehot, "c_ret": np.concatenate(parts, 1).astype(np.float32)}


_INS = ["x", "mem", "w_in", "cmp_pe_k", "cmp_w1_k", "cmp_w2_k", "cmp_pe_v", "cmp_w1_v", "cmp_w2_v", "rel_bias",
        "w_mem_kv", "w_br_nsa", "w_br_ret", "w_br_mem", "w_o", "w_up", "conv_w", "conv_b", "w_down", "g_pre_mix",
        "g_post_mix", "g_mem", "g_pre_ffn", "g_post_ffn"]


def kernel(**inputs):
    import concourse.bacc as bacc
    from concourse.bass_utils import run_bass_kernel_spmd

    nc = bacc.Bacc("TRN2", target_bir_lowering=False, num_devices=1)
    arrays = {f"in_{n}": np.ascontiguousarray(inputs[n]) for n in _INS}
    arrays.update(constants())
    args = [nc.dram_tensor(n, a.shape, mybir.dt.from_np(a.dtype), kind="ExternalInput").ap() for n, a in arrays.items()]
    scratch = nc.dram_tensor("bias_rows", (HEADS, P, REL), F32).ap()
    out = nc.dram_tensor("out_y", (1, S, D), F32, kind="ExternalOutput").ap()
    build(nc, *args, scratch, out)
    r = run_bass_kernel_spmd(nc, [arrays], core_ids=[0])
    return r.results[0]["out_y"]
```

```python
import math
from contextlib import ExitStack

import numpy as np
import concourse.bass as bass
from concourse import mybir

F32 = mybir.dt.float32
F32R = mybir.dt.float32r
ACT = mybir.ActivationFunctionType
ALU = mybir.AluOpType
AX = mybir.AxisListType

P = 128
S = 256
D = 2048
KT = D // P
TT = S // P
GW = 256
CK = 4
EPS = 1e-6
HEADS, GROUPS, DH = 8, 2, 128
HPG = HEADS // GROUPS
CB, CS = 32, 16
NC = (S - CB) // CS + 1
NC0 = (P - CB) // CS + 1
RH, RDK, RDV = 4, 128, 256
MH, MD = 4, 256
FF = 5632
BUCKETS, MAXD = 32, 128
MASKED = -1e30
REL = 384
STEPS = FF // 512

C_NQ = 0
C_KV = 1024
C_NG = C_KV + 1536
C_RQ = C_NG + 24
C_RK = C_RQ + 512
C_RV = C_RK + 512
C_RG = C_RV + 1024
C_MQ = C_RG + 1024
C_BG = C_MQ + 1024

PHASES = [("mq", 4, 4), ("mk", 4, 4), ("mv", 4, 4), ("nq", 4, 4), ("kv0", 3, 3), ("cmp", 4, 2),
          ("kv1", 3, 3), ("rqk", 4, 4), ("rv", 4, 4), ("rg", 4, 4),
          ("bg0", 8, 8), ("br0", 4, 8), ("bg1", 8, 8), ("br1", 4, 8), ("bg2", 8, 8), ("br2", 4, 8),
          ("wo", 8, 8), ("up0", 4, 4), ("ffn", 6 * (STEPS - 1), 4 * (STEPS - 1)), ("dn", 2, 0)]
Q0, G0 = {}, {}
_q = _g = 0
for _n, _a, _b in PHASES:
    Q0[_n], G0[_n] = _q, _g
    _q, _g = _q + _a, _g + _b
QUADS = _q

A_X, A_M = 0, 4096
A_MQ, A_MK, A_MV = 0, 2048, 4096
A_NQ = 6144
A_KC, A_VC, A_KS, A_VS, A_KW, A_VW = (8192 + 512 * n for n in range(6))
A_RQ, A_RK, A_RV, A_RG = 0, 1024, 4096, 6144
A_MERGED, A_GATE = 0, 8192
NSA_P = [(768, NC0), (0, P), (P, P), (768 + NC0, NC), (2 * P, S), (2 * P + S, S)]
W_P, W_PT, W_CT, W_QS = 0, 792, 1560, 1816
W_MP, W_MPT, W_MS, W_MVS = 0, 512, 1024, 1536
W_QR, W_RT, W_IN, W_YB = 0, 512, 1024, 1408
W_RGT = 2048
W_RB = 1408
W_SIG, W_HID = 0, 0
W_Y, W_PROD, W_TMP = 0, 1024, 0


NSA_LINKS, RET_LINKS = 11, 8
NSA_BEFORE, NSA_AFTER = (0, 1, 2), (3,)


class Chain:

    def __init__(self, eng, sem):
        self.eng, self.sem, self.n, self.base = eng, sem, 0, 0

    def add(self, ins):
        ins.then_inc(self.sem, 1)
        self.n += 1

    def wait(self):
        self.eng.wait_ge(self.sem, self.base + self.n)

    def link(self, ins):
        self.add(ins)
        self.wait()

    def enter(self, i, per):
        self.start = self.n
        self.base, self.n = self.start + per * i, 0

    def leave(self, trips, per):
        assert self.n == per, (self.n, per)
        self.base, self.n = 0, self.start + trips * per


def build(nc, x, mem, w_in, cmp_pe_k, cmp_w1_k, cmp_w2_k, cmp_pe_v, cmp_w1_v, cmp_w2_v, rel_bias,
          w_mem_kv, w_br_nsa, w_br_ret, w_br_mem, w_o, w_up, conv_w, conv_b, w_down, g_pre_mix,
          g_post_mix, g_mem, g_pre_ffn, g_post_ffn, c_eye, c_rot, c_onehot, c_ret, scratch, out):
    ctx = ExitStack()
    with ctx:
        def sb(name, shape, dt=F32):
            return ctx.enter_context(nc.sbuf_tensor(name, shape, dt))

        def sem(name):
            return ctx.enter_context(nc.semaphore(name))

        h_hi, h_lo = (sb(n, [P, KT, S], F32R) for n in ("h_hi", "h_lo"))
        m_hi, m_lo = (sb(n, [P, KT, S], F32R) for n in ("m_hi", "m_lo"))
        r_hi, r_lo = (sb(n, [P, 8 * S + P], F32R) for n in ("r_hi", "r_lo"))
        wraw = sb("wraw", [P, 4, CK, GW])
        whi, wlo = (sb(n, [P, 4, CK, GW], F32R) for n in ("whi", "wlo"))
        arena = sb("arena", [P, 12288])
        tables = sb("tables", [P, 2048])
        work = sb("work", [P, 2560])
        eye = sb("eye", [P, P])
        rot = sb("rot", [P, P])
        gain = sb("gain", [P, 3 * KT])
        conv = sb("conv", [P, 4, 88])
        wgr = sb("wgr", [P, KT, 24])
        wgh, wgl = (sb(n, [P, 24 * KT + P - 24], F32R) for n in ("wgh", "wgl"))
        sig = sb("sig", [P, TT, 24])
        kc = sb("kc", [P, GROUPS, CS])
        vc = sb("vc", [NC, GROUPS, DH])
        hid = sb("hid", [P, 2, 2, 2 * CS])
        w2 = sb("w2", [P, 2, 2, DH])
        peT = sb("peT", [P, 2, CB])
        st = sb("st", [P, 64])
        sq = sb("sq", [P, 2, TT, 8])

        ps = [ctx.enter_context(nc.psum_tensor(f"bank{i}", [P, 512], F32)) for i in range(8)]

        loaded = [sem(f"loaded{c}") for c in range(4)]
        hi_done, lo_done = sem("hi_done"), sem("lo_done")
        pe_done = sem("pe_done")
        evac = [sem(f"evac{b}") for b in range(2)]
        dch, ach, pch = sem("vector_chain"), sem("scalar_chain"), sem("pool_chain")
        s_x = [sem(f"x_in{n}") for n in range(2 * TT)]
        s_m = [sem(f"mem_in{n}") for n in range(2 * TT)]
        s_eye, s_const, s_rows, s_rows2 = sem("eye_in"), sem("rot_in"), sem("gain_rows_in"), sem("conv_rows_in")
        s_wg, s_pe2, s_oh = sem("wg_in"), sem("pe_w2_in"), sem("onehot_in")
        s_ssq, s_var, s_rstd, s_xn = sem("ssq"), sem("var"), sem("rstd"), sem("xn")
        s_tr, s_trh, s_trl = sem("transposed"), sem("tile_hi"), sem("tile_lo")
        s_half = sem("half_const")
        s_vt, s_ve, s_neg, s_wide = sem("vectors_transposed"), sem("vectors_out"), sem("masked_row"), sem("bias_columns")
        s_rb, s_rbc, s_scr, s_tab, s_tab2 = sem("bias_row"), sem("bias_row_out"), sem("bias_stored"), sem("bias_in"), sem("ret_in")
        s_wgh, s_wgl, s_gp, s_gt, s_sig = sem("wg_hi"), sem("wg_lo"), sem("gate_ps"), sem("gate_tanh"), sem("gate_sig")
        s_bk, s_bkh, s_bkl = sem("blocks"), sem("blocks_hi"), sem("blocks_lo")
        s_ht, s_hid, s_kc, s_kce = sem("hid_tanh"), sem("hid"), sem("kc_ps"), sem("kc_out")
        m_st, m_s, m_nm, m_ex, m_p, m_t, m_te, m_o, m_h, m_l = (sem("mem_" + n) for n in (
            "staged", "scores", "max", "exp", "probs", "transposed", "pt", "out", "hi", "lo"))
        a_st, a_s, a_nm, a_ex, a_p, a_t, a_ta, a_tv, a_o, a_h, a_l = (sem("nsa_" + n) for n in (
            "staged", "scores", "max", "exp", "probs", "transposed", "pt_win", "pt_sel", "out", "hi", "lo"))
        r_r, r_q, r_i, r_d, r_o, r_v, r_rs, r_y, r_t, r_h, r_l = (sem("ret_" + n) for n in (
            "rotated", "qk", "inner", "decayed", "out", "var", "rstd", "y", "transposed", "hi", "lo"))
        s_rgt, s_stats = sem("rg_tanh"), sem("stats_made")
        s_mg, s_mgh, s_mgl = sem("merged"), sem("merged_hi"), sem("merged_lo")
        s_gpost = sem("gpost_in")
        s_sq, s_pad, s_gsc = sem("group_squares"), sem("pads"), sem("gain_used")
        s_gtt, s_hn, s_htt, s_hcp = sem("gates_transposed"), sem("hidden"), sem("hidden_transposed"), sem("hidden_copied")
        s_x2 = sem("x2")
        s_y, s_gelu, s_prod, s_ah, s_al = sem("conv_tap2"), sem("gelu"), sem("prod"), sem("act_hi"), sem("act_lo")
        s_f0, s_dn = sem("f_zero"), sem("down_out")
        s_fin, s_out = sem("final"), sem("out_stored")

        block = ctx.enter_context(nc.Block())

        X = arena[:, A_X:A_X + 4096].rearrange("p (t n) -> p t n", t=TT)
        M = arena[:, A_M:A_M + 4096].rearrange("p (t n) -> p t n", t=TT)
        GP = tables[:, :]
        half = st[:, 60:61]

        def bank(g, t=None):
            b = ps[g][:, :].rearrange("p (t n) -> p t n", t=TT)
            return b if t is None else b[:, t, :]

        def blocks(src, n):
            return src[:, 1024 * n:1024 * (n + 1)].rearrange("p (j g n) -> p j g n", j=CB, g=GROUPS)[:, :, :, 0:NC]

        def wblocks(n):
            return work[:, 960 * n:960 * (n + 1)].rearrange("p (j g n) -> p j g n", j=CB, g=GROUPS)

        def up_group(s):
            return 2 * s + G0["up0"] // 2

        def piece(v, n):
            return v[:, n % 2, 1024 * (n // 2):1024 * (n // 2 + 1)]

        def rows(w, k0, col, n=GW, kt=CK):
            return w[0, k0 * P:(k0 + kt) * P, :].rearrange("(k p) n -> p k n", p=P)[:, :, bass.ds(col, n)]

        @block.sync
        def _(sp):
            def quad(q, src):
                for c in range(4):
                    if q:
                        sp.wait_ge(lo_done, 4 * (q - 1) + c + 1)
                    sp.dma_start(wraw[:, c], src(c)).then_inc(loaded[c], 16)

            def loop(q0, trips, per, sources):
                with sp.Fori(0, trips) as i:
                    free = [sp.snap(4 * per * i + (4 * (q0 - 1) + k + 1)) for k in range(4 * per)]
                    src = sources(i)
                    for j in range(per):
                        for c in range(4):
                            sp.wait_ge(lo_done, free[4 * j + c])
                            sp.dma_start(wraw[:, c], src[j](c)).then_inc(loaded[c], 16)

            def cols(w, base, count=2):
                def sources(i):
                    at = [sp.snap(count * GW * i + (base + GW * j)) for j in range(count)]
                    return [lambda c, o=o: rows(w, 4 * c, o) for o in at]
                return sources

            def quarters(dst, src, sems):
                for n in range(2 * TT):
                    sp.dma_start(piece(dst, n), src[0, (n % 2) * P:(n % 2 + 1) * P, 1024 * (n // 2):1024 * (n // 2 + 1)]).then_inc(sems[n], 16)

            quarters(X, x, s_x)
            for n, g in enumerate((g_pre_mix, g_mem, g_pre_ffn)):
                sp.dma_start(work[n * KT:(n + 1) * KT, 0:P], g.rearrange("o (k p) -> (o k) p", p=P)).then_inc(s_rows, 16)
            sp.dma_start(eye[:, :], c_eye[:, :]).then_inc(s_eye, 16)
            quad(0, lambda c: rows(w_in, 4 * c, C_MQ))
            quarters(M, mem, s_m)
            for k in range(3):
                sp.dma_start(work[0:88, P * (1 + k):P * (2 + k)],
                             conv_w[0, k:k + 1, :].rearrange("o (k p) -> (o k) p", p=P)).then_inc(s_rows2, 16)
            sp.dma_start(work[0:88, 4 * P:5 * P], conv_b.rearrange("o (k p) -> (o k) p", p=P)).then_inc(s_rows2, 16)
            sp.dma_start(work[0:CB, 5 * P:6 * P], cmp_pe_k[0]).then_inc(s_rows2, 16)
            sp.dma_start(work[0:CB, 6 * P:7 * P], cmp_pe_v[0]).then_inc(s_rows2, 16)
            sp.dma_start(work[0:BUCKETS, W_RB:W_RB + HEADS], rel_bias[:, :]).then_inc(s_oh, 16)
            sp.dma_start(work[0:BUCKETS + 1, 1024:1024 + REL], c_onehot[:, :]).then_inc(s_oh, 16)
            sp.dma_start(rot[:, :], c_rot[:, :]).then_inc(s_const, 16)
            sp.dma_start(wgr[:, :, :], rows(w_in, 0, C_NG, 24, KT)).then_inc(s_wg, 16)
            sp.dma_start(w2[:, 0], cmp_w2_k[0].rearrange("(k p) n -> p k n", p=P)).then_inc(s_pe2, 16)
            sp.dma_start(w2[:, 1], cmp_w2_v[0].rearrange("(k p) n -> p k n", p=P)).then_inc(s_pe2, 16)
            quad(1, lambda c: rows(w_in, 4 * c, C_MQ + GW))
            quad(2, lambda c: rows(w_in, 4 * c, C_MQ + 2 * GW))
            sp.wait_ge(s_rbc, HEADS)
            sp.dma_start(scratch.rearrange("h p n -> p h n"),
                         arena[:, A_GATE:A_GATE + HEADS * REL].rearrange("p (h n) -> p h n", h=HEADS)).then_inc(s_scr, 16)
            quad(3, lambda c: rows(w_in, 4 * c, C_MQ + 3 * GW))
            sp.wait_ge(s_scr, 16)
            sp.dma_start(tables[:, :].rearrange("p (h n) -> p h n", h=HEADS),
                         bass.AP(scratch.tensor, P - 1, [[REL - 1, P], [P * REL, HEADS], [1, S]])).then_inc(s_tab, 16)
            loop(Q0["mk"], 4, 2, cols(w_mem_kv[:, :, :], 0))
            loop(Q0["nq"], 2, 2, cols(w_in, C_NQ))
            for n in range(3):
                quad(Q0["kv0"] + n, lambda c: rows(w_in, 4 * c, C_KV + n * GW))
            for n, w in enumerate((cmp_w1_k, cmp_w1_v)):
                for j in range(2):
                    quad(Q0["cmp"] + 2 * n + j, lambda c: rows(w, 16 * j + 4 * c, 0))
            for n in range(3):
                quad(Q0["kv1"] + n, lambda c: rows(w_in, 4 * c, C_KV + (3 + n) * GW))
            loop(Q0["rqk"], 6, 2, cols(w_in, C_RQ))
            sp.wait_ge(a_nm, HEADS)
            sp.dma_start(tables[:, :], c_ret[:, :]).then_inc(s_tab2, 16)
            for n, (b, w) in enumerate(((2, w_br_mem), (0, w_br_nsa), (1, w_br_ret))):
                loop(Q0[f"bg{n}"], 4, 2, cols(w_in, C_BG + b * D))
                if n == 1:
                    sp.wait_ge(r_d, RH)
                    sp.dma_start(GP, g_post_mix.to_broadcast([P, D])).then_inc(s_gpost, 16)

                def pairs(i):
                    at = [sp.snap(4 * GW * i + GW * j) for j in range(4)]
                    return [lambda c, j=j: rows(w, 4 * (c % 2), at[2 * j + c // 2]) for j in range(2)]
                loop(Q0[f"br{n}"], 2, 2, pairs)
            for n in range(2):
                quad(Q0["wo"] + n, lambda c: rows(w_o, 4 * c, GW * n))
                if n == 0:
                    sp.wait_ge(s_mgl, KT // 2)
                    quarters(X, x, s_x)
            loop(Q0["wo"] + 2, 3, 2, cols(w_o, 2 * GW))

            def up_col(n):
                return (n // 2) * GW + (n % 2) * FF

            def down(r0):
                w = w_down[0, bass.ds(r0, 512), :].rearrange("(k p) n -> p k n", p=P)
                return [lambda c, j=j: w[:, :, (4 * j + c) * GW:(4 * j + c + 1) * GW] for j in range(2)]

            for n in range(4):
                quad(Q0["up0"] + n, lambda c: rows(w_up, 4 * c, up_col(n)))
                if n == 1:
                    sp.wait_ge(s_gsc, 1)
                    sp.dma_start(GP, g_post_ffn.to_broadcast([P, D])).then_inc(s_gpost, 16)

            def step(i):
                at = [sp.snap(512 * i + (512 + up_col(n))) for n in range(4)]
                return [lambda c, o=o: rows(w_up, 4 * c, o) for o in at] + down(sp.snap(512 * i))
            loop(Q0["ffn"], STEPS - 1, 6, step)
            for j in range(2):
                quad(Q0["dn"] + j, down((STEPS - 1) * 512)[j])
            for n in range(2 * TT):
                sp.wait_ge(s_fin, n + 1)
                sp.dma_start(out[0, (n % 2) * P:(n % 2 + 1) * P, 1024 * (n // 2):1024 * (n // 2 + 1)], piece(M, n)).then_inc(s_out, 16)
            sp.wait_ge(s_out, 16 * 2 * TT)

        @block.gpsimd
        def _(pool):
            nc.gpsimd.memset(half, -0.5).then_inc(s_half, 1)
            pool.wait_ge(s_half, 1)
            nc.gpsimd.memset(work[BUCKETS:BUCKETS + 1, W_RB:W_RB + HEADS], MASKED).then_inc(s_neg, 1)
            pool.wait_ge(s_neg, 1)
            for n, pad in enumerate((r_hi[:, 8 * S:], r_lo[:, 8 * S:], wgh[:, 24 * KT:], wgl[:, 24 * KT:])):
                nc.gpsimd.memset(pad.bitcast(F32), 0.0).then_inc(s_pad, 1)
                pool.wait_ge(s_pad, n + 1)

            def rstd(n):
                pool.wait_ge(s_var, n + 1)
                nc.gpsimd.tensor_tensor(st[:, 4:6], st[:, 2:4], half.to_broadcast([P, 2]), ALU.pow).then_inc(s_rstd, 1)

            rstd(0)
            rstd(1)
            pool.wait_ge(s_scr, 16)
            for b in range(2):
                pool.wait_ge(evac[b], G0["nq"] // 2)
            with pool.Fori(0, MH) as m:
                pool.wait_ge(m_o, m + 1)
                nc.gpsimd.tensor_copy(work[:, W_MS:W_MS + 512], arena[:, bass.ds(512 * m + A_MQ, 512)]).then_inc(m_st, 1)
                pool.wait_ge(m_st, 2 * m + 1)
                nc.gpsimd.tensor_copy(work[:, W_MVS:W_MVS + 512], arena[:, bass.ds(512 * m + A_MV, 512)]).then_inc(m_st, 1)
            pool.wait_ge(s_bkl, 2)
            with pool.Fori(0, HEADS) as h:
                pool.wait_ge(a_s, h + 1)
                nc.gpsimd.tensor_copy(work[:, W_QS:W_QS + S], arena[:, bass.ds(S * h + A_NQ, S)]).then_inc(a_st, 1)
            with pool.Fori(0, RH) as r:
                pool.wait_ge(r_v, r + 1)
                nc.gpsimd.tensor_tensor(st[:, 44:46], st[:, 42:44], half.to_broadcast([P, 2]), ALU.pow).then_inc(r_rs, 1)
            rstd(2)
            rstd(3)
            pool.wait_ge(s_trl, 3 * KT // 2)
            nc.gpsimd.memset(arena[:, A_M:A_M + 4096], 0.0).then_inc(s_f0, 1)
            rstd(4)

        @block.scalar
        def _(act):
            def hi(q, c):
                act.wait_ge(loaded[c], 16 * q + 16)
                if not (isinstance(q, int) and q == 0):
                    act.wait_ge(pe_done, 4 * q + (c - 3))
                nc.scalar.activation(whi[:, c], wraw[:, c], ACT.Copy).then_inc(hi_done, 1)

            def ahead(q, chunks=range(4)):
                for c in chunks:
                    hi(q + 1, c)

            def plain(q0, trips):
                with act.Fori(0, trips) as i:
                    for j in range(2):
                        ahead(2 * i + (q0 + j))

            def squares(n, src, sems):
                if n >= 2:
                    act.wait_ge(s_var, n - 1)
                for k in range(2 * TT):
                    act.wait_ge(*sems(k))
                    nc.scalar.activation((r_hi, r_lo)[k % 2][:, 1024 * (k // 2):1024 * (k // 2 + 1)], piece(src, k), ACT.Square,
                                         accum_out=sq[:, n % 2, k % 2, k // 2:k // 2 + 1]).then_inc(s_ssq, 1)

            def tiles_hi(dst, n):
                for k in range(0, KT, 2):
                    act.wait_ge(s_tr, (KT * n + k) // 2 + 1)
                    for u in range(2):
                        e = nc.scalar.activation(dst[:, k + u, :], bank(2 + (k // 2) % 6, u), ACT.Copy,
                                                 scale=gain[:, n * KT + k + u:n * KT + k + u + 1])
                    e.then_inc(s_trh, 1)

            squares(0, X, lambda k: (s_x[k], 16))
            for c in range(4):
                hi(0, c)
            act.wait_ge(s_ve, 1)
            tiles_hi(h_hi, 0)
            ahead(0)
            act.wait_ge(s_wg, 16)
            act.wait_ge(s_pad, 4)
            nc.scalar.activation(wgh[:, 0:24 * KT], wgr[:, :, :].rearrange("p k n -> p (k n)"), ACT.Copy).then_inc(s_wgh, 1)
            ahead(1)
            act.wait_ge(s_ssq, 4)
            squares(1, M, lambda k: (s_m[k], 16))
            act.wait_ge(s_gp, 1)
            nc.scalar.activation(work[0:24, W_SIG:W_SIG + S], ps[7][0:24, 0:S], ACT.Tanh, scale=0.5).then_inc(s_gt, 1)
            ahead(2)
            tiles_hi(m_hi, 1)
            ahead(3)
            plain(Q0["mk"], 4)

            with act.Fori(0, 2) as i:
                for j in range(2):
                    m, q = 2 * i + j, 2 * i + (Q0["nq"] + j)
                    act.wait_ge(m_nm, m + 1)
                    for t in range(TT):
                        e = nc.scalar.activation(work[:, W_MP + S * t:W_MP + S * (t + 1)], bank(2, t), ACT.Exp,
                                                 bias=st[:, 32 + t:33 + t], accum_out=st[:, 34 + t:35 + t])
                    e.then_inc(m_ex, 1)
                    ahead(q)
                    act.wait_ge(m_o, m + 2)
                    nc.scalar.activation(m_hi[:, bass.ds(2 * m, 2), :], bank(6), ACT.Copy).then_inc(m_h, 1)
            ahead(Q0["kv0"])
            ahead(Q0["kv0"] + 1)
            for n in range(2):
                act.wait_ge(s_bk, n + 1)
                nc.scalar.activation(blocks(r_hi, n), wblocks(n), ACT.Copy).then_inc(s_bkh, 1)
            ahead(Q0["kv0"] + 2)
            for n in range(2):
                ahead(Q0["cmp"] + 2 * n)
                ahead(Q0["cmp"] + 2 * n + 1)
                nc.scalar.activation(work[0:2 * CS, W_HID + S * n:W_HID + S * (n + 1)], ps[(G0["cmp"] + n) % 2][0:2 * CS, 0:S],
                                     ACT.Tanh, scale=0.5).then_inc(s_ht, 1)
            for n in range(3):
                ahead(Q0["kv1"] + n)

            for g, ph in enumerate(("rqk", "rv")):
                with act.Fori(0, 2) as i:
                    for j in range(2):
                        h, q = 2 * i + (HPG * g + j), 2 * i + (Q0[ph] + j)
                        act.wait_ge(a_nm, h + 1)
                        for n, (o, w) in enumerate(NSA_P):
                            e = nc.scalar.activation(work[:, W_P + o:W_P + o + w], work[:, W_P + o:W_P + o + w], ACT.Exp,
                                                     bias=st[:, n:n + 1], accum_out=st[:, 12 + n:13 + n])
                        e.then_inc(a_ex, 1)
                        ahead(q, NSA_BEFORE)
                        act.wait_ge(a_t, h + 1)
                        nc.scalar.activation(work[:, W_PT + 384:W_PT + 768], ps[5][:, 0:384], ACT.Copy)
                        nc.scalar.activation(work[0:NC, W_CT + P:W_CT + 2 * P], ps[5][0:NC, 384:512], ACT.Copy).then_inc(a_ta, 1)
                        ahead(q, NSA_AFTER)
                        act.wait_ge(a_o, h + 1)
                        nc.scalar.activation(m_hi[:, bass.ds(h + 8, 1), :], ps[6][:, 0:S].unsqueeze(1), ACT.Copy).then_inc(a_h, 1)
            with act.Fori(0, 2) as i:
                for j in range(2):
                    ahead(2 * i + (Q0["rg"] + j))
                    act.wait_ge(evac[1 - j], i + (G0["rg"] // 2 + j))
                    nc.scalar.activation(work[:, W_RGT:W_RGT + 512], ps[j][:, :], ACT.Tanh, scale=0.5).then_inc(s_rgt, 1)

            for n in range(3):
                q0 = Q0[f"bg{n}"]
                for b in range(2):
                    act.wait_ge(evac[b], G0[f"bg{n}"] // 2)
                if n == 0:
                    with act.Fori(0, 2) as i:
                        for j in range(2):
                            r, q = 2 * i + j, 2 * i + (q0 + j)
                            ahead(q)
                            nc.scalar.activation(arena[:, bass.ds(1024 * i + (A_GATE + 512 * j), 512)], ps[j][:, :],
                                                 ACT.Tanh, scale=0.5).then_inc(evac[j], 1)
                            act.wait_ge(r_t, r + 1)
                            nc.scalar.activation(r_hi[:, bass.ds(512 * r, 512)], ps[6][:, :], ACT.Copy).then_inc(r_h, 1)
                with act.Fori(0, 2 if n == 0 else 4) as i:
                    for j in range(2):
                        k = 8 - (4 if n == 0 else 8) + j
                        ahead(2 * i + (q0 + k))
                        nc.scalar.activation(arena[:, bass.ds(1024 * i + (A_GATE + 512 * k), 512)], ps[j][:, :],
                                             ACT.Tanh, scale=0.5).then_inc(evac[j], 1)
                if n < 2:
                    plain(Q0[f"br{n}"], 2)
            with act.Fori(0, 2) as i:
                for j in range(2):
                    for b in range(2):
                        ahead(2 * i + (Q0["br2"] + j), (2 * b, 2 * b + 1))
                        k = 4 * i + (2 * j + b)
                        act.wait_ge(s_mg, k + 1)
                        nc.scalar.activation(m_hi[:, bass.ds(2 * k, 2), :].rearrange("p k s -> p (k s)"),
                                             arena[:, bass.ds(512 * k + A_MERGED, 512)], ACT.Copy, scale=0.5).then_inc(s_mgh, 1)
            act.wait_ge(s_var, 1)
            with act.Fori(0, 4) as i:
                for j in range(2):
                    ahead(2 * i + (Q0["wo"] + j))
                    for t in range(TT):
                        e = nc.scalar.activation(work[:, 512 * j + S * t:512 * j + S * (t + 1)], bank(j, t), ACT.Square,
                                                 accum_out=sq[:, 0, t, bass.ds(2 * i + j, 1)])
                    e.then_inc(s_sq, 1)
            squares(3, X, lambda k: (s_x2, k + 1))
            tiles_hi(h_hi, 2)

            def up_quads(q, s):
                for n in range(4):
                    a, j = n // 2, n % 2
                    ahead(q + n)
                    if not (isinstance(s, int) and a == 0):
                        act.wait_ge(s_prod, 2 * s + a)
                    for t in range(2):
                        col = 4 * s + (44 * j + 2 * a + t)
                        e = nc.scalar.activation(work[:, W_Y + 512 * j + S * t:W_Y + 512 * j + S * (t + 1)], bank(j, t),
                                                 ACT.Identity, bias=conv[:, 3, bass.ds(col, 1)], scale=conv[:, 2, bass.ds(col, 1)])
                    e.then_inc(s_y, 1)
                    if j:
                        act.wait_ge(evac[0], up_group(s) + a + 1)
                        nc.scalar.activation(work[:, W_Y:W_Y + 512], work[:, W_Y:W_Y + 512], ACT.Gelu_apprx_tanh).then_inc(s_gelu, 1)

            def split_hi(s):
                act.wait_ge(s_prod, 2 * s + 2)
                nc.scalar.activation(r_hi[:, 0:1024], work[:, W_PROD:W_PROD + 1024], ACT.Copy).then_inc(s_ah, 1)

            up_quads(Q0["up0"], 0)
            split_hi(0)
            with act.Fori(0, STEPS - 1) as i:
                q = 6 * i + Q0["ffn"]
                up_quads(q, i + 1)
                ahead(q + 4)
                ahead(q + 5)
                split_hi(i + 1)
            for g in range(8):
                if g < 4:
                    ahead(Q0["dn"], (g,))
                act.wait_ge(s_dn, 4 + 8 * (STEPS - 1) + g + 1)
                for t in range(TT):
                    e = nc.scalar.activation(h_hi[:, 2 * g + t, :], M[:, t, GW * g:GW * (g + 1)], ACT.Square,
                                             accum_out=sq[:, 0, t, g:g + 1])
                e.then_inc(s_sq, 1)

        @block.vector
        def _(dve):
            V = nc.vector
            ch = Chain(dve, dch)
            for free in (m_l, a_l, r_l):
                dve.sem_inc(free, 1)
            dve.sem_inc(s_dn, 4)

            def lo(q, c):
                dve.wait_ge(hi_done, 4 * q + (c + 1))
                V.tensor_tensor(wlo[:, c], wraw[:, c], whi[:, c].bitcast(F32), ALU.subtract).then_inc(lo_done, 1)

            def ahead(q, chunks=range(4)):
                for c in chunks:
                    lo(q + 1, c)

            def store(q, b, dst, scale=None):
                dve.wait_ge(pe_done, 4 * q + 4)
                if scale is None:
                    return V.tensor_copy(dst, ps[b][:, :]).then_inc(evac[b], 1)
                return V.tensor_scalar(dst, ps[b][:, :], scale, None, ALU.mult).then_inc(evac[b], 1)

            def stores(q0, trips, base, scale=None):
                with dve.Fori(0, trips) as i:
                    for j in range(2):
                        ahead(2 * i + (q0 + j))
                        store(2 * i + (q0 + j), j, arena[:, bass.ds(1024 * i + (base + 512 * j), 512)], scale)

            def mean_square(n, parts, ready):
                dve.wait_ge(*ready)
                ch.link(V.tensor_reduce(st[:, 0:2], sq[:, n % 2, :, 0:parts], AX.X, ALU.add))
                V.tensor_scalar(st[:, 2:4], st[:, 0:2], 1.0 / D, EPS, ALU.mult, ALU.add).then_inc(s_var, 1)
                dve.wait_ge(s_rstd, n + 1)

            def normed(dst, src):
                for k in range(2 * TT):
                    V.tensor_scalar(piece(dst, k), piece(src, k), st[:, 4 + k % 2:5 + k % 2], None, ALU.mult).then_inc(s_xn, 1)

            def tiles_lo(dst_hi, dst, n):
                for k in range(0, KT, 2):
                    dve.wait_ge(s_trh, (KT * n + k) // 2 + 1)
                    for u in range(2):
                        e = V.scalar_tensor_tensor(dst[:, k + u, :], bank(2 + (k // 2) % 6, u), gain[:, n * KT + k + u:n * KT + k + u + 1],
                                                   dst_hi[:, k + u, :].bitcast(F32), ALU.mult, ALU.subtract)
                    e.then_inc(s_trl, 1)

            dve.wait_ge(s_vt, 1)
            V.tensor_copy(gain[:, :], ps[2][:, 0:48]).then_inc(s_ve, 1)
            mean_square(0, 2, (s_ssq, 4))
            normed(X, X)
            for c in range(4):
                lo(0, c)
            dve.wait_ge(s_ve, 1)
            tiles_lo(h_hi, h_lo, 0)
            ahead(0)
            store(0, 0, arena[:, A_MQ:A_MQ + 512], 1.0 / math.sqrt(MD))
            dve.wait_ge(s_wgh, 1)
            V.tensor_tensor(wgl[:, 0:24 * KT], wgr[:, :, :].rearrange("p k n -> p (k n)"), wgh[:, 0:24 * KT].bitcast(F32),
                            ALU.subtract).then_inc(s_wgl, 1)
            dve.wait_ge(s_oh, 32)
            dve.wait_ge(s_neg, 1)
            V.tensor_copy(work[0:BUCKETS + 1, 1536:2560].rearrange("p (h n) -> p h n", h=HEADS),
                          work[0:BUCKETS + 1, W_RB:W_RB + HEADS].unsqueeze(2).to_broadcast([BUCKETS + 1, HEADS, P])).then_inc(s_wide, 1)
            ahead(1)
            store(1, 1, arena[:, A_MQ + 512:A_MQ + 1024], 1.0 / math.sqrt(MD))
            dve.wait_ge(s_vt, 2)
            V.tensor_copy(conv[:, :, :].rearrange("p a n -> p (a n)"), ps[2][:, 0:352])
            V.tensor_copy(peT[:, :, :].rearrange("p a n -> p (a n)"), ps[3][:, 0:64]).then_inc(s_ve, 1)
            for h in range(HEADS):
                dve.wait_ge(s_vt, 3 + h)
                V.tensor_copy(arena[:, A_GATE + REL * h:A_GATE + REL * (h + 1)], ps[4 + h % 3][:, 0:REL]).then_inc(s_rbc, 1)
            mean_square(1, 2, (s_ssq, 8))
            normed(M, M)
            ahead(2)
            store(2, 0, arena[:, A_MQ + 1024:A_MQ + 1536], 1.0 / math.sqrt(MD))
            dve.wait_ge(s_gtt, 1)
            V.tensor_scalar(sig[:, :, :], ps[7][:, 256:304].rearrange("p (t n) -> p t n", t=TT), 0.5, 0.5, ALU.mult, ALU.add).then_inc(s_sig, 1)
            tiles_lo(m_hi, m_lo, 1)
            ahead(3)
            store(3, 1, arena[:, A_MQ + 1536:A_MQ + 2048], 1.0 / math.sqrt(MD))
            stores(Q0["mk"], 4, A_MK)

            with dve.Fori(0, 2) as i:
                ch.enter(i, 2)
                for j in range(2):
                    m, q = 2 * i + j, 2 * i + (Q0["nq"] + j)
                    dve.wait_ge(m_s, m + 1)
                    V.tensor_reduce(st[:, 32:34], bank(2), AX.X, ALU.max, negate=True).then_inc(m_nm, 1)
                    ahead(q, (0,))
                    dve.wait_ge(m_ex, m + 1)
                    ch.link(V.reciprocal(st[:, 36:38], st[:, 34:36]))
                    for t in range(TT):
                        e = V.tensor_scalar(work[:, W_MP + S * t:W_MP + S * (t + 1)], work[:, W_MP + S * t:W_MP + S * (t + 1)],
                                            st[:, 36 + t:37 + t], None, ALU.mult)
                    e.then_inc(m_p, 1)
                    ahead(q, (1, 2))
                    dve.wait_ge(m_t, m + 1)
                    V.tensor_copy(work[:, W_MPT:W_MPT + 512], ps[4][:, :]).then_inc(m_te, 1)
                    ahead(q, (3,))
                    store(q, j, arena[:, bass.ds(1024 * i + (A_NQ + 512 * j), 512)], DH ** -0.5)
                    dve.wait_ge(m_h, m + 1)
                    V.tensor_tensor(m_lo[:, bass.ds(2 * m, 2), :], bank(6), m_hi[:, bass.ds(2 * m, 2), :].bitcast(F32),
                                    ALU.subtract).then_inc(m_l, 1)
                ch.leave(2, 2)
            for n, dst in enumerate((A_KC, A_VC)):
                ahead(Q0["kv0"] + n)
                store(Q0["kv0"] + n, n, arena[:, dst:dst + 512])
            dve.wait_ge(evac[0], G0["kv0"] // 2 + 1)
            dve.wait_ge(evac[1], G0["kv0"] // 2 + 1)
            dve.wait_ge(s_ve, 2)
            for n, src in enumerate((A_KC, A_VC)):
                base = arena[:, src:src + 512]
                for g in range(GROUPS):
                    e = V.tensor_tensor(work[:, 960 * n:960 * (n + 1)].rearrange("p (j g n) -> p j g n", j=CB, g=GROUPS)[:, :, g, :],
                                        bass.AP(base.tensor, base.offset + S * g, [base.ap[0], [1, CB], [CS, NC]]),
                                        peT[:, n, :].unsqueeze(2).to_broadcast([P, CB, NC]), ALU.add)
                e.then_inc(s_bk, 1)
            for n in range(2):
                dve.wait_ge(s_bkh, n + 1)
                V.tensor_tensor(blocks(r_lo, n), wblocks(n), blocks(r_hi, n).bitcast(F32), ALU.subtract).then_inc(s_bkl, 1)
            ahead(Q0["kv0"] + 2)
            store(Q0["kv0"] + 2, 0, arena[:, A_KS:A_KS + 512])
            for n in range(2):
                ahead(Q0["cmp"] + 2 * n)
                ahead(Q0["cmp"] + 2 * n + 1)
                b = (G0["cmp"] + n) % 2
                dve.wait_ge(s_ht, n + 1)
                hn = work[0:2 * CS, W_HID + S * n:W_HID + S * (n + 1)]
                V.scalar_tensor_tensor(hn, hn, 1.0, ps[b][0:2 * CS, 0:S], ALU.add, ALU.mult).then_inc(evac[b], 1)
            for n, dst in enumerate((A_VS, A_KW, A_VW)):
                ahead(Q0["kv1"] + n)
                store(Q0["kv1"] + n, (G0["kv1"] + n) % 2, arena[:, dst:dst + 512])
                if n == 0:
                    dve.wait_ge(s_htt, 1)
                    V.tensor_copy(hid[:, :, :, :].rearrange("p a t n -> p (a t n)"), ps[7][:, 0:8 * CS]).then_inc(s_hcp, 1)
                if n == 1:
                    dve.wait_ge(s_kc, 1)
                    V.tensor_scalar(kc[:, :, :], ps[7][:, 8 * CS:10 * CS].rearrange("p (g n) -> p g n", g=GROUPS), 0.5, None, ALU.mult)
                    V.tensor_scalar(vc[:, :, :], ps[7][0:NC, 256:512].rearrange("p (g n) -> p g n", g=GROUPS), 0.5, None,
                                    ALU.mult).then_inc(s_kce, 1)

            dve.wait_ge(s_tab, 16)
            dve.wait_ge(s_sig, 1)
            for g, (ph, base) in enumerate((("rqk", A_RQ), ("rv", A_RV))):
                with dve.Fori(0, 2) as i:
                    ch.enter(i, NSA_LINKS * 2)
                    for j in range(2):
                        h, q = 2 * i + (HPG * g + j), 2 * i + (Q0[ph] + j)
                        dve.wait_ge(a_s, h + 2)

                        def bias(lo_, n, step=1):
                            return tables[:, bass.ds(S * h + lo_, n, step)]
                        p0, p1 = work[:, W_P:W_P + 256].rearrange("p (b n) -> p b n", b=2), work[:, W_P + 256:W_P + 768].rearrange("p (b n) -> p b n", b=2)
                        c0, c1 = work[:, W_P + 768:W_P + 768 + NC0], work[:, W_P + 768 + NC0:W_P + 768 + NC0 + NC]
                        ch.add(V.tensor_tensor(p0, bank(2)[:, :, 0:P], bias(P, P).unsqueeze(1).to_broadcast([P, 2, P]), ALU.add))
                        ch.add(V.tensor_tensor(p1, bank(3), bias(0, S).unsqueeze(1).to_broadcast([P, 2, S]), ALU.add))
                        ch.add(V.tensor_tensor(c0, ps[2][:, P:P + NC0], bias(P + CB - 1, NC0, CS), ALU.add))
                        ch.link(V.tensor_tensor(c1, ps[2][:, P + CS:P + CS + NC], bias(CB - 1, NC, CS), ALU.add))
                        ch.add(V.tensor_reduce(st[:, 7:9], p0, AX.X, ALU.max))
                        ch.add(V.tensor_reduce(st[:, 10:12], p1, AX.X, ALU.max))
                        ch.add(V.tensor_reduce(st[:, 6:7], c0, AX.X, ALU.max))
                        ch.link(V.tensor_reduce(st[:, 9:10], c1, AX.X, ALU.max))
                        V.tensor_scalar(st[:, 0:6], st[:, 6:12], MASKED / 10, -1.0, ALU.max, ALU.mult).then_inc(a_nm, 1)
                        ahead(q, NSA_BEFORE[:1])
                        dve.wait_ge(a_ex, h + 1)
                        ch.link(V.tensor_scalar(st[:, 12:18], st[:, 12:18], 1e-30, None, ALU.max))
                        ch.link(V.reciprocal(st[:, 18:24], st[:, 12:18]))
                        ch.link(V.tensor_tensor(st[:, 18:24].rearrange("p (t b) -> p t b", t=TT), st[:, 18:24].rearrange("p (t b) -> p t b", t=TT),
                                                sig[:, :, :].rearrange("p t (b h) -> p t b h", b=3)[:, :, :, bass.ds(h, 1)].squeeze(), ALU.mult))
                        for n, (o, w) in enumerate(NSA_P):
                            e = V.tensor_scalar(work[:, W_P + o:W_P + o + w], work[:, W_P + o:W_P + o + w],
                                                st[:, 18 + n:19 + n], None, ALU.mult)
                        e.then_inc(a_p, 1)
                        ahead(q, NSA_BEFORE[1:])
                        dve.wait_ge(a_t, h + 1)
                        V.tensor_copy(work[:, W_PT:W_PT + 384], ps[4][:, 0:384])
                        V.tensor_copy(work[0:NC0, W_CT:W_CT + P], ps[4][0:NC0, 384:512]).then_inc(a_tv, 1)
                        ahead(q, NSA_AFTER)
                        store(q, j, arena[:, bass.ds(1024 * i + (base + 512 * j), 512)])
                        dve.wait_ge(a_h, h + 1)
                        V.tensor_tensor(m_lo[:, bass.ds(h + 8, 1), :], ps[6][:, 0:S].unsqueeze(1), m_hi[:, bass.ds(h + 8, 1), :].bitcast(F32),
                                        ALU.subtract).then_inc(a_l, 1)
                    ch.leave(2, NSA_LINKS * 2)
            with dve.Fori(0, 2) as i:
                for j in range(2):
                    ahead(2 * i + (Q0["rg"] + j))
                    dve.wait_ge(s_rgt, 2 * i + (j + 1))
                    V.scalar_tensor_tensor(arena[:, bass.ds(1024 * i + (A_RG + 512 * j), 512)], work[:, W_RGT:W_RGT + 512], 1.0,
                                           ps[j][:, :], ALU.add, ALU.mult).then_inc(evac[j], 1)

            dve.wait_ge(s_tab2, 16)
            for b in range(2):
                dve.wait_ge(evac[b], G0["bg0"] // 2)
            qk = arena[:, A_RQ:A_RQ + 2048].rearrange("p (a n) -> p a n", a=2)
            with dve.Fori(0, 2) as i:
                ch.enter(i, RET_LINKS * 2)
                for j in range(2):
                    r, q = 2 * i + j, 2 * i + (Q0["bg0"] + j)
                    qr = work[:, W_QR:W_QR + 512]
                    ch.add(V.tensor_tensor(qr.rearrange("p (a n) -> p a n", a=2), qk[:, :, bass.ds(S * r, S)],
                                           tables[:, 0:512].rearrange("p (a n) -> p a n", a=2), ALU.mult))
                    dve.wait_ge(r_r, r + 1)
                    ch.link(V.tensor_tensor(work[:, W_RT:W_RT + 512], ps[2][:, :], tables[:, 512:1024], ALU.mult))
                    V.tensor_tensor(qr, qr, work[:, W_RT:W_RT + 512], ALU.add).then_inc(r_q, 1)
                    ahead(q, (0,))
                    dve.wait_ge(r_i, r + 1)
                    V.tensor_tensor(work[:, W_IN:W_IN + S], ps[3][:, 0:S], tables[:, bass.ds(S * r + 1024, S)], ALU.mult)
                    V.tensor_tensor(work[:, W_IN + S:W_IN + S + P], ps[3][:, S:S + P], tables[:, bass.ds(S * r + 1024, P)],
                                    ALU.mult).then_inc(r_d, 1)
                    ahead(q, (1,))
                    dve.wait_ge(r_o, r + 1)
                    for t in range(TT):
                        ch.add(V.bn_stats(st[:, 46 + 6 * t:52 + 6 * t], bank(4, t)))
                    ch.wait()
                    dve.sem_inc(s_stats, 1)
                    for t in range(TT):
                        ch.add(V.bn_aggr(st[:, 24 + 2 * t:26 + 2 * t], st[:, 46 + 6 * t:52 + 6 * t]))
                    ch.wait()
                    V.tensor_scalar(st[:, 42:44], st[:, 24:28].rearrange("p (t a) -> p a t", t=TT)[:, 1, :], EPS, None, ALU.add).then_inc(r_v, 1)
                    dve.wait_ge(r_rs, r + 1)
                    for t in range(TT):
                        ch.add(V.tensor_scalar(work[:, W_YB + S * t:W_YB + S * (t + 1)], bank(4, t), st[:, 24 + 2 * t:25 + 2 * t],
                                               st[:, 44 + t:45 + t], ALU.subtract, ALU.mult))
                    ch.wait()
                    V.scalar_tensor_tensor(work[:, W_YB:W_YB + 512], work[:, W_YB:W_YB + 512], 0.5,
                                           arena[:, bass.ds(512 * r + A_RG, 512)], ALU.mult, ALU.mult).then_inc(r_y, 1)
                    ahead(q, (2, 3))
                    dve.wait_ge(r_h, r + 1)
                    V.tensor_tensor(r_lo[:, bass.ds(512 * r, 512)], ps[6][:, :], r_hi[:, bass.ds(512 * r, 512)].bitcast(F32),
                                    ALU.subtract).then_inc(r_l, 1)
                ch.leave(2, RET_LINKS * 2)

            for n in range(3):
                q0 = Q0[f"bg{n}"] + (4 if n == 0 else 0)
                with dve.Fori(0, 2 if n == 0 else 4) as i:
                    for j in range(2):
                        ahead(2 * i + (q0 + j))
                for b in range(2):
                    dve.wait_ge(evac[b], G0[f"br{n}"] // 2)
                with dve.Fori(0, 2) as i:
                    ch.enter(i, 4 if n else 0)
                    for j in range(2):
                        for b in range(2):
                            q, k = 2 * i + (Q0[f"br{n}"] + j), 4 * i + (2 * j + b)
                            ahead(q, (2 * b, 2 * b + 1))
                            gate, sum_ = arena[:, bass.ds(512 * k + A_GATE, 512)], arena[:, bass.ds(512 * k + A_MERGED, 512)]
                            dve.wait_ge(pe_done, 4 * q + (2 * b + 2))
                            if n == 0:
                                V.scalar_tensor_tensor(sum_, gate, 1.0, ps[b][:, :], ALU.add, ALU.mult).then_inc(evac[b], 1)
                                continue
                            tmp = work[:, W_TMP + 512 * b:W_TMP + 512 * (b + 1)]
                            ch.link(V.scalar_tensor_tensor(tmp, gate, 1.0, ps[b][:, :], ALU.add, ALU.mult))
                            e = V.tensor_tensor(sum_, sum_, tmp, ALU.add)
                            if n == 1:
                                e.then_inc(evac[b], 1)
                                continue
                            dve.sem_inc(evac[b], 1)
                            e.then_inc(s_mg, 1)
                            dve.wait_ge(s_mgh, k + 1)
                            V.scalar_tensor_tensor(m_lo[:, bass.ds(2 * k, 2), :].rearrange("p k s -> p (k s)"), sum_, 0.5,
                                                   m_hi[:, bass.ds(2 * k, 2), :].rearrange("p k s -> p (k s)").bitcast(F32),
                                                   ALU.mult, ALU.subtract).then_inc(s_mgl, 1)
                    ch.leave(2, 4 if n else 0)
            dve.wait_ge(s_gpost, 16)
            with dve.Fori(0, 4) as i:
                for j in range(2):
                    ahead(2 * i + (Q0["wo"] + j))
                    dve.wait_ge(s_sq, 2 * i + (j + 1))
                    V.tensor_tensor(M[:, :, bass.ds(512 * i + GW * j, GW)], bank(j),
                                    GP[:, bass.ds(512 * i + GW * j, GW)].unsqueeze(1).to_broadcast([P, TT, GW]), ALU.mult).then_inc(evac[j], 1)
            mean_square(2, 8, (s_sq, 8))
            dve.wait_ge(evac[0], G0["up0"] // 2)
            dve.wait_ge(evac[1], G0["up0"] // 2)
            dve.sem_inc(s_gsc, 1)

            def post(dst, k, done):
                V.scalar_tensor_tensor(piece(dst, k), piece(M, k), st[:, 4 + k % 2:5 + k % 2], piece(X, k), ALU.mult, ALU.add).then_inc(done, 1)

            for k in range(2 * TT):
                dve.wait_ge(s_x[k], 32)
                post(X, k, s_x2)
            mean_square(3, 2, (s_ssq, 12))
            normed(M, X)
            tiles_lo(h_hi, h_lo, 2)

            def up_quads(q, s):
                for n in range(4):
                    a, j = n // 2, n % 2
                    ahead(q + n)
                    dve.wait_ge(s_y, 4 * s + (n + 1))
                    for tap in (1, 0):
                        for t in range(2):
                            d = 2 - tap
                            y = work[:, W_Y + 512 * j + S * t + d:W_Y + 512 * j + S * (t + 1)]
                            e = V.scalar_tensor_tensor(y, bank(j, t)[:, 0:S - d], conv[:, tap, bass.ds(4 * s + (44 * j + 2 * a + t), 1)], y,
                                                       ALU.mult, ALU.add)
                            if tap:
                                ch.add(e)
                        if tap:
                            ch.wait()
                    e.then_inc(evac[j], 1)
                    if j:
                        dve.wait_ge(s_gelu, 2 * s + (a + 1))
                        dve.wait_ge(evac[1], up_group(s) + a + 1)
                        if not isinstance(s, int):
                            dve.wait_ge(s_ah, s)
                        V.tensor_tensor(work[:, W_PROD + 512 * a:W_PROD + 512 * (a + 1)], work[:, W_Y:W_Y + 512],
                                        work[:, W_Y + 512:W_Y + 1024], ALU.mult).then_inc(s_prod, 1)

            def split_lo(s):
                dve.wait_ge(s_ah, s + 1)
                V.tensor_tensor(r_lo[:, 0:1024], work[:, W_PROD:W_PROD + 1024], r_hi[:, 0:1024].bitcast(F32), ALU.subtract).then_inc(s_al, 1)

            def down_group(q, g):
                dve.wait_ge(pe_done, 4 * q + (g + 1))
                f = M[:, :, GW * g:GW * (g + 1)]
                return V.tensor_tensor(f, bank(2 + g % 4), f, ALU.add)

            def down(q):
                for g in range(8):
                    ahead(q + g // 4, (g % 4,))
                    down_group(q, g).then_inc(s_dn, 1)

            up_quads(Q0["up0"], 0)
            split_lo(0)
            dve.wait_ge(s_f0, 1)
            with dve.Fori(0, STEPS - 1) as i:
                ch.enter(i, 8)
                q = 6 * i + Q0["ffn"]
                up_quads(q, i + 1)
                down(q + 4)
                split_lo(i + 1)
                ch.leave(STEPS - 1, 8)
            dve.wait_ge(s_gpost, 32)

            def times_gain(g):
                dve.wait_ge(s_sq, 8 + g + 1)
                f = M[:, :, GW * g:GW * (g + 1)]
                ch.add(V.tensor_tensor(f, f, GP[:, GW * g:GW * (g + 1)].unsqueeze(1).to_broadcast([P, TT, GW]), ALU.mult))

            for g in range(8):
                if g < 4:
                    ahead(Q0["dn"], (g,))
                down_group(Q0["dn"], g).then_inc(s_dn, 1)
                if g:
                    times_gain(g - 1)
            times_gain(7)
            mean_square(4, 8, (s_sq, 16))
            for k in range(2 * TT):
                post(M, k, s_fin)

        @block.tensor
        def _(pe):
            T = nc.tensor

            def chunk_t(q, c, b, hi_, lo_, k0, first, last, n=S):
                pe.wait_ge(lo_done, 4 * q + (c + 1))
                for k in range(CK):
                    for t in range(2):
                        wh, wl = whi[:, c, k, t * P:(t + 1) * P], wlo[:, c, k, t * P:(t + 1) * P]
                        xh, xl = hi_(k0 + k), lo_(k0 + k)
                        o = bank(b, t)[:, 0:n]
                        T.matmul(o, wh, xh, start=first and k == 0 and t == 0, stop=False, skip_group_check=True)
                        T.matmul(o, wh, xl, start=False, stop=False, skip_group_check=True)
                        e = T.matmul(o, wl, xh, start=False, stop=last and k == CK - 1, skip_group_check=True)
                e.then_inc(pe_done, 1)

            def chunk_n(q, c, b, hi_, lo_, k0, first, last):
                pe.wait_ge(lo_done, 4 * q + (c + 1))
                for k in range(CK):
                    for t in range(TT):
                        xh, xl = hi_(k0 + k)[:, t * P:(t + 1) * P], lo_(k0 + k)[:, t * P:(t + 1) * P]
                        wh, wl = whi[:, c, k, :], wlo[:, c, k, :]
                        o = bank(b, t)
                        T.matmul(o, xh, wh, start=first and k == 0 and t == 0, stop=False, skip_group_check=True)
                        T.matmul(o, xh, wl, start=False, stop=False, skip_group_check=True)
                        e = T.matmul(o, xl, wh, start=False, stop=last and k == CK - 1, skip_group_check=True)
                e.then_inc(pe_done, 1)

            def tiles(src, first=0):
                return lambda k: src[:, first + k, :]

            def flat(src):
                return lambda k: src[:, S * k:S * (k + 1)]

            H, MM = (tiles(h_hi), tiles(h_lo)), (tiles(m_hi), tiles(m_lo))
            YM = MM
            YA = (tiles(m_hi, 8), tiles(m_lo, 8))
            YR = (flat(r_hi), flat(r_lo))

            def bank_free(b, before):
                if not (isinstance(before, int) and before == 0):
                    pe.wait_ge(evac[b], before)

            def quad(chunk, q, b, before, x_, between={}, tiles_ready=None):
                if -1 in between:
                    between[-1]()
                bank_free(b, before)
                for c in range(4):
                    if tiles_ready is not None:
                        pe.wait_ge(s_trl, tiles_ready + 2 * c + 2)
                    chunk(q, c, b, *x_, 4 * c, c == 0, c == 3)
                    if c in between:
                        between[c]()

            def quads(chunk, ph, trips, x_, k=0):
                with pe.Fori(0, trips) as i:
                    for j in range(2):
                        quad(chunk, 2 * i + (Q0[ph] + k + j), j, i + (G0[ph] + k) // 2, x_)

            def transpose_tiles(src, n, before):
                for k in range(0, KT, 2):
                    if k % 8 == 0:
                        pe.wait_ge(s_xn, before + 2 * (k // 8) + 2)
                    if k >= 12:
                        pe.wait_ge(s_trl, (KT * n + k) // 2 - 5)
                    for u in range(2):
                        for t in range(TT):
                            e = T.transpose(bank(2 + (k // 2) % 6, u)[:, t * P:(t + 1) * P], src[:, t, (k + u) * P:(k + u + 1) * P], eye[:, :])
                    e.then_inc(s_tr, 1)

            for free in (m_o, a_s):
                pe.sem_inc(free, 1)
            pe.wait_ge(s_rows, 48)
            pe.wait_ge(s_eye, 16)
            T.transpose(ps[2][:, 0:48], work[0:48, 0:P], eye[0:48, 0:48]).then_inc(s_vt, 1)
            pe.wait_ge(s_ve, 1)
            transpose_tiles(X, 0, 0)
            quad(chunk_t, 0, 0, 0, H, tiles_ready=0)
            quad(chunk_t, 1, 1, 0, H)
            pe.wait_ge(s_rows2, 96)
            for k in range(4):
                T.transpose(ps[2][:, 88 * k:88 * (k + 1)], work[0:88, P * (1 + k):P * (2 + k)], eye[0:88, 0:88])
            for k in range(2):
                e = T.transpose(ps[3][:, 32 * k:32 * (k + 1)], work[0:CB, P * (5 + k):P * (6 + k)], eye[0:CB, 0:CB])
            e.then_inc(s_vt, 1)
            pe.wait_ge(s_wgl, 1)
            for k in range(KT):
                wh, wl = wgh[:, 24 * k:24 * k + P], wgl[:, 24 * k:24 * k + P]
                T.matmul(ps[7][:, 0:S], wh, h_hi[:, k, :], start=k == 0, stop=False)
                T.matmul(ps[7][:, 0:S], wh, h_lo[:, k, :], start=False, stop=False)
                e = T.matmul(ps[7][:, 0:S], wl, h_hi[:, k, :], start=False, stop=k == KT - 1)
            e.then_inc(s_gp, 1)
            pe.wait_ge(s_wide, 1)
            for h in range(HEADS):
                if h >= 3:
                    pe.wait_ge(s_rbc, h - 2)
                T.matmul(ps[4 + h % 3][:, 0:REL], work[0:BUCKETS + 1, 1536 + P * h:1536 + P * (h + 1)],
                         work[0:BUCKETS + 1, 1024:1024 + REL], start=True, stop=True).then_inc(s_vt, 1)
            pe.wait_ge(s_gt, 1)
            for t in range(TT):
                e = T.transpose(ps[7][:, 256 + 24 * t:256 + 24 * (t + 1)], work[0:24, W_SIG + P * t:W_SIG + P * (t + 1)], eye[0:24, 0:24])
            e.then_inc(s_gtt, 1)
            quad(chunk_t, 2, 0, 1, H)
            pe.wait_ge(s_sig, 1)
            pe.wait_ge(s_rbc, HEADS)
            transpose_tiles(M, 1, 4)
            quad(chunk_t, 3, 1, 1, H)
            pe.wait_ge(s_trl, KT)
            quads(chunk_t, "mk", 2, MM)
            quads(chunk_n, "mv", 2, MM)

            with pe.Fori(0, 2) as i:
                for j in range(2):
                    m, q = 2 * i + j, 2 * i + (Q0["nq"] + j)

                    def scores():
                        pe.wait_ge(m_st, 2 * m + 2)
                        if j == 0:
                            for b in range(2):
                                pe.wait_ge(evac[b], G0["nq"] // 2)
                        for t in range(TT):
                            for d in range(2):
                                e = T.matmul(bank(2, t), work[:, W_MS + S * d + P * t:W_MS + S * d + P * (t + 1)],
                                             arena[:, bass.ds(512 * m + (A_MK + S * d), S)], start=d == 0, stop=d == 1)
                        e.then_inc(m_s, 1)

                    def transposes():
                        pe.wait_ge(m_p, m + 1)
                        for u in range(TT):
                            for t in range(TT):
                                e = T.transpose(bank(4, u)[:, t * P:(t + 1) * P], work[:, W_MP + S * t + P * u:W_MP + S * t + P * (u + 1)], eye[:, :])
                        e.then_inc(m_t, 1)

                    def output():
                        pe.wait_ge(m_te, m + 1)
                        pe.wait_ge(m_l, m + 1)
                        for d in range(2):
                            for u in range(TT):
                                e = T.matmul(bank(6, d), work[:, W_MVS + S * u + P * d:W_MVS + S * u + P * (d + 1)],
                                             work[:, W_MPT + S * u:W_MPT + S * (u + 1)], start=u == 0, stop=u == 1)
                        e.then_inc(m_o, 1)

                    quad(chunk_t, q, j, i + G0["nq"] // 2, H, {-1: scores, 2: transposes, 3: output})
            for n in range(3):
                quad(chunk_t, Q0["kv0"] + n, n % 2, (G0["kv0"] + n) // 2, H)
            pe.wait_ge(s_bkl, 2)
            for n in range(2):
                g = G0["cmp"] + n
                bank_free(g % 2, g // 2)
                o = ps[g % 2][:, 0:S]
                for c in range(8):
                    pe.wait_ge(lo_done, 4 * (Q0["cmp"] + 2 * n) + c + 1)
                    for k in range(CK):
                        at = 1024 * n + 32 * (4 * c + k)
                        xh, xl = r_hi[:, at:at + P], r_lo[:, at:at + P]
                        T.matmul(o, xh, whi[:, c % 4, k, :], start=c == 0 and k == 0, stop=False)
                        T.matmul(o, xh, wlo[:, c % 4, k, :], start=False, stop=False)
                        e = T.matmul(o, xl, whi[:, c % 4, k, :], start=False, stop=c == 7 and k == CK - 1)
                    e.then_inc(pe_done, 1)
            for n in range(3):
                g = G0["kv1"] + n
                between = {}
                if n == 0:
                    def hidden():
                        for b in range(2):
                            pe.wait_ge(evac[b], G0["kv1"] // 2 + (b == 0))
                        for a in range(2):
                            for t in range(2):
                                e = T.transpose(ps[7][:, 32 * (2 * a + t):32 * (2 * a + t + 1)],
                                                work[0:2 * CS, W_HID + S * a + P * t:W_HID + S * a + P * (t + 1)], eye[0:32, 0:32])
                        e.then_inc(s_htt, 1)
                    between = {1: hidden}
                if n == 1:
                    def compressed():
                        pe.wait_ge(s_hcp, 1)
                        pe.wait_ge(s_pe2, 32)
                        for t in range(2):
                            T.matmul(ps[7][:, 8 * CS:10 * CS], w2[:, 0, t, :], hid[:, 0, t, :], start=t == 0, stop=t == 1)
                        for g2 in range(GROUPS):
                            for t in range(2):
                                e = T.matmul(ps[7][0:NC, 256 + DH * g2:256 + DH * (g2 + 1)], hid[:, 1, t, CS * g2:CS * g2 + NC],
                                             w2[:, 1, t, :], start=t == 0, stop=t == 1)
                        e.then_inc(s_kc, 1)
                    between = {0: compressed}
                quad(chunk_t if n == 1 else chunk_n, Q0["kv1"] + n, g % 2, g // 2, H, between)

            for g, ph in enumerate(("rqk", "rv")):
                with pe.Fori(0, 2) as i:
                    for j in range(2):
                        h, q = 2 * i + (HPG * g + j), 2 * i + (Q0[ph] + j)

                        def scores():
                            pe.wait_ge(a_st, h + 1)
                            if g == 0 and j == 0:
                                pe.wait_ge(s_kce, 1)
                                for b in range(2):
                                    pe.wait_ge(evac[b], G0["rqk"] // 2)
                            q0, q1 = work[:, W_QS:W_QS + P], work[:, W_QS + P:W_QS + S]
                            for n, k in enumerate((A_KS, A_KW)):
                                T.matmul(bank(2, n)[:, 0:P], q0, arena[:, k + S * g:k + S * g + P], start=True, stop=True)
                                T.matmul(bank(3, n), q1, arena[:, k + S * g:k + S * (g + 1)], start=True, stop=True)
                            T.matmul(ps[2][:, P:P + NC0], q0, kc[:, g, 0:NC0], start=True, stop=True)
                            T.matmul(ps[2][:, P + CS:P + CS + NC], q1, kc[:, g, 0:NC], start=True, stop=True).then_inc(a_s, 1)

                        def transposes():
                            pe.wait_ge(a_p, h + 1)
                            for n in range(2):
                                b = ps[4 + n]
                                T.transpose(b[:, 0:P], work[:, W_P + P * n:W_P + P * (n + 1)], eye[:, :])
                                for u in range(TT):
                                    o = W_P + S * (1 + n) + P * u
                                    T.transpose(b[:, P * (1 + u):P * (2 + u)], work[:, o:o + P], eye[:, :])
                            T.transpose(ps[4][0:NC0, 384:512], work[:, W_P + 768:W_P + 768 + NC0], eye[:, :])
                            T.transpose(ps[5][0:NC, 384:512], work[:, W_P + 768 + NC0:W_P + 768 + NC0 + NC], eye[:, :]).then_inc(a_t, 1)

                        def output():
                            pe.wait_ge(a_ta, h + 1)
                            pe.wait_ge(a_tv, h + 1)
                            pe.wait_ge(a_l, h + 1)
                            for n, v in enumerate((A_VS, A_VW)):
                                T.matmul(ps[6][:, 0:S], arena[:, v + DH * g:v + DH * (g + 1)], work[:, W_PT + 384 * n:W_PT + 384 * n + S],
                                         start=n == 0, stop=False, skip_group_check=True)
                                T.matmul(ps[6][:, P:S], arena[:, v + S + DH * g:v + S + DH * (g + 1)],
                                         work[:, W_PT + 384 * n + S:W_PT + 384 * (n + 1)], start=False, stop=False, skip_group_check=True)
                            T.matmul(ps[6][:, 0:P], vc[0:NC0, g, :], work[0:NC0, W_CT:W_CT + P], start=False, stop=False, skip_group_check=True)
                            T.matmul(ps[6][:, P:S], vc[:, g, :], work[0:NC, W_CT + P:W_CT + S], start=False, stop=True,
                                     skip_group_check=True).then_inc(a_o, 1)

                        quad((chunk_t, chunk_n)[g], q, j, i + G0[ph] // 2, H, {-1: scores, NSA_BEFORE[-1]: transposes, 3: output})
            quads(chunk_n, "rg", 2, H)

            pe.wait_ge(s_const, 16)
            with pe.Fori(0, 2) as i:
                for j in range(2):
                    r, q = 2 * i + j, 2 * i + (Q0["bg0"] + j)

                    def rotate():
                        for n, a in enumerate((A_RQ, A_RK)):
                            e = T.matmul(bank(2, n), rot[:, :], arena[:, bass.ds(S * r + a, S)], start=True, stop=True)
                        e.then_inc(r_r, 1)

                    def inner():
                        pe.wait_ge(r_q, r + 1)
                        k = W_QR + S
                        T.matmul(ps[3][:, 0:S], work[:, k:k + P], work[:, W_QR:W_QR + S], start=True, stop=True)
                        T.matmul(ps[3][:, S:S + P], work[:, k + P:k + S], work[:, W_QR + P:W_QR + S], start=True, stop=True).then_inc(r_i, 1)

                    def output():
                        pe.wait_ge(r_d, r + 1)
                        v = [arena[:, bass.ds(512 * r + (A_RV + S * u), S)] for u in range(TT)]
                        T.matmul(bank(4, 0), work[:, W_IN:W_IN + P], v[0], start=True, stop=True)
                        T.matmul(bank(4, 1), work[:, W_IN + P:W_IN + 2 * P], v[0], start=True, stop=False)
                        T.matmul(bank(4, 1), work[:, W_IN + 2 * P:W_IN + 3 * P], v[1], start=False, stop=True).then_inc(r_o, 1)

                    def transposes():
                        pe.wait_ge(r_y, r + 1)
                        pe.wait_ge(r_l, r + 1)
                        for u in range(2):
                            for t in range(TT):
                                e = T.transpose(bank(6, u)[:, t * P:(t + 1) * P], work[:, W_YB + S * t + P * u:W_YB + S * t + P * (u + 1)], eye[:, :])
                        e.then_inc(r_t, 1)

                    quad(chunk_t, q, j, i + G0["bg0"] // 2, H, {-1: rotate, 0: inner, 1: output, 3: transposes})
            for n, y in enumerate((YM, YA, YR)):
                if n == 0:
                    quads(chunk_t, "bg0", 2, H, 4)
                else:
                    quads(chunk_t, f"bg{n}", 4, H)
                if n == 2:
                    pe.wait_ge(r_l, RH + 1)
                with pe.Fori(0, 2) as i:
                    for j in range(2):
                        for c in range(4):
                            if c % 2 == 0:
                                bank_free(c // 2, 2 * i + (G0[f"br{n}"] // 2 + j))
                            chunk_t(2 * i + (Q0[f"br{n}"] + j), c, c // 2, *y, 4 * (c % 2), c % 2 == 0, c % 2 == 1)
            pe.wait_ge(s_mgl, KT // 2)
            quads(chunk_n, "wo", 4, MM)
            transpose_tiles(M, 2, 8)

            def up_quads(q, s):
                for n in range(4):
                    quad(chunk_t, q + n, n % 2, up_group(s) + n // 2, H,
                         tiles_ready=KT if isinstance(s, int) and n == 0 else None)

            def down(q, s):
                pe.wait_ge(s_al, s + 1)
                for g in range(8):
                    pe.wait_ge(s_dn, 8 * s + g + 1)
                    chunk_n(q + g // 4, g % 4, 2 + g % 4, *YR, 0, True, True)

            up_quads(Q0["up0"], 0)
            with pe.Fori(0, STEPS - 1) as i:
                q = 6 * i + Q0["ffn"]
                up_quads(q, i + 1)
                down(q + 4, i)
            down(Q0["dn"], STEPS - 1)


def constants():
    eye = np.eye(P, dtype=np.float32)
    rot = np.zeros((P, P), np.float32)
    for d in range(P // 2):
        rot[d + P // 2, d] = -1.0
        rot[d, d + P // 2] = 1.0
    onehot = np.zeros((BUCKETS + 1, REL), np.float32)
    for c in range(REL):
        rel = S - 1 - c
        if rel < 0:
            onehot[BUCKETS, c] = 1.0
            continue
        b = rel
        if rel >= BUCKETS // 2:
            b = BUCKETS // 2 + int(math.log(rel / (BUCKETS // 2)) / math.log(MAXD / (BUCKETS // 2)) * (BUCKETS - BUCKETS // 2))
        onehot[min(b, BUCKETS - 1), c] = 1.0
    theta = (np.float32(1.0) / np.power(np.float32(10000.0), np.linspace(0.0, 1.0, RDK // 2, dtype=np.float32))).astype(np.float32)
    ang = (theta[:, None] * np.arange(S, dtype=np.float32)[None, :]).astype(np.float32).astype(np.float64)
    cos, sin = np.tile(np.cos(ang), (2, 1)), np.tile(np.sin(ang), (2, 1))
    scale = RDK ** -0.5
    parts = [cos, cos * scale, sin, sin * scale]
    diff = np.arange(S)[None, :] - np.arange(P)[:, None]
    for hh in range(RH):
        parts.append(np.where(diff >= 0, (1.0 - 2.0 ** (-5.0 - hh)) ** np.maximum(diff, 0), 0.0))
    return {"c_eye": eye, "c_rot": rot, "c_onehot": onehot, "c_ret": np.concatenate(parts, 1).astype(np.float32)}


_INS = ["x", "mem", "w_in", "cmp_pe_k", "cmp_w1_k", "cmp_w2_k", "cmp_pe_v", "cmp_w1_v", "cmp_w2_v", "rel_bias",
        "w_mem_kv", "w_br_nsa", "w_br_ret", "w_br_mem", "w_o", "w_up", "conv_w", "conv_b", "w_down", "g_pre_mix",
        "g_post_mix", "g_mem", "g_pre_ffn", "g_post_ffn"]


def kernel(**inputs):
    import concourse.bacc as bacc
    from concourse.bass_utils import run_bass_kernel_spmd

    nc = bacc.Bacc("TRN2", target_bir_lowering=False, num_devices=1)
    arrays = {f"in_{n}": np.ascontiguousarray(inputs[n]) for n in _INS}
    arrays.update(constants())
    args = [nc.dram_tensor(n, a.shape, mybir.dt.from_np(a.dtype), kind="ExternalInput").ap() for n, a in arrays.items()]
    scratch = nc.dram_tensor("bias_rows", (HEADS, P, REL), F32).ap()
    out = nc.dram_tensor("out_y", (1, S, D), F32, kind="ExternalOutput").ap()
    build(nc, *args, scratch, out)
    r = run_bass_kernel_spmd(nc, [arrays], core_ids=[0])
    return r.results[0]["out_y"]
```

```python
import math
from contextlib import ExitStack

import numpy as np
import concourse.bass as bass
from concourse import mybir

F32 = mybir.dt.float32
F32R = mybir.dt.float32r
ACT = mybir.ActivationFunctionType
ALU = mybir.AluOpType
AX = mybir.AxisListType

P = 128
S = 256
D = 2048
KT = D // P
TT = S // P
GW = 256
CK = 4
EPS = 1e-6
HEADS, GROUPS, DH = 8, 2, 128
HPG = HEADS // GROUPS
CB, CS = 32, 16
NC = (S - CB) // CS + 1
NC0 = (P - CB) // CS + 1
RH, RDK = 4, 128
MH, MD = 4, 256
FF = 5632
BUCKETS, MAXD = 32, 128
MASKED = -1e30
REL = 384
STEPS = FF // 512

C_NQ = 0
C_KV = 1024
C_NG = C_KV + 1536
C_RQ = C_NG + 24
C_RK = C_RQ + 512
C_RV = C_RK + 512
C_RG = C_RV + 1024
C_MQ = C_RG + 1024
C_BG = C_MQ + 1024

PHASES = [("mq", 4, 4), ("mk", 4, 4), ("mv", 4, 4), ("nq", 4, 4), ("kv0", 3, 3), ("mix", 7, 3),
          ("rqk", 4, 4), ("rv", 4, 4), ("rg", 4, 4),
          ("bg0", 8, 8), ("br0", 4, 8), ("bg1", 8, 8), ("br1", 4, 8), ("bg2", 8, 8), ("br2", 4, 8),
          ("wo", 8, 8), ("up0", 4, 4), ("ffn", 6 * (STEPS - 1), 4 * (STEPS - 1)), ("dn", 2, 0)]
Q0, G0 = {}, {}
_q = _g = 0
for _n, _a, _b in PHASES:
    Q0[_n], G0[_n] = _q, _g
    _q, _g = _q + _a, _g + _b

MIX = [("cmp", 0), ("kv", 0), ("cmp", 1), ("kv", 1), ("cmp", 2), ("cmp", 3), ("kv", 2)]

A_X, A_M = 0, 4096
A_MQ, A_MK, A_MV = 0, 2048, 4096
A_NQ = 6144
A_KC, A_VC, A_KS, A_VS, A_KW, A_VW = (8192 + 512 * n for n in range(6))
A_RQ, A_RK, A_RSW, A_RV, A_RG = 0, 1024, 2048, 4096, 6144
A_MERGED, A_GATE = 0, 8192
NSA_P = [(768, NC0), (0, P), (P, P), (768 + NC0, NC), (2 * P, S), (2 * P + S, S)]
W_P, W_PT, W_CT, W_QS = 0, 792, 1560, 1816
W_MP, W_MPT, W_MS, W_MVS = 0, 512, 1024, 1536
W_QR, W_RT, W_IN, W_YB = 0, 512, 1024, 1408
W_RGT = 2048
W_RB = 1408
W_SIG, W_HID, W_HT = 0, 0, 1024
W_Y, W_PROD, W_TMP = 0, 1024, 0

NORM_PARTS = [(0, 0, 1024), (1, 0, 1024), (0, 1024, 1024), (1, 1024, 1024)]
OUT_PARTS = [(0, 0, 512), (0, 512, 1024), (1, 0, 1024), (1, 1024, 512), (0, 1536, 512), (1, 1536, 512)]
NSA_LINKS, RET_LINKS = 11, 6
NSA_BEFORE, NSA_AFTER = (0, 1, 2), (3,)


class Chain:

    def __init__(self, eng, sem):
        self.eng, self.sem, self.n, self.base = eng, sem, 0, 0

    def add(self, ins):
        ins.then_inc(self.sem, 1)
        self.n += 1

    def wait(self):
        self.eng.wait_ge(self.sem, self.base + self.n)

    def link(self, ins):
        self.add(ins)
        self.wait()

    def enter(self, i, per):
        self.start = self.n
        self.base, self.n = self.start + per * i, 0

    def leave(self, trips, per):
        assert self.n == per, (self.n, per)
        self.base, self.n = 0, self.start + trips * per


def build(nc, x, mem, w_in, cmp_pe_k, cmp_w1_k, cmp_w2_k, cmp_pe_v, cmp_w1_v, cmp_w2_v, rel_bias,
          w_mem_kv, w_br_nsa, w_br_ret, w_br_mem, w_o, w_up, conv_w, conv_b, w_down, g_pre_mix,
          g_post_mix, g_mem, g_pre_ffn, g_post_ffn, c_eye, c_stack, c_onehot, c_ret, scratch, out):
    ctx = ExitStack()
    with ctx:
        def sb(name, shape, dt=F32):
            return ctx.enter_context(nc.sbuf_tensor(name, shape, dt))

        def sem(name):
            return ctx.enter_context(nc.semaphore(name))

        h_hi, h_lo = (sb(n, [P, KT, S], F32R) for n in ("h_hi", "h_lo"))
        m_hi, m_lo = (sb(n, [P, KT, S], F32R) for n in ("m_hi", "m_lo"))
        r_hi, r_lo = (sb(n, [P, 8 * S + P], F32R) for n in ("r_hi", "r_lo"))
        wraw = sb("wraw", [P, 4, CK, GW])
        whi, wlo = (sb(n, [P, 4, CK, GW], F32R) for n in ("whi", "wlo"))
        arena = sb("arena", [P, 12288])
        tables = sb("tables", [P, 2048])
        work = sb("work", [P, 2560])
        eye = sb("eye", [P, P])
        stack = sb("stack", [64, 56])
        gain = sb("gain", [P, 3 * KT])
        conv = sb("conv", [P, 4, 88])
        wgr = sb("wgr", [P, KT, 24])
        wg = sb("wg", [P, 48 * KT + P - 48], F32R)
        sig = sb("sig", [P, TT, 24])
        kc = sb("kc", [P, GROUPS, CS])
        vc = sb("vc", [NC, GROUPS, DH])
        hid = sb("hid", [P, 2, 2, 2 * CS])
        w2 = sb("w2", [P, 2, 2, DH])
        peT = sb("peT", [P, 2, CB])
        st = sb("st", [P, 64])
        sq = sb("sq", [P, 2, TT, 8])

        ps = [ctx.enter_context(nc.psum_tensor(f"bank{i}", [P, 512], F32)) for i in range(8)]

        loaded = [sem(f"loaded{c}") for c in range(4)]
        hi_done, lo_done = sem("hi_done"), sem("lo_done")
        pe_done = sem("pe_done")
        evac = [sem(f"evac{b}") for b in range(2)]
        dch = sem("vector_chain")
        s_x = [sem(f"x_in{n}") for n in range(2 * TT)]
        s_m = [sem(f"mem_in{n}") for n in range(2 * TT)]
        s_eye, s_rows, s_rows2, s_wg = sem("eye_in"), sem("gain_rows_in"), sem("conv_rows_in"), sem("gate_columns_in")
        s_pe2, s_oh, s_tab, s_tab2 = sem("w2_in"), sem("onehot_in"), sem("bias_tables_in"), sem("retention_tables_in")
        s_gpost = sem("post_gain_in")
        s_half, s_neg, s_pad = sem("half_const"), sem("masked_row"), sem("pads_zero")
        s_ssq, s_sq, s_var, s_rstd, s_xn = sem("squares"), sem("group_squares"), sem("mean_square"), sem("rstd"), sem("normed")
        s_tr, s_trh, s_trl = sem("transposed"), sem("tile_hi"), sem("tile_lo")
        s_vt, s_ve, s_rbc, s_scr = sem("vectors_transposed"), sem("vectors_out"), sem("bias_row_out"), sem("bias_stored")
        s_wgh, s_wgl, s_gp, s_gc = sem("gate_columns_hi"), sem("gate_columns_lo"), sem("gate_product"), sem("gate_copied")
        s_gtt, s_gt, s_sig = sem("gate_by_token"), sem("gate_tanh"), sem("gate_sigmoid")
        s_bk, s_bkh, s_bkl = sem("blocks"), sem("blocks_hi"), sem("blocks_lo")
        s_cpo, s_htt, s_ht, s_hcp = sem("compression_copied"), sem("hidden_transposed"), sem("hidden_tanh"), sem("hidden_made")
        s_kc, s_kce = sem("compressed"), sem("compressed_out")
        m_qst, m_vst, m_s, m_nm, m_ex, m_p, m_t, m_te, m_o, m_h, m_l = (sem("mem_" + n) for n in (
            "queries_staged", "values_staged", "scores", "max", "exp", "probs", "transposed", "pt", "out", "hi", "lo"))
        a_st, a_s, a_nm, a_ex, a_p, a_t, a_ta, a_tv, a_o, a_h, a_l = (sem("nsa_" + n) for n in (
            "staged", "scores", "max", "exp", "probs", "transposed", "pt_win", "pt_sel", "out", "hi", "lo"))
        r_c, r_q, r_i, r_d, r_o, r_v, r_rs, r_y, r_t, r_h, r_l = (sem("ret_" + n) for n in (
            "products", "qk", "inner", "decayed", "out", "var", "rstd", "y", "transposed", "hi", "lo"))
        s_swap, s_rgt, s_stats = sem("halves_swapped"), sem("ret_gate_tanh"), sem("stats_made")
        s_mg, s_mgh, s_mgl = sem("merged"), sem("merged_hi"), sem("merged_lo")
        s_gsc, s_x2 = sem("post_gain_used"), sem("x2")
        s_y, s_gelu, s_prod, s_ah, s_al = sem("conv_tap2"), sem("gelu"), sem("prod"), sem("act_hi"), sem("act_lo")
        s_f0, s_dn = sem("f_zero"), sem("down_added")
        s_fin, s_out = sem("final"), sem("out_stored")

        block = ctx.enter_context(nc.Block())

        X = arena[:, A_X:A_X + 4096].rearrange("p (t n) -> p t n", t=TT)
        M = arena[:, A_M:A_M + 4096].rearrange("p (t n) -> p t n", t=TT)
        GP = tables[:, :]
        half = st[:, 60:61]

        def bank(g, t=None):
            b = ps[g][:, :].rearrange("p (t n) -> p t n", t=TT)
            return b if t is None else b[:, t, :]

        def blocks(n, u):
            return (r_hi, r_lo)[n][:, 0:2048].rearrange("p (j u g n) -> p j u g n", j=CB, u=2, g=GROUPS)[:, :, u, :, 0:NC]

        def gates(u):
            return wg[:, 0:48 * KT].rearrange("p (k u n) -> p k u n", u=2, n=24)[:, :, u, :]

        def wblocks(n):
            return work[:, 960 * n:960 * (n + 1)].rearrange("p (j g n) -> p j g n", j=CB, g=GROUPS)

        def up_group(s):
            return 2 * s + G0["up0"] // 2

        def piece(v, n):
            return v[:, n % 2, 1024 * (n // 2):1024 * (n // 2 + 1)]

        def rows(w, k0, col, n=GW, kt=CK):
            return w[0, k0 * P:(k0 + kt) * P, :].rearrange("(k p) n -> p k n", p=P)[:, :, bass.ds(col, n)]

        @block.sync
        def _(sp):
            def quad(q, src):
                for c in range(4):
                    if q:
                        sp.wait_ge(lo_done, 4 * (q - 1) + c + 1)
                    sp.dma_start(wraw[:, c], src(c)).then_inc(loaded[c], 16)

            def loop(q0, trips, per, sources):
                with sp.Fori(0, trips) as i:
                    free = [sp.snap(4 * per * i + (4 * (q0 - 1) + k + 1)) for k in range(4 * per)]
                    src = sources(i)
                    for j in range(per):
                        for c in range(4):
                            sp.wait_ge(lo_done, free[4 * j + c])
                            sp.dma_start(wraw[:, c], src[j](c)).then_inc(loaded[c], 16)

            def cols(w, base, count=2):
                def sources(i):
                    at = [sp.snap(count * GW * i + (base + GW * j)) for j in range(count)]
                    return [lambda c, o=o: rows(w, 4 * c, o) for o in at]
                return sources

            def quarters(dst, src, sems):
                for n in range(2 * TT):
                    sp.dma_start(piece(dst, n), src[0, (n % 2) * P:(n % 2 + 1) * P, 1024 * (n // 2):1024 * (n // 2 + 1)]).then_inc(sems[n], 16)

            quarters(X, x, s_x)
            sp.dma_start(eye[:, :], c_eye[:, :]).then_inc(s_eye, 16)
            for n, g in enumerate((g_pre_mix, g_mem, g_pre_ffn)):
                sp.dma_start(work[n * KT:(n + 1) * KT, 0:P], g.rearrange("o (k p) -> (o k) p", p=P)).then_inc(s_rows, 16)
            quad(0, lambda c: rows(w_in, 4 * c, C_MQ))
            quarters(M, mem, s_m)
            for k in range(3):
                sp.dma_start(work[0:88, P * (1 + k):P * (2 + k)],
                             conv_w[0, k:k + 1, :].rearrange("o (k p) -> (o k) p", p=P)).then_inc(s_rows2, 16)
            sp.dma_start(work[0:88, 4 * P:5 * P], conv_b.rearrange("o (k p) -> (o k) p", p=P)).then_inc(s_rows2, 16)
            sp.dma_start(work[0:CB, 5 * P:6 * P], cmp_pe_k[0]).then_inc(s_rows2, 16)
            sp.dma_start(work[0:CB, 6 * P:7 * P], cmp_pe_v[0]).then_inc(s_rows2, 16)
            sp.dma_start(stack[:, :], c_stack[:, :]).then_inc(s_oh, 16)
            sp.dma_start(work[0:BUCKETS, W_RB:W_RB + HEADS], rel_bias[:, :]).then_inc(s_oh, 16)
            sp.dma_start(work[0:BUCKETS + 1, 1024:1024 + REL], c_onehot[:, :]).then_inc(s_oh, 16)
            sp.dma_start(wgr[:, :, :], rows(w_in, 0, C_NG, 24, KT)).then_inc(s_wg, 16)
            sp.dma_start(w2[:, 0], cmp_w2_k[0].rearrange("(k p) n -> p k n", p=P)).then_inc(s_pe2, 16)
            sp.dma_start(w2[:, 1], cmp_w2_v[0].rearrange("(k p) n -> p k n", p=P)).then_inc(s_pe2, 16)
            quad(1, lambda c: rows(w_in, 4 * c, C_MQ + GW))
            quad(2, lambda c: rows(w_in, 4 * c, C_MQ + 2 * GW))
            sp.wait_ge(s_rbc, 1)
            sp.dma_start(scratch[:, :, :], arena[0:HEADS, A_GATE:A_GATE + REL].unsqueeze(1).to_broadcast([HEADS, P, REL])).then_inc(s_scr, 16)
            quad(3, lambda c: rows(w_in, 4 * c, C_MQ + 3 * GW))
            sp.wait_ge(s_scr, 16)
            sp.dma_start(tables[:, :].rearrange("p (h n) -> p h n", h=HEADS),
                         bass.AP(scratch.tensor, P - 1, [[REL - 1, P], [P * REL, HEADS], [1, S]])).then_inc(s_tab, 16)
            loop(Q0["mk"], 4, 2, cols(w_mem_kv[:, :, :], 0))
            loop(Q0["nq"], 2, 2, cols(w_in, C_NQ))
            for n in range(3):
                quad(Q0["kv0"] + n, lambda c: rows(w_in, 4 * c, C_KV + n * GW))
            for m, (kind, n) in enumerate(MIX):
                if kind == "cmp":
                    quad(Q0["mix"] + m, lambda c: rows((cmp_w1_k, cmp_w1_v)[n // 2], 16 * (n % 2) + 4 * c, 0))
                else:
                    quad(Q0["mix"] + m, lambda c: rows(w_in, 4 * c, C_KV + (3 + n) * GW))
            loop(Q0["rqk"], 4, 2, cols(w_in, C_RQ))
            for b in range(2):
                sp.wait_ge(evac[b], G0["rv"] // 2)
            for n in range(2):
                sp.dma_start(arena[P // 2 * n:P // 2 * (n + 1), A_RSW:A_RSW + 2048],
                             arena[P // 2 * (1 - n):P // 2 * (2 - n), A_RQ:A_RQ + 2048]).then_inc(s_swap, 16)
            loop(Q0["rg"], 2, 2, cols(w_in, C_RQ + 8 * GW))
            sp.wait_ge(a_nm, HEADS)
            sp.dma_start(tables[:, :], c_ret[:, :]).then_inc(s_tab2, 16)
            for n, (b, w) in enumerate(((2, w_br_mem), (0, w_br_nsa), (1, w_br_ret))):
                loop(Q0[f"bg{n}"], 4, 2, cols(w_in, C_BG + b * D))
                if n == 1:
                    sp.wait_ge(r_d, RH)
                    sp.dma_start(GP, g_post_mix.to_broadcast([P, D])).then_inc(s_gpost, 16)

                def pairs(i):
                    at = [sp.snap(4 * GW * i + GW * j) for j in range(4)]
                    return [lambda c, j=j: rows(w, 4 * (c % 2), at[2 * j + c // 2]) for j in range(2)]
                loop(Q0[f"br{n}"], 2, 2, pairs)
            for n in range(2):
                quad(Q0["wo"] + n, lambda c: rows(w_o, 4 * c, GW * n))
            sp.wait_ge(s_mgl, KT // 2)
            quarters(X, x, s_x)
            loop(Q0["wo"] + 2, 3, 2, cols(w_o, 2 * GW))

            def up_col(n):
                return (n // 2) * GW + (n % 2) * FF

            def down(r0):
                w = w_down[0, bass.ds(r0, 512), :].rearrange("(k p) n -> p k n", p=P)
                return [lambda c, j=j: w[:, :, (4 * j + c) * GW:(4 * j + c + 1) * GW] for j in range(2)]

            for n in range(4):
                quad(Q0["up0"] + n, lambda c: rows(w_up, 4 * c, up_col(n)))
                if n == 1:
                    sp.wait_ge(s_gsc, 1)
                    sp.dma_start(GP, g_post_ffn.to_broadcast([P, D])).then_inc(s_gpost, 16)

            def step(i):
                at = [sp.snap(512 * i + (512 + up_col(n))) for n in range(4)]
                return [lambda c, o=o: rows(w_up, 4 * c, o) for o in at] + down(sp.snap(512 * i))
            loop(Q0["ffn"], STEPS - 1, 6, step)
            for j in range(2):
                quad(Q0["dn"] + j, down((STEPS - 1) * 512)[j])
            for n, (t, at, width) in enumerate(OUT_PARTS):
                sp.wait_ge(s_fin, n + 1)
                sp.dma_start(out[0, t * P:(t + 1) * P, at:at + width], M[:, t, at:at + width]).then_inc(s_out, 16)
            sp.wait_ge(s_out, 16 * len(OUT_PARTS))

        @block.gpsimd
        def _(pool):
            nc.gpsimd.memset(half, -0.5).then_inc(s_half, 1)
            pool.wait_ge(s_half, 1)
            nc.gpsimd.memset(work[BUCKETS:BUCKETS + 1, W_RB:W_RB + HEADS], MASKED).then_inc(s_neg, 1)
            pool.wait_ge(s_neg, 1)
            for n, pad in enumerate((r_hi[:, 8 * S:], r_lo[:, 8 * S:], wg[:, 48 * KT:])):
                nc.gpsimd.memset(pad.bitcast(F32), 0.0).then_inc(s_pad, 1)
                pool.wait_ge(s_pad, n + 1)

            def rstd(n):
                pool.wait_ge(s_var, n + 1)
                nc.gpsimd.tensor_tensor(st[:, 4:6], st[:, 2:4], half.to_broadcast([P, 2]), ALU.pow).then_inc(s_rstd, 1)

            rstd(0)
            rstd(1)
            pool.wait_ge(s_scr, 16)
            for b in range(2):
                pool.wait_ge(evac[b], G0["mk"] // 2)
            nc.gpsimd.tensor_copy(work[:, W_MS:W_MS + 512], arena[:, A_MQ:A_MQ + 512]).then_inc(m_qst, 1)
            for b in range(2):
                pool.wait_ge(evac[b], G0["nq"] // 2)

            def values(m):
                pool.wait_ge(m_qst, m + 1)
                pool.wait_ge(m_o, m + 1)
                nc.gpsimd.tensor_copy(work[:, W_MVS:W_MVS + 512], arena[:, bass.ds(512 * m + A_MV, 512)]).then_inc(m_vst, 1)

            with pool.Fori(0, MH - 1) as m:
                values(m)
                pool.wait_ge(m_s, m + 1)
                pool.wait_ge(m_vst, m + 1)
                nc.gpsimd.tensor_copy(work[:, W_MS:W_MS + 512], arena[:, bass.ds(512 * m + (A_MQ + 512), 512)]).then_inc(m_qst, 1)
            values(MH - 1)
            pool.wait_ge(s_bkl, 2)
            with pool.Fori(0, HEADS) as h:
                pool.wait_ge(a_s, h + 1)
                nc.gpsimd.tensor_copy(work[:, W_QS:W_QS + S], arena[:, bass.ds(S * h + A_NQ, S)]).then_inc(a_st, 1)
            pool.wait_ge(s_tab2, 16)
            pool.wait_ge(a_o, HEADS)
            pool.wait_ge(s_swap, 32)

            def qk(src):
                return src.rearrange("p (a n) -> p a n", a=2)

            def rotate(r):
                qr, turned = work[:, W_QR:W_QR + 512], work[:, W_RT:W_RT + 512]
                nc.gpsimd.tensor_tensor(qk(qr), qk(arena[:, A_RQ:A_RQ + 2048])[:, :, bass.ds(S * r, S)], qk(tables[:, 0:512]),
                                        ALU.mult).then_inc(r_c, 1)
                nc.gpsimd.tensor_tensor(qk(turned), qk(arena[:, A_RSW:A_RSW + 2048])[:, :, bass.ds(S * r, S)], qk(tables[:, 512:1024]),
                                        ALU.mult).then_inc(r_c, 1)
                pool.wait_ge(r_c, 2 * r + 2)
                nc.gpsimd.tensor_tensor(qr, qr, turned, ALU.add).then_inc(r_q, 1)

            def head_rstd(r):
                pool.wait_ge(r_v, r + 1)
                nc.gpsimd.tensor_tensor(st[:, 44:46], st[:, 42:44], half.to_broadcast([P, 2]), ALU.pow).then_inc(r_rs, 1)

            rotate(0)
            with pool.Fori(0, RH - 1) as r:
                pool.wait_ge(r_q, r + 1)
                pool.wait_ge(r_i, r + 1)
                rotate(r + 1)
                head_rstd(r)
            head_rstd(RH - 1)
            rstd(2)
            rstd(3)
            pool.wait_ge(s_trl, 3 * KT // 2)
            nc.gpsimd.memset(arena[:, A_M:A_M + 4096], 0.0).then_inc(s_f0, 1)
            rstd(4)

        @block.scalar
        def _(act):
            def hi(q, c):
                act.wait_ge(loaded[c], 16 * q + 16)
                if not (isinstance(q, int) and q == 0):
                    act.wait_ge(pe_done, 4 * q + (c - 3))
                nc.scalar.activation(whi[:, c], wraw[:, c], ACT.Copy).then_inc(hi_done, 1)

            def ahead(q, chunks=range(4)):
                for c in chunks:
                    hi(q + 1, c)

            def plain(q0, trips):
                with act.Fori(0, trips) as i:
                    for j in range(2):
                        ahead(2 * i + (q0 + j))

            def squares(n, src, sems):
                if n >= 2:
                    act.wait_ge(s_var, n - 1)
                for k in range(2 * TT):
                    act.wait_ge(*sems(k))
                    nc.scalar.activation((r_hi, r_lo)[k % 2][:, 1024 * (k // 2):1024 * (k // 2 + 1)], piece(src, k), ACT.Square,
                                         accum_out=sq[:, n % 2, k % 2, k // 2:k // 2 + 1]).then_inc(s_ssq, 1)

            def tiles_hi(dst, n, pairs=range(0, KT, 2)):
                for k in pairs:
                    act.wait_ge(s_tr, (KT * n + k) // 2 + 1)
                    for u in range(2):
                        e = nc.scalar.activation(dst[:, k + u, :], bank(2 + (k // 2) % 6, u), ACT.Copy,
                                                 scale=gain[:, n * KT + k + u:n * KT + k + u + 1])
                    e.then_inc(s_trh, 1)

            squares(0, X, lambda k: (s_x[k], 16))
            hi(0, 0)
            act.wait_ge(s_ve, 1)
            for c in range(4):
                if c < 3:
                    hi(0, c + 1)
                tiles_hi(h_hi, 0, range(4 * c, 4 * c + 4, 2))
            ahead(0)
            act.wait_ge(s_wg, 16)
            act.wait_ge(s_pad, 3)
            nc.scalar.activation(gates(0), wgr[:, :, :], ACT.Copy).then_inc(s_wgh, 1)
            ahead(1)
            act.wait_ge(s_ssq, 4)
            squares(1, M, lambda k: (s_m[k], 16))
            ahead(2, (0, 1))
            act.wait_ge(s_gtt, 1)
            nc.scalar.activation(sig[:, :, :], ps[7][:, 256:304].rearrange("p (t n) -> p t n", t=TT), ACT.Tanh, scale=0.5).then_inc(s_gt, 1)
            ahead(2, (2, 3))
            tiles_hi(m_hi, 1)
            ahead(3)
            plain(Q0["mk"], 4)

            with act.Fori(0, 2) as i:
                for j in range(2):
                    m, q = 2 * i + j, 2 * i + (Q0["nq"] + j)
                    act.wait_ge(m_nm, m + 1)
                    for t in range(TT):
                        e = nc.scalar.activation(work[:, W_MP + S * t:W_MP + S * (t + 1)], bank(2, t), ACT.Exp,
                                                 bias=st[:, 32 + t:33 + t], accum_out=st[:, 34 + t:35 + t])
                    e.then_inc(m_ex, 1)
                    ahead(q)
                    act.wait_ge(m_o, m + 2)
                    nc.scalar.activation(m_hi[:, bass.ds(2 * m, 2), :], bank(6), ACT.Copy).then_inc(m_h, 1)
            ahead(Q0["kv0"])
            ahead(Q0["kv0"] + 1)
            for n in range(2):
                act.wait_ge(s_bk, n + 1)
                nc.scalar.activation(blocks(n, 0), wblocks(n), ACT.Copy).then_inc(s_bkh, 1)
            ahead(Q0["kv0"] + 2)
            for m, part in enumerate(MIX):
                q = Q0["mix"] + m
                ahead(q, (0,))
                if part == ("kv", 2):
                    act.wait_ge(s_htt, 1)
                    nc.scalar.activation(work[:, W_HT:W_HT + 8 * CS], ps[7][:, 0:8 * CS], ACT.Tanh, scale=0.5).then_inc(s_ht, 1)
                ahead(q, (1, 2, 3))

            for g, ph in enumerate(("rqk", "rv")):
                with act.Fori(0, 2) as i:
                    for j in range(2):
                        h, q = 2 * i + (HPG * g + j), 2 * i + (Q0[ph] + j)
                        act.wait_ge(a_nm, h + 1)
                        for n, (o, w) in enumerate(NSA_P):
                            e = nc.scalar.activation(work[:, W_P + o:W_P + o + w], work[:, W_P + o:W_P + o + w], ACT.Exp,
                                                     bias=st[:, n:n + 1], accum_out=st[:, 12 + n:13 + n])
                        e.then_inc(a_ex, 1)
                        ahead(q, NSA_BEFORE)
                        act.wait_ge(a_t, h + 1)
                        nc.scalar.activation(work[:, W_PT + 384:W_PT + 768], ps[5][:, 0:384], ACT.Copy)
                        nc.scalar.activation(work[0:NC, W_CT + P:W_CT + 2 * P], ps[5][0:NC, 384:512], ACT.Copy).then_inc(a_ta, 1)
                        ahead(q, NSA_AFTER)
                        act.wait_ge(a_o, h + 1)
                        nc.scalar.activation(m_hi[:, bass.ds(h + 8, 1), :], ps[6][:, 0:S].unsqueeze(1), ACT.Copy).then_inc(a_h, 1)
            with act.Fori(0, 2) as i:
                for j in range(2):
                    q = 2 * i + (Q0["rg"] + j)
                    ahead(q, (0, 1, 2))
                    act.wait_ge(pe_done, 4 * q + 4)
                    act.wait_ge(evac[1 - j], i + (G0["rg"] // 2 + j))
                    nc.scalar.activation(work[:, W_RGT:W_RGT + 512], ps[j][:, :], ACT.Tanh, scale=0.5).then_inc(s_rgt, 1)
                    ahead(q, (3,))

            for n in range(3):
                q0 = Q0[f"bg{n}"]
                for b in range(2):
                    act.wait_ge(evac[b], G0[f"bg{n}"] // 2)
                if n == 0:
                    with act.Fori(0, 2) as i:
                        for j in range(2):
                            r, q = 2 * i + j, 2 * i + (q0 + j)
                            ahead(q)
                            act.wait_ge(r_t, r + 1)
                            nc.scalar.activation(r_hi[:, bass.ds(512 * r, 512)], ps[6][:, :], ACT.Copy).then_inc(r_h, 1)
                            nc.scalar.activation(arena[:, bass.ds(1024 * i + (A_GATE + 512 * j), 512)], ps[j][:, :],
                                                 ACT.Tanh, scale=0.5).then_inc(evac[j], 1)
                with act.Fori(0, 2 if n == 0 else 4) as i:
                    for j in range(2):
                        k = 8 - (4 if n == 0 else 8) + j
                        ahead(2 * i + (q0 + k))
                        nc.scalar.activation(arena[:, bass.ds(1024 * i + (A_GATE + 512 * k), 512)], ps[j][:, :],
                                             ACT.Tanh, scale=0.5).then_inc(evac[j], 1)
                if n < 2:
                    plain(Q0[f"br{n}"], 2)
            with act.Fori(0, 2) as i:
                for j in range(2):
                    for b in range(2):
                        ahead(2 * i + (Q0["br2"] + j), (2 * b, 2 * b + 1))
                        k = 4 * i + (2 * j + b)
                        act.wait_ge(s_mg, k + 1)
                        nc.scalar.activation(m_hi[:, bass.ds(2 * k, 2), :].rearrange("p k s -> p (k s)"),
                                             arena[:, bass.ds(512 * k + A_MERGED, 512)], ACT.Copy, scale=0.5).then_inc(s_mgh, 1)
            act.wait_ge(s_var, 1)
            with act.Fori(0, 4) as i:
                for j in range(2):
                    q = 2 * i + (Q0["wo"] + j)
                    ahead(q, (0, 1, 2))
                    act.wait_ge(pe_done, 4 * q + 4)
                    for t in range(TT):
                        e = nc.scalar.activation(work[:, 512 * j + S * t:512 * j + S * (t + 1)], bank(j, t), ACT.Square,
                                                 accum_out=sq[:, 0, t, bass.ds(2 * i + j, 1)])
                    e.then_inc(s_sq, 1)
                    ahead(q, (3,))
            squares(3, X, lambda k: (s_x2, k + 1))
            tiles_hi(h_hi, 2)

            def up_quads(q, s):
                for n in range(4):
                    a, j = n // 2, n % 2
                    ahead(q + n)
                    if not (isinstance(s, int) and a == 0):
                        act.wait_ge(s_prod, 2 * s + a)
                    for t in range(2):
                        col = 4 * s + (44 * j + 2 * a + t)
                        e = nc.scalar.activation(work[:, W_Y + 512 * j + S * t:W_Y + 512 * j + S * (t + 1)], bank(j, t),
                                                 ACT.Identity, bias=conv[:, 3, bass.ds(col, 1)], scale=conv[:, 2, bass.ds(col, 1)])
                    e.then_inc(s_y, 1)
                    if j:
                        act.wait_ge(evac[0], up_group(s) + a + 1)
                        nc.scalar.activation(work[:, W_Y:W_Y + 512], work[:, W_Y:W_Y + 512], ACT.Gelu_apprx_tanh).then_inc(s_gelu, 1)

            def split_hi(s, u):
                act.wait_ge(s_prod, 2 * s + 2)
                nc.scalar.activation(r_hi[:, 1024 * u:1024 * (u + 1)], work[:, W_PROD:W_PROD + 1024], ACT.Copy).then_inc(s_ah, 1)

            up_quads(Q0["up0"], 0)
            split_hi(0, 0)
            with act.Fori(0, (STEPS - 1) // 2) as i:
                for u in range(2):
                    q = 12 * i + (Q0["ffn"] + 6 * u)
                    up_quads(q, 2 * i + (u + 1))
                    ahead(q + 4)
                    split_hi(2 * i + (u + 1), 1 - u)
                    ahead(q + 5)
            ahead(Q0["dn"], (0,))
            for g in range(8):
                if g < 3:
                    ahead(Q0["dn"], (g + 1,))
                act.wait_ge(s_dn, 4 + 8 * (STEPS - 1) + g + 1)
                for t in range(TT):
                    e = nc.scalar.activation(h_hi[:, 2 * g + t, :], M[:, t, GW * g:GW * (g + 1)], ACT.Square,
                                             accum_out=sq[:, 0, t, g:g + 1])
                e.then_inc(s_sq, 1)

        @block.vector
        def _(dve):
            V = nc.vector
            ch = Chain(dve, dch)
            for free in (m_l, a_l, r_l):
                dve.sem_inc(free, 1)
            dve.sem_inc(s_dn, 4)

            def lo(q, c):
                dve.wait_ge(hi_done, 4 * q + (c + 1))
                V.tensor_tensor(wlo[:, c], wraw[:, c], whi[:, c].bitcast(F32), ALU.subtract).then_inc(lo_done, 1)

            def ahead(q, chunks=range(4)):
                for c in chunks:
                    lo(q + 1, c)

            def store(q, b, dst, scale=None, chunks=(0, 1, 2)):
                ahead(q, chunks)
                dve.wait_ge(pe_done, 4 * q + 4)
                if scale is None:
                    V.tensor_copy(dst, ps[b][:, :]).then_inc(evac[b], 1)
                else:
                    V.tensor_scalar(dst, ps[b][:, :], scale, None, ALU.mult).then_inc(evac[b], 1)
                ahead(q, (3,))

            def stores(q0, trips, base, scale=None):
                with dve.Fori(0, trips) as i:
                    for j in range(2):
                        store(2 * i + (q0 + j), j, arena[:, bass.ds(1024 * i + (base + 512 * j), 512)], scale)

            def mean_square(n, parts, ready, meanwhile=None):
                dve.wait_ge(*ready)
                ch.link(V.tensor_reduce(st[:, 0:2], sq[:, n % 2, :, 0:parts], AX.X, ALU.add))
                V.tensor_scalar(st[:, 2:4], st[:, 0:2], 1.0 / D, EPS, ALU.mult, ALU.add).then_inc(s_var, 1)
                if meanwhile:
                    meanwhile()
                dve.wait_ge(s_rstd, n + 1)

            def normed(dst, src):
                for t, at, width in NORM_PARTS:
                    V.tensor_scalar(dst[:, t, at:at + width], src[:, t, at:at + width], st[:, 4 + t:5 + t], None,
                                    ALU.mult).then_inc(s_xn, 1)

            def tiles_lo(dst_hi, dst, n, pairs=range(0, KT, 2)):
                for k in pairs:
                    dve.wait_ge(s_trh, (KT * n + k) // 2 + 1)
                    for u in range(2):
                        e = V.scalar_tensor_tensor(dst[:, k + u, :], bank(2 + (k // 2) % 6, u), gain[:, n * KT + k + u:n * KT + k + u + 1],
                                                   dst_hi[:, k + u, :].bitcast(F32), ALU.mult, ALU.subtract)
                    e.then_inc(s_trl, 1)

            dve.wait_ge(s_vt, 1)
            V.tensor_copy(gain[:, :], ps[2][:, 0:48]).then_inc(s_ve, 1)
            mean_square(0, 2, (s_ssq, 4))
            normed(X, X)
            dve.wait_ge(s_ve, 1)
            for c in range(4):
                lo(0, c)
                tiles_lo(h_hi, h_lo, 0, range(4 * c, 4 * c + 4, 2))
            store(0, 0, arena[:, A_MQ:A_MQ + 512], 1.0 / math.sqrt(MD))
            dve.wait_ge(s_wgh, 1)
            V.tensor_tensor(gates(1), wgr[:, :, :], gates(0).bitcast(F32), ALU.subtract).then_inc(s_wgl, 1)
            store(1, 1, arena[:, A_MQ + 512:A_MQ + 1024], 1.0 / math.sqrt(MD))
            dve.wait_ge(s_vt, 2)
            V.tensor_copy(conv[:, :, :].rearrange("p a n -> p (a n)"), ps[2][:, 0:352])
            V.tensor_copy(peT[:, :, :].rearrange("p a n -> p (a n)"), ps[3][:, 0:64]).then_inc(s_ve, 1)
            dve.wait_ge(s_vt, 3)
            V.tensor_copy(arena[0:HEADS, A_GATE:A_GATE + REL], ps[4][0:HEADS, 0:REL]).then_inc(s_rbc, 1)
            dve.wait_ge(s_gp, 1)
            V.tensor_copy(work[0:48, W_SIG:W_SIG + S], ps[7][0:48, 0:S]).then_inc(s_gc, 1)
            mean_square(1, 2, (s_ssq, 8))
            normed(M, M)
            ahead(2, (0, 1))
            dve.wait_ge(s_gt, 1)
            V.tensor_scalar(sig[:, :, :], sig[:, :, :], 0.5, 0.5, ALU.mult, ALU.add).then_inc(s_sig, 1)
            store(2, 0, arena[:, A_MQ + 1024:A_MQ + 1536], 1.0 / math.sqrt(MD), (2,))
            tiles_lo(m_hi, m_lo, 1)
            store(3, 1, arena[:, A_MQ + 1536:A_MQ + 2048], 1.0 / math.sqrt(MD))
            stores(Q0["mk"], 4, A_MK)

            with dve.Fori(0, 2) as i:
                ch.enter(i, 2)
                for j in range(2):
                    m, q = 2 * i + j, 2 * i + (Q0["nq"] + j)
                    dve.wait_ge(m_s, m + 1)
                    V.tensor_reduce(st[:, 32:34], bank(2), AX.X, ALU.max, negate=True).then_inc(m_nm, 1)
                    ahead(q, (0,))
                    dve.wait_ge(m_ex, m + 1)
                    ch.link(V.reciprocal(st[:, 36:38], st[:, 34:36]))
                    for t in range(TT):
                        e = V.tensor_scalar(work[:, W_MP + S * t:W_MP + S * (t + 1)], work[:, W_MP + S * t:W_MP + S * (t + 1)],
                                            st[:, 36 + t:37 + t], None, ALU.mult)
                    e.then_inc(m_p, 1)
                    ahead(q, (1, 2))
                    dve.wait_ge(m_t, m + 1)
                    V.tensor_copy(work[:, W_MPT:W_MPT + 512], ps[4][:, :]).then_inc(m_te, 1)
                    store(q, j, arena[:, bass.ds(1024 * i + (A_NQ + 512 * j), 512)], DH ** -0.5, ())
                    dve.wait_ge(m_h, m + 1)
                    V.tensor_tensor(m_lo[:, bass.ds(2 * m, 2), :], bank(6), m_hi[:, bass.ds(2 * m, 2), :].bitcast(F32),
                                    ALU.subtract).then_inc(m_l, 1)
                ch.leave(2, 2)
            for n, dst in enumerate((A_KC, A_VC)):
                store(Q0["kv0"] + n, n, arena[:, dst:dst + 512])
            dve.wait_ge(evac[0], G0["kv0"] // 2 + 1)
            dve.wait_ge(evac[1], G0["kv0"] // 2 + 1)
            dve.wait_ge(s_ve, 2)
            for n, src in enumerate((A_KC, A_VC)):
                base = arena[:, src:src + 512]
                for g in range(GROUPS):
                    e = V.tensor_tensor(work[:, 960 * n:960 * (n + 1)].rearrange("p (j g n) -> p j g n", j=CB, g=GROUPS)[:, :, g, :],
                                        bass.AP(base.tensor, base.offset + S * g, [base.ap[0], [1, CB], [CS, NC]]),
                                        peT[:, n, :].unsqueeze(2).to_broadcast([P, CB, NC]), ALU.add)
                e.then_inc(s_bk, 1)
            for n in range(2):
                dve.wait_ge(s_bkh, n + 1)
                V.tensor_tensor(blocks(n, 1), wblocks(n), blocks(n, 0).bitcast(F32), ALU.subtract).then_inc(s_bkl, 1)
            store(Q0["kv0"] + 2, 0, arena[:, A_KS:A_KS + 512])
            for m, (kind, n) in enumerate(MIX):
                q, b = Q0["mix"] + m, (G0["mix"] + n) % 2
                if kind == "kv" and n < 2:
                    store(q, b, arena[:, (A_VS, A_KW)[n]:(A_VS, A_KW)[n] + 512])
                elif kind == "kv":
                    ahead(q, (0,))
                    dve.wait_ge(s_ht, 1)
                    V.scalar_tensor_tensor(hid[:, :, :, :].rearrange("p a t n -> p (a t n)"), work[:, W_HT:W_HT + 8 * CS], 1.0,
                                           ps[7][:, 0:8 * CS], ALU.add, ALU.mult).then_inc(s_hcp, 1)
                    ahead(q, (1, 2))
                    dve.wait_ge(s_kc, 1)
                    V.tensor_scalar(kc[:, :, :], ps[7][:, 8 * CS:10 * CS].rearrange("p (g n) -> p g n", g=GROUPS), 0.5, None, ALU.mult)
                    V.tensor_scalar(vc[:, :, :], ps[7][0:NC, 256:512].rearrange("p (g n) -> p g n", g=GROUPS), 0.5, None,
                                    ALU.mult).then_inc(s_kce, 1)
                    store(q, b, arena[:, A_VW:A_VW + 512], chunks=())
                elif n % 2 == 0:
                    ahead(q)
                else:
                    ahead(q, (0, 1, 2))
                    dve.wait_ge(pe_done, 4 * q + 4)
                    V.tensor_copy(work[0:4 * CS, W_HID + S * (n // 2):W_HID + S * (n // 2 + 1)], ps[2 + n // 2][0:4 * CS, 0:S]).then_inc(s_cpo, 1)
                    ahead(q, (3,))

            dve.wait_ge(s_tab, 16)
            dve.wait_ge(s_sig, 1)
            for g, (ph, base) in enumerate((("rqk", A_RQ), ("rv", A_RV))):
                with dve.Fori(0, 2) as i:
                    ch.enter(i, NSA_LINKS * 2)
                    for j in range(2):
                        h, q = 2 * i + (HPG * g + j), 2 * i + (Q0[ph] + j)
                        dve.wait_ge(a_s, h + 2)

                        def bias(lo_, n, step=1):
                            return tables[:, bass.ds(S * h + lo_, n, step)]
                        p0, p1 = work[:, W_P:W_P + 256].rearrange("p (b n) -> p b n", b=2), work[:, W_P + 256:W_P + 768].rearrange("p (b n) -> p b n", b=2)
                        c0, c1 = work[:, W_P + 768:W_P + 768 + NC0], work[:, W_P + 768 + NC0:W_P + 768 + NC0 + NC]
                        ch.add(V.tensor_tensor(p0, bank(2)[:, :, 0:P], bias(P, P).unsqueeze(1).to_broadcast([P, 2, P]), ALU.add))
                        ch.add(V.tensor_tensor(p1, bank(3), bias(0, S).unsqueeze(1).to_broadcast([P, 2, S]), ALU.add))
                        ch.add(V.tensor_tensor(c0, ps[2][:, P:P + NC0], bias(P + CB - 1, NC0, CS), ALU.add))
                        ch.link(V.tensor_tensor(c1, ps[2][:, P + CS:P + CS + NC], bias(CB - 1, NC, CS), ALU.add))
                        ch.add(V.tensor_reduce(st[:, 7:9], p0, AX.X, ALU.max))
                        ch.add(V.tensor_reduce(st[:, 10:12], p1, AX.X, ALU.max))
                        ch.add(V.tensor_reduce(st[:, 6:7], c0, AX.X, ALU.max))
                        ch.link(V.tensor_reduce(st[:, 9:10], c1, AX.X, ALU.max))
                        V.tensor_scalar(st[:, 0:6], st[:, 6:12], MASKED / 10, -1.0, ALU.max, ALU.mult).then_inc(a_nm, 1)
                        dve.wait_ge(a_ex, h + 1)
                        ch.link(V.tensor_scalar(st[:, 12:18], st[:, 12:18], 1e-30, None, ALU.max))
                        ch.link(V.reciprocal(st[:, 18:24], st[:, 12:18]))
                        ch.link(V.tensor_tensor(st[:, 18:24].rearrange("p (t b) -> p t b", t=TT), st[:, 18:24].rearrange("p (t b) -> p t b", t=TT),
                                                sig[:, :, :].rearrange("p t (b h) -> p t b h", b=3)[:, :, :, bass.ds(h, 1)].squeeze(), ALU.mult))
                        for n, (o, w) in enumerate(NSA_P):
                            e = V.tensor_scalar(work[:, W_P + o:W_P + o + w], work[:, W_P + o:W_P + o + w],
                                                st[:, 18 + n:19 + n], None, ALU.mult)
                        e.then_inc(a_p, 1)
                        ahead(q, NSA_BEFORE)
                        dve.wait_ge(a_t, h + 1)
                        V.tensor_copy(work[:, W_PT:W_PT + 384], ps[4][:, 0:384])
                        V.tensor_copy(work[0:NC0, W_CT:W_CT + P], ps[4][0:NC0, 384:512]).then_inc(a_tv, 1)
                        store(q, j, arena[:, bass.ds(1024 * i + (base + 512 * j), 512)], chunks=())
                        dve.wait_ge(a_h, h + 1)
                        V.tensor_tensor(m_lo[:, bass.ds(h + 8, 1), :], ps[6][:, 0:S].unsqueeze(1), m_hi[:, bass.ds(h + 8, 1), :].bitcast(F32),
                                        ALU.subtract).then_inc(a_l, 1)
                    ch.leave(2, NSA_LINKS * 2)
            with dve.Fori(0, 2) as i:
                for j in range(2):
                    q = 2 * i + (Q0["rg"] + j)
                    ahead(q, (0, 1, 2))
                    dve.wait_ge(s_rgt, 2 * i + (j + 1))
                    V.scalar_tensor_tensor(arena[:, bass.ds(1024 * i + (A_RG + 512 * j), 512)], work[:, W_RGT:W_RGT + 512], 1.0,
                                           ps[j][:, :], ALU.add, ALU.mult).then_inc(evac[j], 1)
                    ahead(q, (3,))

            dve.wait_ge(s_tab2, 16)
            for b in range(2):
                dve.wait_ge(evac[b], G0["bg0"] // 2)
            with dve.Fori(0, 2) as i:
                ch.enter(i, RET_LINKS * 2)
                for j in range(2):
                    r, q = 2 * i + j, 2 * i + (Q0["bg0"] + j)
                    ahead(q, (0,))
                    dve.wait_ge(r_i, r + 1)
                    V.tensor_tensor(work[:, W_IN:W_IN + S], ps[3][:, 0:S], tables[:, bass.ds(S * r + 1024, S)], ALU.mult)
                    V.tensor_tensor(work[:, W_IN + S:W_IN + S + P], ps[3][:, S:S + P], tables[:, bass.ds(S * r + 1024, P)],
                                    ALU.mult).then_inc(r_d, 1)
                    ahead(q, (1,))
                    dve.wait_ge(r_o, r + 1)
                    for t in range(TT):
                        ch.add(V.bn_stats(st[:, 46 + 6 * t:52 + 6 * t], bank(4, t)))
                    ch.wait()
                    dve.sem_inc(s_stats, 1)
                    for t in range(TT):
                        ch.add(V.bn_aggr(st[:, 24 + 2 * t:26 + 2 * t], st[:, 46 + 6 * t:52 + 6 * t]))
                    ch.wait()
                    V.tensor_scalar(st[:, 42:44], st[:, 24:28].rearrange("p (t a) -> p a t", t=TT)[:, 1, :], EPS, None, ALU.add).then_inc(r_v, 1)
                    dve.wait_ge(r_rs, r + 1)
                    for t in range(TT):
                        ch.add(V.tensor_scalar(work[:, W_YB + S * t:W_YB + S * (t + 1)], bank(4, t), st[:, 24 + 2 * t:25 + 2 * t],
                                               st[:, 44 + t:45 + t], ALU.subtract, ALU.mult))
                    ch.wait()
                    V.scalar_tensor_tensor(work[:, W_YB:W_YB + 512], work[:, W_YB:W_YB + 512], 0.5,
                                           arena[:, bass.ds(512 * r + A_RG, 512)], ALU.mult, ALU.mult).then_inc(r_y, 1)
                    ahead(q, (2, 3))
                    dve.wait_ge(r_h, r + 1)
                    V.tensor_tensor(r_lo[:, bass.ds(512 * r, 512)], ps[6][:, :], r_hi[:, bass.ds(512 * r, 512)].bitcast(F32),
                                    ALU.subtract).then_inc(r_l, 1)
                ch.leave(2, RET_LINKS * 2)

            for n in range(3):
                q0 = Q0[f"bg{n}"] + (4 if n == 0 else 0)
                with dve.Fori(0, 2 if n == 0 else 4) as i:
                    for j in range(2):
                        ahead(2 * i + (q0 + j))
                for b in range(2):
                    dve.wait_ge(evac[b], G0[f"br{n}"] // 2)
                with dve.Fori(0, 2) as i:
                    ch.enter(i, (0, 8, 4)[n])
                    for j in range(2):
                        for b in range(2):
                            q, k = 2 * i + (Q0[f"br{n}"] + j), 4 * i + (2 * j + b)
                            gate, sum_ = arena[:, bass.ds(512 * k + A_GATE, 512)], arena[:, bass.ds(512 * k + A_MERGED, 512)]
                            if n == 0:
                                ahead(q, (2 * b, 2 * b + 1))
                                dve.wait_ge(pe_done, 4 * q + (2 * b + 2))
                                V.scalar_tensor_tensor(sum_, gate, 1.0, ps[b][:, :], ALU.add, ALU.mult).then_inc(evac[b], 1)
                                continue
                            tmp = work[:, W_TMP + 512 * b:W_TMP + 512 * (b + 1)]
                            dve.wait_ge(pe_done, 4 * q + (2 * b + 2))
                            ch.link(V.scalar_tensor_tensor(tmp, gate, 1.0, ps[b][:, :], ALU.add, ALU.mult))
                            dve.sem_inc(evac[b], 1)
                            e = V.tensor_tensor(sum_, sum_, tmp, ALU.add)
                            if n == 1:
                                ch.add(e)
                                ahead(q, (2 * b, 2 * b + 1))
                                continue
                            e.then_inc(s_mg, 1)
                            ahead(q, (2 * b, 2 * b + 1))
                            dve.wait_ge(s_mgh, k + 1)
                            V.scalar_tensor_tensor(m_lo[:, bass.ds(2 * k, 2), :].rearrange("p k s -> p (k s)"), sum_, 0.5,
                                                   m_hi[:, bass.ds(2 * k, 2), :].rearrange("p k s -> p (k s)").bitcast(F32),
                                                   ALU.mult, ALU.subtract).then_inc(s_mgl, 1)
                    ch.leave(2, (0, 8, 4)[n])
            dve.wait_ge(s_gpost, 16)

            def wo_group(i, j):
                q = 2 * i + (Q0["wo"] + j)
                ahead(q, (0, 1, 2))
                dve.wait_ge(s_sq, 2 * i + (j + 1))
                V.tensor_tensor(M[:, :, bass.ds(512 * i + GW * j, GW)], bank(j),
                                GP[:, bass.ds(512 * i + GW * j, GW)].unsqueeze(1).to_broadcast([P, TT, GW]), ALU.mult).then_inc(evac[j], 1)
                return q

            with dve.Fori(0, 3) as i:
                for j in range(2):
                    ahead(wo_group(i, j), (3,))
            ahead(wo_group(3, 0), (3,))
            last = wo_group(3, 1)
            mean_square(2, 8, (s_sq, 8))
            dve.wait_ge(evac[0], G0["up0"] // 2)
            dve.wait_ge(evac[1], G0["up0"] // 2)
            dve.sem_inc(s_gsc, 1)

            def post(dst, t, at, width, done):
                own = slice(at, at + width)
                V.scalar_tensor_tensor(dst[:, t, own], M[:, t, own], st[:, 4 + t:5 + t], X[:, t, own], ALU.mult, ALU.add).then_inc(done, 1)

            for k in range(2 * TT):
                dve.wait_ge(s_x[k], 32)
                post(X, k % 2, 1024 * (k // 2), 1024, s_x2)
            ahead(last, (3,))
            mean_square(3, 2, (s_ssq, 12))
            normed(M, X)
            tiles_lo(h_hi, h_lo, 2)

            def up_quads(q, s):
                for n in range(4):
                    a, j = n // 2, n % 2
                    ahead(q + n)
                    dve.wait_ge(s_y, 4 * s + (n + 1))
                    for tap in (1, 0):
                        for t in range(2):
                            d = 2 - tap
                            y = work[:, W_Y + 512 * j + S * t + d:W_Y + 512 * j + S * (t + 1)]
                            e = V.scalar_tensor_tensor(y, bank(j, t)[:, 0:S - d], conv[:, tap, bass.ds(4 * s + (44 * j + 2 * a + t), 1)], y,
                                                       ALU.mult, ALU.add)
                            if tap:
                                ch.add(e)
                        if tap:
                            ch.wait()
                    e.then_inc(evac[j], 1)
                    if j:
                        dve.wait_ge(s_gelu, 2 * s + (a + 1))
                        dve.wait_ge(evac[1], up_group(s) + a + 1)
                        if not isinstance(s, int):
                            dve.wait_ge(s_ah, s)
                        V.tensor_tensor(work[:, W_PROD + 512 * a:W_PROD + 512 * (a + 1)], work[:, W_Y:W_Y + 512],
                                        work[:, W_Y + 512:W_Y + 1024], ALU.mult).then_inc(s_prod, 1)

            def split_lo(s, u):
                dve.wait_ge(s_ah, s + 1)
                V.tensor_tensor(r_lo[:, 1024 * u:1024 * (u + 1)], work[:, W_PROD:W_PROD + 1024],
                                r_hi[:, 1024 * u:1024 * (u + 1)].bitcast(F32), ALU.subtract).then_inc(s_al, 1)

            def down_group(q, g):
                dve.wait_ge(pe_done, 4 * q + (g + 1))
                f = M[:, :, GW * g:GW * (g + 1)]
                return V.tensor_tensor(f, bank(2 + g % 4), f, ALU.add)

            up_quads(Q0["up0"], 0)
            split_lo(0, 0)
            dve.wait_ge(s_f0, 1)
            with dve.Fori(0, (STEPS - 1) // 2) as i:
                ch.enter(i, 16)
                for u in range(2):
                    q = 12 * i + (Q0["ffn"] + 6 * u)
                    up_quads(q, 2 * i + (u + 1))
                    for g in range(8):
                        ahead(q + 4 + g // 4, (g % 4,))
                        down_group(q + 4, g).then_inc(s_dn, 1)
                        if g == 3:
                            split_lo(2 * i + (u + 1), 1 - u)
                ch.leave((STEPS - 1) // 2, 16)
            dve.wait_ge(s_gpost, 32)

            def times_gain(g):
                dve.wait_ge(s_sq, 8 + g + 1)
                f = M[:, :, GW * g:GW * (g + 1)]
                ch.add(V.tensor_tensor(f, f, GP[:, GW * g:GW * (g + 1)].unsqueeze(1).to_broadcast([P, TT, GW]), ALU.mult))

            for g in range(8):
                if g < 4:
                    ahead(Q0["dn"], (g,))
                down_group(Q0["dn"], g).then_inc(s_dn, 1)
                if g:
                    times_gain(g - 1)
            mean_square(4, 8, (s_sq, 16), lambda: times_gain(7))
            ch.wait()
            for part in OUT_PARTS:
                post(M, *part, s_fin)

        @block.tensor
        def _(pe):
            T = nc.tensor

            def chunk_t(q, c, b, hi_, lo_, k0, first, last):
                pe.wait_ge(lo_done, 4 * q + (c + 1))
                for k in range(CK):
                    for t in range(2):
                        wh, wl = whi[:, c, k, t * P:(t + 1) * P], wlo[:, c, k, t * P:(t + 1) * P]
                        xh, xl = hi_(k0 + k), lo_(k0 + k)
                        o = bank(b, t)
                        T.matmul(o, wh, xh, start=first and k == 0 and t == 0, stop=False, skip_group_check=True)
                        T.matmul(o, wh, xl, start=False, stop=False, skip_group_check=True)
                        e = T.matmul(o, wl, xh, start=False, stop=last and k == CK - 1, skip_group_check=True)
                e.then_inc(pe_done, 1)

            def chunk_n(q, c, b, hi_, lo_, k0, first, last):
                pe.wait_ge(lo_done, 4 * q + (c + 1))
                for k in range(CK):
                    for t in range(TT):
                        xh, xl = hi_(k0 + k)[:, t * P:(t + 1) * P], lo_(k0 + k)[:, t * P:(t + 1) * P]
                        wh, wl = whi[:, c, k, :], wlo[:, c, k, :]
                        o = bank(b, t)
                        T.matmul(o, xh, wh, start=first and k == 0 and t == 0, stop=False, skip_group_check=True)
                        T.matmul(o, xh, wl, start=False, stop=False, skip_group_check=True)
                        e = T.matmul(o, xl, wh, start=False, stop=last and k == CK - 1, skip_group_check=True)
                e.then_inc(pe_done, 1)

            def tiles(src, first=0):
                return lambda k: src[:, first + k, :]

            def flat(src):
                return lambda k: src[:, S * k:S * (k + 1)]

            H, MM = (tiles(h_hi), tiles(h_lo)), (tiles(m_hi), tiles(m_lo))
            YM = MM
            YA = (tiles(m_hi, 8), tiles(m_lo, 8))
            YR = (flat(r_hi), flat(r_lo))

            def bank_free(b, before):
                if not (isinstance(before, int) and before == 0):
                    pe.wait_ge(evac[b], before)

            def quad(chunk, q, b, before, x_, between={}, tiles_ready=None):
                if -1 in between:
                    between[-1]()
                bank_free(b, before)
                for c in range(4):
                    if tiles_ready is not None:
                        pe.wait_ge(tiles_ready[0], tiles_ready[1] + 2 * c + 2)
                    chunk(q, c, b, *x_, 4 * c, c == 0, c == 3)
                    if c in between:
                        between[c]()

            def quads(chunk, ph, trips, x_, k=0):
                with pe.Fori(0, trips) as i:
                    for j in range(2):
                        quad(chunk, 2 * i + (Q0[ph] + k + j), j, i + (G0[ph] + k) // 2, x_)

            def transpose_tiles(src, n, pairs):
                for k in pairs:
                    if k in (0, 4):
                        pe.wait_ge(s_xn, len(NORM_PARTS) * n + k // 2 + 2)
                    if k == 5 and n == 1:
                        pe.wait_ge(s_gt, 1)
                    if k >= 6:
                        pe.wait_ge(s_trl, KT * n // 2 + k - 5)
                    for u in range(2):
                        for t in range(TT):
                            e = T.transpose(bank(2 + k % 6, u)[:, t * P:(t + 1) * P], src[:, t, (2 * k + u) * P:(2 * k + u + 1) * P], eye[:, :])
                    e.then_inc(s_tr, 1)

            for free in (m_o, a_s):
                pe.sem_inc(free, 1)
            pe.wait_ge(s_rows, 48)
            pe.wait_ge(s_eye, 16)
            T.transpose(ps[2][:, 0:48], work[0:48, 0:P], eye[0:48, 0:48]).then_inc(s_vt, 1)
            pe.wait_ge(s_ve, 1)
            transpose_tiles(X, 0, range(4))
            quad(chunk_t, 0, 0, 0, H, {0: lambda: transpose_tiles(X, 0, (4, 5)), 1: lambda: transpose_tiles(X, 0, (6, 7))},
                 tiles_ready=(s_trl, 0))
            quad(chunk_t, 1, 1, 0, H)
            pe.wait_ge(s_rows2, 96)
            for k in range(4):
                T.transpose(ps[2][:, 88 * k:88 * (k + 1)], work[0:88, P * (1 + k):P * (2 + k)], eye[0:88, 0:88])
            for k in range(2):
                e = T.transpose(ps[3][:, 32 * k:32 * (k + 1)], work[0:CB, P * (5 + k):P * (6 + k)], eye[0:CB, 0:CB])
            e.then_inc(s_vt, 1)
            pe.wait_ge(s_wgl, 1)
            for k in range(KT):
                w = wg[:, 48 * k:48 * k + P]
                T.matmul(ps[7][:, 0:S], w, h_hi[:, k, :], start=k == 0, stop=False)
                e = T.matmul(ps[7][:, 0:S], w, h_lo[:, k, :], start=False, stop=k == KT - 1)
            e.then_inc(s_gp, 1)
            pe.wait_ge(s_oh, 48)
            pe.wait_ge(s_neg, 1)
            T.matmul(ps[4][0:HEADS, 0:REL], work[0:BUCKETS + 1, W_RB:W_RB + HEADS],
                     work[0:BUCKETS + 1, 1024:1024 + REL], start=True, stop=True).then_inc(s_vt, 1)

            def gates_to_tokens():
                pe.wait_ge(s_gc, 1)
                for t in range(TT):
                    e = T.matmul(ps[7][:, 256 + 24 * t:256 + 24 * (t + 1)], work[0:48, W_SIG + P * t:W_SIG + P * (t + 1)],
                                 stack[0:48, 32:56], start=True, stop=True)
                e.then_inc(s_gtt, 1)
            quad(chunk_t, 2, 0, 1, H, {0: gates_to_tokens})
            pe.wait_ge(s_rbc, 1)
            transpose_tiles(M, 1, range(6))
            quad(chunk_t, 3, 1, 1, H, {0: lambda: transpose_tiles(M, 1, (6, 7))})
            pe.wait_ge(s_trl, KT)
            quads(chunk_t, "mk", 2, MM)
            quads(chunk_n, "mv", 2, MM)

            with pe.Fori(0, 2) as i:
                for j in range(2):
                    m, q = 2 * i + j, 2 * i + (Q0["nq"] + j)

                    def scores():
                        pe.wait_ge(m_qst, m + 1)
                        if j == 0:
                            for b in range(2):
                                pe.wait_ge(evac[b], G0["nq"] // 2)
                        for t in range(TT):
                            for d in range(2):
                                e = T.matmul(bank(2, t), work[:, W_MS + S * d + P * t:W_MS + S * d + P * (t + 1)],
                                             arena[:, bass.ds(512 * m + (A_MK + S * d), S)], start=d == 0, stop=d == 1)
                        e.then_inc(m_s, 1)

                    def transposes():
                        pe.wait_ge(m_p, m + 1)
                        for u in range(TT):
                            for t in range(TT):
                                e = T.transpose(bank(4, u)[:, t * P:(t + 1) * P], work[:, W_MP + S * t + P * u:W_MP + S * t + P * (u + 1)], eye[:, :])
                        e.then_inc(m_t, 1)

                    def output():
                        pe.wait_ge(m_te, m + 1)
                        pe.wait_ge(m_vst, m + 1)
                        pe.wait_ge(m_l, m + 1)
                        for d in range(2):
                            for u in range(TT):
                                e = T.matmul(bank(6, d), work[:, W_MVS + S * u + P * d:W_MVS + S * u + P * (d + 1)],
                                             work[:, W_MPT + S * u:W_MPT + S * (u + 1)], start=u == 0, stop=u == 1)
                        e.then_inc(m_o, 1)

                    quad(chunk_t, q, j, i + G0["nq"] // 2, H, {-1: scores, 2: transposes, 3: output})
            for n in range(3):
                quad(chunk_t, Q0["kv0"] + n, n % 2, (G0["kv0"] + n) // 2, H)
            def hidden():
                pe.wait_ge(s_cpo, 2)
                for a in range(2):
                    for t in range(2):
                        e = T.matmul(ps[7][:, 32 * (2 * a + t):32 * (2 * a + t + 1)],
                                     work[0:4 * CS, W_HID + S * a + P * t:W_HID + S * a + P * (t + 1)], stack[0:4 * CS, 0:32],
                                     start=True, stop=True)
                e.then_inc(s_htt, 1)

            def compressed():
                pe.wait_ge(s_hcp, 1)
                pe.wait_ge(s_pe2, 32)
                for t in range(2):
                    T.matmul(ps[7][:, 8 * CS:10 * CS], w2[:, 0, t, :], hid[:, 0, t, :], start=t == 0, stop=t == 1)
                for g2 in range(GROUPS):
                    for t in range(2):
                        e = T.matmul(ps[7][0:NC, 256 + DH * g2:256 + DH * (g2 + 1)], hid[:, 1, t, CS * g2:CS * g2 + NC],
                                     w2[:, 1, t, :], start=t == 0, stop=t == 1)
                e.then_inc(s_kc, 1)

            for m, (kind, n) in enumerate(MIX):
                q, g = Q0["mix"] + m, G0["mix"] + n
                if kind == "kv":
                    quad(chunk_t if n == 1 else chunk_n, q, g % 2, g // 2, H, {0: hidden, 2: compressed} if n == 2 else {})
                    continue
                a, half = n // 2, n % 2
                pe.wait_ge(s_bkl, a + 1)
                o = ps[2 + a][:, 0:S]
                for c in range(4):
                    pe.wait_ge(lo_done, 4 * q + c + 1)
                    for k in range(CK):
                        at = 4 * CS * (16 * half + 4 * c + k)
                        x_ = (r_hi, r_lo)[a][:, at:at + P]
                        T.matmul(o, x_, whi[:, c, k, :], start=half == 0 and c == 0 and k == 0, stop=False)
                        e = T.matmul(o, x_, wlo[:, c, k, :], start=False, stop=half == 1 and c == 3 and k == CK - 1)
                    e.then_inc(pe_done, 1)

            for g, ph in enumerate(("rqk", "rv")):
                with pe.Fori(0, 2) as i:
                    for j in range(2):
                        h, q = 2 * i + (HPG * g + j), 2 * i + (Q0[ph] + j)

                        def scores():
                            pe.wait_ge(a_st, h + 1)
                            if g == 0 and j == 0:
                                pe.wait_ge(s_kce, 1)
                                for b in range(2):
                                    pe.wait_ge(evac[b], G0["rqk"] // 2)
                            q0, q1 = work[:, W_QS:W_QS + P], work[:, W_QS + P:W_QS + S]
                            for n, k in enumerate((A_KS, A_KW)):
                                T.matmul(bank(2, n)[:, 0:P], q0, arena[:, k + S * g:k + S * g + P], start=True, stop=True)
                                T.matmul(bank(3, n), q1, arena[:, k + S * g:k + S * (g + 1)], start=True, stop=True)
                            T.matmul(ps[2][:, P:P + NC0], q0, kc[:, g, 0:NC0], start=True, stop=True)
                            T.matmul(ps[2][:, P + CS:P + CS + NC], q1, kc[:, g, 0:NC], start=True, stop=True).then_inc(a_s, 1)

                        def transposes():
                            pe.wait_ge(a_p, h + 1)
                            for n in range(2):
                                b = ps[4 + n]
                                T.transpose(b[:, 0:P], work[:, W_P + P * n:W_P + P * (n + 1)], eye[:, :])
                                for u in range(TT):
                                    o = W_P + S * (1 + n) + P * u
                                    T.transpose(b[:, P * (1 + u):P * (2 + u)], work[:, o:o + P], eye[:, :])
                            T.transpose(ps[4][0:NC0, 384:512], work[:, W_P + 768:W_P + 768 + NC0], eye[:, :])
                            T.transpose(ps[5][0:NC, 384:512], work[:, W_P + 768 + NC0:W_P + 768 + NC0 + NC], eye[:, :]).then_inc(a_t, 1)

                        def output():
                            pe.wait_ge(a_ta, h + 1)
                            pe.wait_ge(a_tv, h + 1)
                            pe.wait_ge(a_l, h + 1)
                            for n, v in enumerate((A_VS, A_VW)):
                                T.matmul(ps[6][:, 0:S], arena[:, v + DH * g:v + DH * (g + 1)], work[:, W_PT + 384 * n:W_PT + 384 * n + S],
                                         start=n == 0, stop=False, skip_group_check=True)
                                T.matmul(ps[6][:, P:S], arena[:, v + S + DH * g:v + S + DH * (g + 1)],
                                         work[:, W_PT + 384 * n + S:W_PT + 384 * (n + 1)], start=False, stop=False, skip_group_check=True)
                            T.matmul(ps[6][:, 0:P], vc[0:NC0, g, :], work[0:NC0, W_CT:W_CT + P], start=False, stop=False, skip_group_check=True)
                            T.matmul(ps[6][:, P:S], vc[:, g, :], work[0:NC, W_CT + P:W_CT + S], start=False, stop=True,
                                     skip_group_check=True).then_inc(a_o, 1)

                        quad((chunk_t, chunk_n)[g], q, j, i + G0[ph] // 2, H, {-1: scores, NSA_BEFORE[-1]: transposes, 3: output})
            quads(chunk_n, "rg", 2, H)

            with pe.Fori(0, 2) as i:
                for j in range(2):
                    r, q = 2 * i + j, 2 * i + (Q0["bg0"] + j)

                    def inner():
                        pe.wait_ge(r_q, r + 1)
                        k = W_QR + S
                        T.matmul(ps[3][:, 0:S], work[:, k:k + P], work[:, W_QR:W_QR + S], start=True, stop=True)
                        T.matmul(ps[3][:, S:S + P], work[:, k + P:k + S], work[:, W_QR + P:W_QR + S], start=True, stop=True).then_inc(r_i, 1)

                    def output():
                        pe.wait_ge(r_d, r + 1)
                        v = [arena[:, bass.ds(512 * r + (A_RV + S * u), S)] for u in range(TT)]
                        T.matmul(bank(4, 0), work[:, W_IN:W_IN + P], v[0], start=True, stop=True)
                        T.matmul(bank(4, 1), work[:, W_IN + P:W_IN + 2 * P], v[0], start=True, stop=False)
                        T.matmul(bank(4, 1), work[:, W_IN + 2 * P:W_IN + 3 * P], v[1], start=False, stop=True).then_inc(r_o, 1)

                    def transposes():
                        pe.wait_ge(r_y, r + 1)
                        pe.wait_ge(r_l, r + 1)
                        for u in range(2):
                            for t in range(TT):
                                e = T.transpose(bank(6, u)[:, t * P:(t + 1) * P], work[:, W_YB + S * t + P * u:W_YB + S * t + P * (u + 1)], eye[:, :])
                        e.then_inc(r_t, 1)

                    quad(chunk_t, q, j, i + G0["bg0"] // 2, H, {0: inner, 1: output, 3: transposes})
            for n, y in enumerate((YM, YA, YR)):
                if n == 0:
                    quads(chunk_t, "bg0", 2, H, 4)
                else:
                    quads(chunk_t, f"bg{n}", 4, H)
                if n == 2:
                    pe.wait_ge(r_l, RH + 1)
                with pe.Fori(0, 2) as i:
                    for j in range(2):
                        for c in range(4):
                            if c % 2 == 0:
                                bank_free(c // 2, 2 * i + (G0[f"br{n}"] // 2 + j))
                            chunk_t(2 * i + (Q0[f"br{n}"] + j), c, c // 2, *y, 4 * (c % 2), c % 2 == 0, c % 2 == 1)
            quad(chunk_n, Q0["wo"], 0, G0["wo"] // 2, MM, tiles_ready=(s_mgl, 0))
            quad(chunk_n, Q0["wo"] + 1, 1, G0["wo"] // 2, MM)
            quads(chunk_n, "wo", 3, MM, 2)

            def up_quads(q, s):
                for n in range(4):
                    if isinstance(s, int) and n == 0:
                        transpose_tiles(M, 2, range(4))
                        quad(chunk_t, q, 0, up_group(s), H, {0: lambda: transpose_tiles(M, 2, (4, 5)),
                                                            1: lambda: transpose_tiles(M, 2, (6, 7))}, tiles_ready=(s_trl, KT))
                        continue
                    quad(chunk_t, q + n, n % 2, up_group(s) + n // 2, H)

            def down(q, s, u):
                pe.wait_ge(s_al, s + 1)
                for g in range(8):
                    pe.wait_ge(s_dn, 8 * s + g + 1)
                    chunk_n(q + g // 4, g % 4, 2 + g % 4, *YR, 4 * u, True, True)

            up_quads(Q0["up0"], 0)
            with pe.Fori(0, (STEPS - 1) // 2) as i:
                for u in range(2):
                    q = 12 * i + (Q0["ffn"] + 6 * u)
                    up_quads(q, 2 * i + (u + 1))
                    down(q + 4, 2 * i + u, u)
            down(Q0["dn"], STEPS - 1, 0)


def constants():
    eye = np.eye(P, dtype=np.float32)
    onehot = np.zeros((BUCKETS + 1, REL), np.float32)
    for c in range(REL):
        rel = S - 1 - c
        if rel < 0:
            onehot[BUCKETS, c] = 1.0
            continue
        b = rel
        if rel >= BUCKETS // 2:
            b = BUCKETS // 2 + int(math.log(rel / (BUCKETS // 2)) / math.log(MAXD / (BUCKETS // 2)) * (BUCKETS - BUCKETS // 2))
        onehot[min(b, BUCKETS - 1), c] = 1.0
    theta = (np.float32(1.0) / np.power(np.float32(10000.0), np.linspace(0.0, 1.0, RDK // 2, dtype=np.float32))).astype(np.float32)
    ang = (theta[:, None] * np.arange(S, dtype=np.float32)[None, :]).astype(np.float32).astype(np.float64)
    cos = np.tile(np.cos(ang), (2, 1))
    sin = np.concatenate([-np.sin(ang), np.sin(ang)], 0)
    scale = RDK ** -0.5
    parts = [cos, cos * scale, sin, sin * scale]
    diff = np.arange(S)[None, :] - np.arange(P)[:, None]
    for hh in range(RH):
        parts.append(np.where(diff >= 0, (1.0 - 2.0 ** (-5.0 - hh)) ** np.maximum(diff, 0), 0.0))
    stack = np.zeros((64, 56), np.float32)
    for i in range(64):
        stack[i, i % 32] = 1.0
    for i in range(48):
        stack[i, 32 + i % 24] = 1.0
    return {"c_eye": eye, "c_stack": stack, "c_onehot": onehot, "c_ret": np.concatenate(parts, 1).astype(np.float32)}


_INS = ["x", "mem", "w_in", "cmp_pe_k", "cmp_w1_k", "cmp_w2_k", "cmp_pe_v", "cmp_w1_v", "cmp_w2_v", "rel_bias",
        "w_mem_kv", "w_br_nsa", "w_br_ret", "w_br_mem", "w_o", "w_up", "conv_w", "conv_b", "w_down", "g_pre_mix",
        "g_post_mix", "g_mem", "g_pre_ffn", "g_post_ffn"]


def kernel(**inputs):
    import concourse.bacc as bacc
    from concourse.bass_utils import run_bass_kernel_spmd

    nc = bacc.Bacc("TRN2", target_bir_lowering=False, num_devices=1)
    arrays = {f"in_{n}": np.ascontiguousarray(inputs[n]) for n in _INS}
    arrays.update(constants())
    args = [nc.dram_tensor(n, a.shape, mybir.dt.from_np(a.dtype), kind="ExternalInput").ap() for n, a in arrays.items()]
    scratch = nc.dram_tensor("bias_rows", (HEADS, P, REL), F32).ap()
    out = nc.dram_tensor("out_y", (1, S, D), F32, kind="ExternalOutput").ap()
    build(nc, *args, scratch, out)
    r = run_bass_kernel_spmd(nc, [arrays], core_ids=[0])
    return r.results[0]["out_y"]
```
